# Optimizing a Trainium2 kernel written in Bass

```python
import math
import jax, jax.numpy as jnp
from jax import lax
import numpy as np

D_MODEL = 1024
BATCH = 1
SEQ = 512
DEPTH = 2

N_Q_HEADS = 8
N_KV_HEADS = 2
HEAD_DIM = 64
GQA_GROUP = N_Q_HEADS // N_KV_HEADS
ATTN_WIDTH = N_Q_HEADS * HEAD_DIM
KV_WIDTH = N_KV_HEADS * HEAD_DIM
WINDOW = 128
BLOCK = 128
ROPE_DIM = HEAD_DIM // 4
ROPE_THETA = 500000.0

HYENA_WIDTH = 512
SHORT_CONV = 3
FILTER_EMB_DIM = 33
FILTER_HIDDEN = 64
DECAY_TARGET = 1e-2
FAST_DECAY_PCT = 0.3
SLOW_DECAY_PCT = 1.5
MAX_DECAY = math.log(DECAY_TARGET) / FAST_DECAY_PCT
MIN_DECAY = math.log(DECAY_TARGET) / SLOW_DECAY_PCT

N_BRANCHES = 2
IN_WIDTH = ATTN_WIDTH + 2 * KV_WIDTH + 3 * HYENA_WIDTH + N_BRANCHES * D_MODEL

N_KEYS = 128
N_EXPERTS = N_KEYS * N_KEYS
PEER_HEADS = 8
PEER_TOPK = 16
QUERY_DIM = 256
HALF_QUERY = QUERY_DIM // 2
PEER_TOKEN_BLOCK = 128

EPS = 1e-6

kernel_name = "hybrid_swa_hyena_peer_encoder"

def rmsnorm(x, g):
    xf = x.astype(jnp.float32)
    r = lax.rsqrt(jnp.mean(xf * xf, axis=-1, keepdims=True) + EPS)
    return (xf * r * g.astype(jnp.float32)).astype(x.dtype)

def rope_tables(positions):
    inv_freq = ROPE_THETA ** (-jnp.arange(0, ROPE_DIM, 2, dtype=jnp.float32) / ROPE_DIM)
    ang = positions.astype(jnp.float32)[..., None] * inv_freq
    return jnp.cos(ang)[:, :, None, :], jnp.sin(ang)[:, :, None, :]

def apply_partial_rope(t, cos, sin):
    half = ROPE_DIM // 2
    t1 = t[..., :half].astype(jnp.float32)
    t2 = t[..., half:ROPE_DIM].astype(jnp.float32)
    rot = jnp.concatenate([t1 * cos - t2 * sin, t2 * cos + t1 * sin], axis=-1).astype(t.dtype)
    return jnp.concatenate([rot, t[..., ROPE_DIM:]], axis=-1)

def window_attention(q, k, v, sink):
    B, S = q.shape[0], q.shape[1]
    nb = S // BLOCK
    qb = q.reshape(B, nb, BLOCK, N_KV_HEADS, GQA_GROUP, HEAD_DIM)

    def band(t):
        tp = jnp.pad(t, ((0, 0), (BLOCK, BLOCK), (0, 0), (0, 0)))
        tp = tp.reshape(B, nb + 2, BLOCK, N_KV_HEADS, HEAD_DIM)
        return jnp.concatenate([tp[:, :-2], tp[:, 1:-1], tp[:, 2:]], axis=2)

    kb, vb = band(k), band(v)
    scale = HEAD_DIM ** -0.5
    s = jnp.einsum('bnqhgd,bnkhd->bnhgqk', qb, kb).astype(jnp.float32) * scale
    blk = jnp.arange(nb)[:, None]
    q_pos = blk * BLOCK + jnp.arange(BLOCK)[None, :]
    k_pos = (blk - 1) * BLOCK + jnp.arange(3 * BLOCK)[None, :]
    valid = (jnp.abs(q_pos[:, :, None] - k_pos[:, None, :]) <= WINDOW) \
        & (k_pos[:, None, :] >= 0) & (k_pos[:, None, :] < S)
    s = jnp.where(valid[None, :, None, None], s, -1e30)
    sink_l = sink.astype(jnp.float32).reshape(N_KV_HEADS, GQA_GROUP)[None, None, :, :, None, None]
    m = jnp.maximum(jnp.max(s, axis=-1, keepdims=True), sink_l)
    p = jnp.exp(s - m)
    denom = jnp.sum(p, axis=-1, keepdims=True) + jnp.exp(sink_l - m)
    out = jnp.einsum('bnhgqk,bnkhd->bnqhgd', (p / denom).astype(v.dtype), vb)
    return out.reshape(B, S, ATTN_WIDTH)

def hyena_filter(L, w1, b1, fr1, w2, b2, fr2, w3, b3):
    t = jnp.linspace(0.0, 1.0, L, dtype=jnp.float32)[:, None]
    bands = (FILTER_EMB_DIM - 1) // 2
    w = 2.0 * math.pi * jnp.arange(L, dtype=jnp.float32)[:, None] / L
    f = jnp.linspace(1e-4, bands - 1, bands, dtype=jnp.float32)[None, :]
    z = jnp.concatenate([t, jnp.cos(f * w), -jnp.sin(f * w)], axis=-1)
    h = jnp.sin(fr1 * (z @ w1 + b1))
    h = jnp.sin(fr2 * (h @ w2 + b2))
    h = (h @ w3 + b3).astype(jnp.float32)
    deltas = jnp.linspace(MIN_DECAY, MAX_DECAY, HYENA_WIDTH, dtype=jnp.float32)
    decay = jnp.exp(-t * jnp.abs(deltas)[None, :])
    h = h.reshape(L, 2, HYENA_WIDTH) * decay[:, None, :]
    h_f, h_b = h[:, 0], h[:, 1]
    return jnp.concatenate([h_f[:1] + h_b[:1], h_f[1:],
                            jnp.zeros((1, HYENA_WIDTH), jnp.float32), h_b[:0:-1]], axis=0)

def hyena_mixer(u, conv_w, conv_b, w1, b1, fr1, w2, b2, fr2, w3, b3, skip):
    B, L = u.shape[0], u.shape[1]
    c3 = 3 * HYENA_WIDTH
    uc = lax.conv_general_dilated(u, conv_w.reshape(SHORT_CONV, 1, c3).astype(u.dtype),
                                  window_strides=(1,), padding=((1, 1),),
                                  dimension_numbers=('NWC', 'WIO', 'NWC'),
                                  feature_group_count=c3) + conv_b
    x0, x1, vv = jnp.split(uc, 3, axis=-1)
    zin = (x1 * vv).astype(jnp.float32)
    kern = hyena_filter(L, w1, b1, fr1, w2, b2, fr2, w3, b3)
    zf = jnp.fft.rfft(zin, n=2 * L, axis=1)
    kf = jnp.fft.rfft(kern, n=2 * L, axis=0)
    y = jnp.fft.irfft(zf * kf[None], n=2 * L, axis=1)[:, :L]
    y = y + zin * skip.astype(jnp.float32)
    return (x0.astype(jnp.float32) * y).astype(u.dtype)

def peer_ffn(xn, w_query, sub_keys, expert_u, expert_v):
    B, S, D = xn.shape
    xt = xn.reshape(B * S // PEER_TOKEN_BLOCK, PEER_TOKEN_BLOCK, D)

    def block(xb):
        c = xb.shape[0]
        q = (xb @ w_query).reshape(c, PEER_HEADS, 2, HALF_QUERY)
        s = jnp.einsum('chpd,pkd->chpk', q, sub_keys)
        s_top, i_top = lax.top_k(s, PEER_TOPK)
        cand = s_top[:, :, 0, :, None] + s_top[:, :, 1, None, :]
        cand_idx = i_top[:, :, 0, :, None] * N_KEYS + i_top[:, :, 1, None, :]
        best, pos = lax.top_k(cand.reshape(c, PEER_HEADS, PEER_TOPK * PEER_TOPK), PEER_TOPK)
        idx = jnp.take_along_axis(cand_idx.reshape(c, PEER_HEADS, PEER_TOPK * PEER_TOPK), pos, axis=-1)
        g = jax.nn.softmax(best.astype(jnp.float32), axis=-1).astype(xb.dtype)
        u = jnp.take(expert_u, idx, axis=0)
        act = jax.nn.gelu(jnp.einsum('chkd,cd->chk', u, xb), approximate=False)
        vsel = jnp.take(expert_v, idx, axis=0)
        return jnp.einsum('chk,chkd->cd', g * act, vsel)

    return lax.map(block, xt).reshape(B, S, D)

def setup_inputs(seed: int = 0) -> dict:
    key = jax.random.key(seed)
    ks = jax.random.split(key, 24)
    f32 = jnp.float32
    nrm = lambda k, shape, scale: jax.random.normal(k, shape, f32) * scale
    C = HYENA_WIDTH
    return {
        "x": nrm(ks[0], (BATCH, SEQ, D_MODEL), 1.0),
        "positions": jnp.broadcast_to(jnp.arange(SEQ, dtype=jnp.int32), (BATCH, SEQ)),
        "norm_mix": 1.0 + nrm(ks[1], (DEPTH, D_MODEL), 0.02),
        "w_in": nrm(ks[2], (DEPTH, D_MODEL, IN_WIDTH), D_MODEL ** -0.5),
        "conv_w": nrm(ks[3], (DEPTH, SHORT_CONV, 3 * C), SHORT_CONV ** -0.5),
        "conv_b": nrm(ks[4], (DEPTH, 3 * C), 0.02),
        "filt_w1": nrm(ks[5], (DEPTH, FILTER_EMB_DIM, FILTER_HIDDEN), FILTER_EMB_DIM ** -0.5),
        "filt_b1": nrm(ks[6], (DEPTH, FILTER_HIDDEN), 0.1),
        "filt_freq1": 1.0 + nrm(ks[7], (DEPTH, FILTER_HIDDEN), 0.1),
        "filt_w2": nrm(ks[8], (DEPTH, FILTER_HIDDEN, FILTER_HIDDEN), FILTER_HIDDEN ** -0.5),
        "filt_b2": nrm(ks[9], (DEPTH, FILTER_HIDDEN), 0.1),
        "filt_freq2": 1.0 + nrm(ks[10], (DEPTH, FILTER_HIDDEN), 0.1),
        "filt_w3": nrm(ks[11], (DEPTH, FILTER_HIDDEN, 2 * C), 0.02 * FILTER_HIDDEN ** -0.5),
        "filt_b3": nrm(ks[12], (DEPTH, 2 * C), 0.002),
        "hyena_skip": nrm(ks[13], (DEPTH, C), 1.0),
        "attn_sink": nrm(ks[14], (DEPTH, N_Q_HEADS), 0.5),
        "w_attn_branch": nrm(ks[15], (DEPTH, ATTN_WIDTH, D_MODEL), ATTN_WIDTH ** -0.5),
        "w_hyena_branch": nrm(ks[16], (DEPTH, C, D_MODEL), C ** -0.5),
        "w_out": nrm(ks[17], (DEPTH, D_MODEL, D_MODEL), D_MODEL ** -0.5),
        "norm_ffn": 1.0 + nrm(ks[18], (DEPTH, D_MODEL), 0.02),
        "w_query": nrm(ks[19], (DEPTH, D_MODEL, PEER_HEADS * QUERY_DIM), D_MODEL ** -0.5),
        "sub_keys": nrm(ks[20], (DEPTH, 2, N_KEYS, HALF_QUERY), HALF_QUERY ** -0.5),
        "expert_u": nrm(ks[21], (DEPTH, N_EXPERTS, D_MODEL), D_MODEL ** -0.5),
        "expert_v": nrm(ks[22], (DEPTH, N_EXPERTS, D_MODEL), PEER_HEADS ** -0.5),
        "norm_final": 1.0 + nrm(ks[23], (D_MODEL,), 0.02),
    }

def reference(x, positions, norm_mix, w_in, conv_w, conv_b, filt_w1, filt_b1, filt_freq1,
              filt_w2, filt_b2, filt_freq2, filt_w3, filt_b3, hyena_skip, attn_sink,
              w_attn_branch, w_hyena_branch, w_out, norm_ffn, w_query, sub_keys,
              expert_u, expert_v, norm_final):
    B, S = x.shape[0], x.shape[1]
    cos, sin = rope_tables(positions)
    splits = [ATTN_WIDTH, ATTN_WIDTH + KV_WIDTH, ATTN_WIDTH + 2 * KV_WIDTH,
              ATTN_WIDTH + 2 * KV_WIDTH + 3 * HYENA_WIDTH,
              ATTN_WIDTH + 2 * KV_WIDTH + 3 * HYENA_WIDTH + D_MODEL]
    for l in range(DEPTH):
        xn = rmsnorm(x, norm_mix[l])
        proj = xn @ w_in[l]
        q, k, v, hy, g_a, g_h = jnp.split(proj, splits, axis=-1)
        q = apply_partial_rope(q.reshape(B, S, N_Q_HEADS, HEAD_DIM), cos, sin)
        k = apply_partial_rope(k.reshape(B, S, N_KV_HEADS, HEAD_DIM), cos, sin)
        v = v.reshape(B, S, N_KV_HEADS, HEAD_DIM)
        y_a = window_attention(q, k, v, attn_sink[l]) @ w_attn_branch[l]
        y_h = hyena_mixer(hy, conv_w[l], conv_b[l], filt_w1[l], filt_b1[l], filt_freq1[l],
                          filt_w2[l], filt_b2[l], filt_freq2[l], filt_w3[l], filt_b3[l],
                          hyena_skip[l]) @ w_hyena_branch[l]
        merged = jax.nn.sigmoid(g_a) * y_a + jax.nn.sigmoid(g_h) * y_h
        x = x + merged @ w_out[l]
        x = x + peer_ffn(rmsnorm(x, norm_ffn[l]), w_query[l], sub_keys[l], expert_u[l], expert_v[l])
    return rmsnorm(x, norm_final)


_drawn_inputs = setup_inputs


def setup_inputs(seed=0):
    import zlib

    import numpy as np

    out = dict(_drawn_inputs(seed))
    spreads = {}
    factors = {'filt_freq1': 3.047, 'filt_freq2': 2.729, 'attn_sink': 8.0, 'norm_final': 2.905}
    for name, (base, spread) in spreads.items():
        noise = np.random.default_rng([zlib.crc32(name.encode()), seed]).standard_normal(out[name].shape)
        drawn = base * np.exp(spread * noise) if base else spread * noise
        out[name] = __import__('jax').numpy.asarray(drawn.astype(out[name].dtype))
    for name, factor in factors.items():
        out[name] = (out[name] * factor).astype(out[name].dtype)
    return out
```

```python
import math
from contextlib import ExitStack

import numpy as np
import concourse.bass as bass
from concourse import mybir

F32 = mybir.dt.float32
F32R = mybir.dt.float32r
I32 = mybir.dt.int32
U32 = mybir.dt.uint32
ACT = mybir.ActivationFunctionType
ALU = mybir.AluOpType
AX = mybir.AxisListType.X

P = 128
DEPTH, SEQ, DM = 2, 512, 1024
NB = SEQ // P
KC = DM // P
QH, KVH, HD = 8, 2, 64
GROUP = QH // KVH
ROT = HD // 8
AW, KVW = QH * HD, KVH * HD
HW = 512
HC = HW // P
NHY = 3 * HC
EMB, HID = 33, 64
HY0 = AW + 2 * KVW
GA0 = HY0 + 3 * HW
GH0 = GA0 + DM
NK, PH, TOPK = 128, 8, 16
HP = 2 * PH
CAND = TOPK * TOPK
EPS = 1e-6
NEG = -3.0e38
TWO_PI_HI = 6.28125
TWO_PI_MID = float(np.float32(0.0019350051879882812))
TWO_PI_LO = float(np.float32(2 * math.pi - TWO_PI_HI - TWO_PI_MID))
PI_IN = 3.1415925
ROUND = 1.5 * 2 ** 23

C_ID, C_IOTA, C_MASK, C_IOTA16, C_FREQ = 0, 128, 256, 640, 656
NCONST = C_FREQ + ROT
L_GMIX, L_GFFN, L_CONVW, L_CONVB, L_SKIP = 0, 8, 16, 16 + 3 * NHY, 16 + 4 * NHY
NCOL = L_SKIP + HC

T_Q, T_KV, T_HY, T_FWD, T_INV, T_BR, T_OUT, T_PQ = 0, 1, 2, 5, 6, 7, 15, 17
NTILES = T_PQ + 4
RING = 3

NPAR = 9
TOK_IT = 128
CB = 64
OH = 16
JG = 4
NG = NK // JG
NOUT = 2 * NB


class Steps:

    def __init__(self, sem):
        self.sem, self.n = sem, 0

    def did(self, ins):
        ins.then_inc(self.sem, 1)
        self.n += 1
        return self.n

    def then(self, eng, n=None):
        eng.wait_ge(self.sem, self.n if n is None else n)


def tile_uses():
    parts = [1] * NTILES
    for n in range(KC):
        parts[T_BR + n] = 4
    got, out = [0] * RING, []
    for t in range(NTILES):
        got[t % RING] += 16 * parts[t]
        out.append((t % RING, got[t % RING]))
    return out


def encoder(nc, x, positions, consts, gfinal, cols, fcols, sink, w1, w2, w3, zemb, decay, fwd, inv,
            w_in, w_ab, w_hb, w_out, w_q, keys, ut, v, out):
    ctx = ExitStack()
    at = [16512]

    def sb(name, shape, dt=F32, offset=None):
        size = 4 * int(np.prod(shape[1:]))
        size = (size + 31) // 32 * 32
        if offset is None:
            offset = at[0]
            at[0] += size
        t = nc.alloc_sbuf_tensor_at(name, shape, dt, offset=offset)
        return t, offset

    def sem(name):
        return nc.alloc_semaphore(name)

    X, _ = sb("X", [P, NB, DM])
    CST, _ = sb("CST", [P, NCONST])
    COL, _ = sb("COL", [P, NCOL])
    FCOL, _ = sb("FCOL", [HID, 4])
    SINK, _ = sb("SINK", [P, QH])
    SINCOS, _ = sb("SINCOS", [P, 2, NB, ROT])
    SMALL, _ = sb("SMALL", [P, 64])
    WR, wr_at = sb("WR", [P, RING, 4096])
    phase_at = at[0]
    ident = CST[:, C_ID:C_ID + P]
    iota = CST[:, C_IOTA:C_IOTA + NK]

    XNT, _ = sb("XNT", [P, KC, SEQ])
    MRG, mrg_at = sb("MRG", [P, KC, SEQ])
    ATT, _ = sb("ATT", [P, 4, SEQ])
    YH, yh_at = sb("YH", [P, HC, SEQ])
    abc_at = at[0]
    KF, _ = sb("KF", [P, 2, HC, HW], offset=mrg_at)
    DEC, _ = sb("DEC", [P, NB, HW], offset=yh_at)
    XS, xs_at = sb("XS", [P, 2, DM])
    QKV, _ = sb("QKV", [P, NB, HY0])
    KREP, _ = sb("KREP", [P, NB, KVH, 2, HD])
    QT, _ = sb("QT", [P, 4, SEQ])
    KT, _ = sb("KT", [P, KVH, SEQ])
    SC, _ = sb("SC", [P, 2, GROUP, 3 * P])
    PT, _ = sb("PT", [P, 2, 3, GROUP * P])
    RT, _ = sb("RT", [P, 4, NB, QH + KVH, ROT])
    end_a = at[0]
    at[0] = abc_at
    HYT, _ = sb("HYT", [P, NHY, SEQ + 2])
    X0, _ = sb("X0", [P, HC, SEQ])
    ZT, _ = sb("ZT", [P, HC, SEQ])
    VT, _ = sb("VT", [P, HC, SEQ])
    ZTOK, _ = sb("ZTOK", [P, NB, HW])
    HS, hs_at = sb("HS", [P, 2, NB, HW])
    YF, _ = sb("YF", [P, 2, HC, HW], offset=hs_at)
    FA, _ = sb("FA", [HID, SEQ])
    FK, _ = sb("FK", [HID, SEQ])
    FR, _ = sb("FR", [HID + 1, SEQ])
    W1, _ = sb("W1", [EMB, HID])
    W2, _ = sb("W2", [HID, HID])
    W3, w3_at = sb("W3", [HID + 1, 2 * HW])
    ZE, _ = sb("ZE", [EMB, SEQ])
    end_b = at[0]
    at[0] = abc_at
    SG, _ = sb("SG", [P, 2, 2, SEQ])
    MP, _ = sb("MP", [P, 2, 2, SEQ])
    at[0] = phase_at
    XHI, _ = sb("XHI", [P, KC, SEQ], F32R)
    XLO, _ = sb("XLO", [P, KC, SEQ], F32R)
    IDXT, idxt_at = sb("IDXT", [P, 3, SEQ])
    def_at = at[0]
    XN2, _ = sb("XN2", [P, KC, SEQ])
    XS2, _ = sb("XS2", [P, 2, DM])
    KEY, _ = sb("KEY", [P, 2, NK])
    PQT, _ = sb("PQT", [P, HP, SEQ])
    PS, _ = sb("PS", [P, HP, NK])
    CD, cd_at = sb("CD", [P, PH, TOPK, TOPK])
    EQ, _ = sb("EQ", [P, PH * TOPK, TOPK])
    TV, _ = sb("TV", [P, HP, TOPK])
    TI, _ = sb("TI", [P, HP, TOPK], U32)
    TIF, _ = sb("TIF", [P, HP, TOPK])
    BV, _ = sb("BV", [P, PH, TOPK])
    BP, _ = sb("BP", [P, PH, TOPK], U32)
    BA, _ = sb("BA", [P, 2, PH * TOPK], U32)
    BAF, _ = sb("BAF", [P, 2, PH * TOPK])
    SEL, _ = sb("SEL", [P, 3, PH * TOPK])
    end_d = at[0]
    at[0] = def_at
    IST, _ = sb("IST", [P, 3, TOK_IT])
    OHA, _ = sb("OHA", [P, 2, OH, NK])
    OHB, _ = sb("OHB", [P, 2, OH, NK])
    GST, _ = sb("GST", [P, 2, NK, CB])
    end_e = at[0]
    URAW, _ = sb("URAW", [P, 2, 2, DM], offset=wr_at)
    VRAW, _ = sb("VRAW", [P, 2, 2, DM], offset=wr_at + 16384)
    GT, _ = sb("GT", [P, 2, SEQ // CB, JG, CB], offset=wr_at + 32768)
    at[0] = idxt_at
    UHI, _ = sb("UHI", [P, JG, KC, P], F32R)
    ULO, _ = sb("ULO", [P, JG, KC, P], F32R)
    VHI, _ = sb("VHI", [P, JG, DM], F32R)
    VLO, _ = sb("VLO", [P, JG, DM], F32R)
    WHI, _ = sb("WHI", [P, 2, JG, SEQ], F32R)
    WLO, _ = sb("WLO", [P, 2, JG, SEQ], F32R)
    AC, _ = sb("AC", [P, 2, SEQ])
    WF, _ = sb("WF", [P, 2, SEQ])
    end_f = at[0]
    OUTB, _ = sb("OUTB", [P, NB, DM], offset=phase_at)
    GFIN, _ = sb("GFIN", [P, DM], offset=phase_at + 16384)
    assert max(end_a, end_b, end_d, end_e, end_f) <= nc.sbuf_usable_end, (end_a, end_b, end_d, end_e, end_f)

    ps = nc.alloc_psum_tensor("ps", [P, 8, 512], F32)
    gd = nc.dram_tensor("g_table", (SEQ // CB, P, NK, CB), F32, kind="Internal").ap()

    SS, SV, SR, ST = SMALL[:, 0:4], SMALL[:, 4:8], SMALL[:, 8:12], SMALL[:, 12:16]
    MX, DSK, DEN, POSF = SMALL[:, 16:24], SMALL[:, 24:32], SMALL[:, 32:40], SMALL[:, 40:44]
    GMX, GSUM = SMALL[:, 44:52], SMALL[:, 52:60]

    first_loads, x_loaded, pos_loaded = sem("first_loads"), sem("x_loaded"), sem("pos_loaded")
    pre_steps, out_stored, next_layer = sem("pre_steps"), sem("out_stored"), sem("next_layer")
    pre_sin = sem("pre_sin")
    went_on = sem("went_on")
    layer_sems = []

    def lsem(name):
        layer_sems.append(sem(name))
        return layer_sems[-1]

    engines_done = lsem("engines_done")
    phase = lsem("phase")
    params = lsem("params")
    w_loaded = [lsem(f"w_loaded{i}") for i in range(RING)]
    act_steps, dve_steps = lsem("act_steps"), lsem("dve_steps")
    sumsq, var_ready, root_ready = lsem("sumsq"), lsem("var_ready"), lsem("root_ready")
    xs_ready, xs_turned, xnt_ready = lsem("xs_ready"), lsem("xs_turned"), lsem("xnt_ready")
    qkv_out, qkv_copied, roped = lsem("qkv_out"), lsem("qkv_copied"), lsem("roped")
    qk_turned, qk_copied = lsem("qk_turned"), lsem("qk_copied")
    sc_out, sc_copied, mx_ready, exp_done = lsem("sc_out"), lsem("sc_copied"), lsem("mx_ready"), lsem("exp_done")
    probs_ready, probs_turned, pt_copied = lsem("probs_ready"), lsem("probs_turned"), lsem("pt_copied")
    o_out, o_copied = lsem("o_out"), lsem("o_copied")
    pads_zero, hy_out, hy_copied = lsem("pads_zero"), lsem("hy_out"), lsem("hy_copied")
    f_out, f_arg, f_sin = lsem("f_out"), lsem("f_arg"), lsem("f_sin")
    h3_out, h3_copied, hs_ready, dec_loaded = lsem("h3_out"), lsem("h3_copied"), lsem("hs_ready"), lsem("dec_loaded")
    kf_out, kf_copied = lsem("kf_out"), lsem("kf_copied")
    z_ready, z_turned, ztok_ready = lsem("z_ready"), lsem("z_turned"), lsem("ztok_ready")
    zf_out, zf_used, yf_ready = lsem("zf_out"), lsem("zf_used"), lsem("yf_ready")
    y_out, y_used = lsem("y_out"), lsem("y_used")
    br_out, sg_ready, br_used, mrg_ready = lsem("br_out"), lsem("sg_ready"), lsem("br_used"), lsem("mrg_ready")
    wo_out, wo_added = lsem("wo_out"), lsem("wo_added")
    xhi_ready = lsem("xhi_ready")
    pq_out, pq_copied, ps_out, ps_copied, ps_free = lsem("pq_out"), lsem("pq_copied"), lsem("ps_out"), lsem("ps_copied"), lsem("ps_free")
    bmax_ready, bexp_ready = lsem("bmax_ready"), lsem("bexp_ready")
    sel_ready, sel_turned, idx_copied = lsem("sel_ready"), lsem("sel_turned"), lsem("idx_copied")
    oh_ready, g_out, g_bank_free = lsem("oh_ready"), lsem("g_out"), lsem("g_bank_free")
    ist_steps = lsem("ist_steps")
    g_stored = [lsem(f"g_stored{i}") for i in range(2)]
    u_loaded = [lsem(f"u_loaded{i}") for i in range(2)]
    v_loaded = [lsem(f"v_loaded{i}") for i in range(2)]
    g_loaded = [lsem(f"g_loaded{i}") for i in range(2)]
    u_hi, u_split, u_done = lsem("u_hi"), lsem("u_split"), lsem("u_done")
    v_hi, v_split = lsem("v_hi"), lsem("v_split")
    act_ready, wf_ready, whi_ready, w_ready = lsem("act_ready"), lsem("wf_ready"), lsem("whi_ready"), lsem("w_ready")
    v_out, out_free = lsem("v_out"), lsem("out_free")

    TILE = tile_uses()

    tile_done = ([(qkv_out, 2 * NB)] * 2 + [(hy_out, 4 * i + 4) for i in range(3)] + [(zf_out, HC), (y_out, HC)]
                 + [(br_out, n + 1) for n in range(KC)] + [(wo_out, NB * i + NB) for i in range(2)]
                 + [(pq_out, 4 * i + 4) for i in range(4)])
    assert len(tile_done) == NTILES

    def need_tile(e, t):
        e.wait_ge(w_loaded[TILE[t][0]], TILE[t][1])

    def arrive(e):
        e.drain().then_inc(phase, 1)

    def all_at(e, n):
        e.wait_ge(phase, 3 * n)

    def end_layer(e, l):
        e.drain().then_inc(engines_done, 1)
        e.wait_ge(next_layer, l + 1)
        e.nop().then_inc(went_on, 1)

    SINCOS_ARGS, FINAL_VAR, FINAL0 = 15, 16, 25

    with nc.Block() as block:

        @block.sync
        def _(sp):
            sp.dma_start(X[:], x.rearrange("(b p) d -> p b d", p=P)).then_inc(x_loaded, 16)
            sp.dma_start(CST[:], consts).then_inc(first_loads, 16)
            with sp.Fori(0, DEPTH) as l:
                loaded = [0]

                def weights(parts):
                    t = loaded[0]
                    loaded[0] += 1
                    if t >= RING:
                        sp.wait_ge(*tile_done[t - RING])
                    for dst, src in parts:
                        sp.dma_start(dst(WR[:, t % RING, :]), src).then_inc(w_loaded[t % RING], 16)

                def cols_of(w, c0, n, kc=KC):
                    return w[l, :, c0:c0 + n].rearrange("(k p) n -> p k n", p=P)

                def at_cols(o, kc, n):
                    return lambda s: s[:, o:o + kc * n].rearrange("p (k n) -> p k n", n=n)

                sp.dma_start(COL[:], cols[l]).then_inc(params, 16)
                sp.dma_start(SINK[:], sink[l].partition_broadcast(P)).then_inc(params, 16)
                sp.dma_start(FCOL[:], fcols[l]).then_inc(params, 16)
                weights([(at_cols(0, KC, AW), cols_of(w_in, 0, AW))])
                weights([(at_cols(0, KC, 2 * KVW), cols_of(w_in, AW, 2 * KVW))])
                for i in range(3):
                    weights([(at_cols(0, KC, 512), cols_of(w_in, HY0 + 512 * i, 512))])
                all_at(sp, 1)
                sp.dma_start(W1[:], w1[l]).then_inc(params, 16)
                sp.dma_start(W2[:], w2[l]).then_inc(params, 16)
                sp.dma_start(W3[:], w3[l]).then_inc(params, 16)
                sp.dma_start(ZE[:], zemb).then_inc(params, 16)
                sp.dma_start(DEC[:], decay).then_inc(dec_loaded, 16)
                weights([(lambda s: s, fwd)])
                weights([(lambda s: s, inv)])
                for n in range(KC):
                    weights([(at_cols(0, KC, P), cols_of(w_in, GA0 + P * n, P)),
                             (at_cols(KC * P, KC, P), cols_of(w_in, GH0 + P * n, P)),
                             (at_cols(2 * KC * P, 4, P), cols_of(w_ab, P * n, P)),
                             (at_cols((2 * KC + 4) * P, 4, P), cols_of(w_hb, P * n, P))])
                for i in range(2):
                    weights([(at_cols(0, KC, 512), cols_of(w_out, 512 * i, 512))])
                for i in range(4):
                    if i == 3:
                        all_at(sp, 3)
                        sp.dma_start(KEY[:], keys[l]).then_inc(params, 16)
                    weights([(at_cols(0, KC, 512), cols_of(w_q, 512 * i, 512))])
                all_at(sp, 4)
                with sp.Fori(0, SEQ // TOK_IT) as it:
                    for s in range(2):
                        dst = gd[it * 2 + s].rearrange("i j c -> i (j c)")
                        sp.wait_ge(g_bank_free, it * 32 + 16 * (s + 1) + 8)
                        sp.dma_start(dst, GST[:, s].rearrange("p j c -> p (j c)")).then_inc(g_stored[s], 16)
                for s in range(2):
                    sp.wait_ge(g_stored[s], 16 * (SEQ // TOK_IT))
                all_at(sp, 5)

                def load_u(jp, slot):
                    sp.dma_start(URAW[:, slot], ut[l, jp]).then_inc(u_loaded[slot], 16)

                def load_v(jp, slot):
                    sp.dma_start(VRAW[:, slot], v[l, jp]).then_inc(v_loaded[slot], 16)

                def load_g(g, slot):
                    src = gd[:, :, bass.ds(g * JG, JG), :].rearrange("b i j c -> i b (j c)")
                    sp.dma_start(GT[:, slot].rearrange("p b j c -> p b (j c)"), src).then_inc(g_loaded[slot], 16)

                def step(g, par, u1=True, g2=True):
                    sp.wait_ge(u_split, g * 4 + 4)
                    load_u(g * 2 + 3, 1)
                    if g2:
                        sp.wait_ge(w_ready, g * 4 + 4)
                        load_g(g + 2, par)
                    sp.wait_ge(v_split, g * 4 + 2)
                    load_v(g * 2 + 2, 0)
                    if u1:
                        sp.wait_ge(u_split, g * 4 + 6)
                        load_u(g * 2 + 4, 0)
                    sp.wait_ge(v_split, g * 4 + 4)
                    load_v(g * 2 + 3, 1)

                load_u(0, 0)
                load_g(0, 0)
                load_u(1, 1)
                load_v(0, 0)
                load_v(1, 1)
                sp.wait_ge(u_split, 2)
                load_u(2, 0)
                load_g(1, 1)
                with sp.Fori(0, (NG - 2) // 2) as it:
                    step(it * 2, 0)
                    step(it * 2 + 1, 1)
                step(NG - 2, 0, u1=False, g2=False)
                end_layer(sp, l)
            sp.dma_start(GFIN[:], gfinal.partition_broadcast(P)).then_inc(first_loads, 16)
            for b in range(NB):
                sp.wait_ge(pre_steps, FINAL0 + b + 1)
                sp.dma_start(out[b * P:(b + 1) * P, :], OUTB[:, b, :]).then_inc(out_stored, 16)
            sp.wait_ge(out_stored, 16 * NB)

        @block.gpsimd
        def _(pool):
            with nc.allow_non_contiguous_dma("positions and sinks are a few words"):
                pool.dma_start(POSF[:].bitcast(I32), positions.rearrange("(b p) -> p b", p=P)).then_inc(pos_loaded, 16)
            with pool.Fori(0, DEPTH) as l:
                all_at(pool, 1)
                pool.memset(HYT[:, :, 0:1], 0.0).then_inc(pads_zero, 1)
                pool.memset(HYT[:, :, SEQ + 1:SEQ + 2], 0.0).then_inc(pads_zero, 1)
                pool.wait_ge(pads_zero, 2)
                pool.memset(FR[HID:HID + 1, :], 1.0).then_inc(pads_zero, 1)
                pool.wait_ge(engines_done, 4)
                for s in layer_sems:
                    pool.sem_clear(s)
                pool.nop().then_inc(next_layer, 1)

        P_A, P_B, P_D = 16 * 3, 16 * 7, 16 * 8

        @block.tensor
        def _(pe):
            pe.wait_ge(first_loads, 16)

            def turn_norm(first, xs):
                for b in range(NB):
                    pe.wait_ge(xs_ready, first + b + 1)
                    for half in range(2):
                        n = 2 * b + half
                        if n >= 4:
                            pe.wait_ge(xnt_ready, 2 * first + n - 3)
                        for k in range(4):
                            last = nc.tensor.transpose(ps[:, n % 4, k * P:(k + 1) * P],
                                                       xs[:, b % 2, (half * 4 + k) * P:(half * 4 + k + 1) * P], ident)
                        last.then_inc(xs_turned, 1)

            with pe.Fori(0, DEPTH) as l:
                turn_norm(0, XS)
                need_tile(pe, T_Q)
                need_tile(pe, T_KV)
                wq = WR[:, T_Q % RING, :].rearrange("p (k n) -> p k n", n=AW)
                wkv = WR[:, T_KV % RING, 0:KC * 2 * KVW].rearrange("p (k n) -> p k n", n=2 * KVW)
                for b in range(NB):
                    pe.wait_ge(xnt_ready, 2 * b + 2)
                    if b >= 2:
                        pe.wait_ge(qkv_copied, 2 * (b - 1))
                    for (w, n, o) in ((wq, AW, 0), (wkv, 2 * KVW, 1)):
                        for k in range(KC):
                            last = nc.tensor.matmul(ps[:, 4 + 2 * (b % 2) + o, 0:n], XNT[:, k, b * P:(b + 1) * P],
                                                    w[:, k, :], start=(k == 0), stop=(k == KC - 1))
                        last.then_inc(qkv_out, 1)
                pe.wait_ge(roped, 3)
                pe.wait_ge(qkv_copied, 2 * NB)
                for c in range(4 + KVH):
                    for b in range(NB):
                        src = (QKV[:, b, c * P:(c + 1) * P] if c < 4 else
                               KREP[:, b, c - 4].rearrange("p r d -> p (r d)"))
                        last = nc.tensor.transpose(ps[:, c, b * P:(b + 1) * P], src, ident)
                    last.then_inc(qk_turned, 1)
                pe.wait_ge(qk_copied, 4 + KVH)

                units = [(b, g) for b in range(NB) for g in range(KVH)]

                def keys_of(b):
                    return max(0, b - 1), min(NB, b + 2)

                def scores(u):
                    b, g = units[u]
                    k0, k1 = keys_of(b)
                    if u >= 1:
                        pe.wait_ge(sc_copied, u)
                    for h in range(GROUP):
                        head = GROUP * g + h
                        rows = slice(HD * (head % 2), HD * (head % 2) + HD)
                        last = nc.tensor.matmul(ps[:, h, 0:(k1 - k0) * P], QT[rows, head // 2, b * P:(b + 1) * P],
                                                KT[rows, g, k0 * P:k1 * P], start=True, stop=True)
                    last.then_inc(sc_out, 1)

                scores(0)
                kbs = 0
                for u, (b, g) in enumerate(units):
                    if u + 1 < len(units):
                        scores(u + 1)
                    k0, k1 = keys_of(b)
                    pe.wait_ge(probs_ready, u + 1)
                    if u >= 1:
                        pe.wait_ge(pt_copied, kbs)
                    for i in range(k1 - k0):
                        for h in range(GROUP):
                            last = nc.tensor.transpose(ps[:, 4 + i, h * P:(h + 1) * P],
                                                       SC[:, u % 2, h, i * P:(i + 1) * P], ident)
                        last.then_inc(probs_turned, 1)
                    kbs += k1 - k0
                    pe.wait_ge(pt_copied, kbs)
                    if u >= 1:
                        pe.wait_ge(o_copied, u)
                    for odd in range(2):
                        for i in range(k1 - k0):
                            pt = PT[:, u % 2, i, :].rearrange("p (a b q) -> p b a q", b=2, q=P)
                            last = nc.tensor.matmul(
                                ps[HD * odd:HD * odd + HD, 7, 0:2 * P].rearrange("p (a q) -> p a q", q=P),
                                QKV[:, k0 + i, AW + KVW + g * HD:AW + KVW + (g + 1) * HD],
                                pt[:, odd], start=(i == 0), stop=(i == k1 - k0 - 1))
                    last.then_inc(o_out, 1)
                arrive(pe)

                all_at(pe, 1)
                pe.wait_ge(params, P_B)
                pe.wait_ge(pads_zero, 3)
                nc.tensor.matmul(ps[0:HID, 4, :], W1[:], ZE[:], start=True, stop=True).then_inc(f_out, 1)

                def hyena_in(n):
                    t = T_HY + n // 4
                    if n % 4 == 0:
                        need_tile(pe, t)
                    if n >= 4:
                        pe.wait_ge(hy_copied, n - 3)
                    w = WR[:, t % RING, :].rearrange("p (k n) -> p k n", n=512)
                    for k in range(KC):
                        last = nc.tensor.matmul(ps[:, n % 4, :], w[:, k, (n % 4) * P:(n % 4 + 1) * P], XNT[:, k, :],
                                                start=(k == 0), stop=(k == KC - 1))
                    last.then_inc(hy_out, 1)

                for n in range(4):
                    hyena_in(n)
                pe.wait_ge(f_sin, 1)
                nc.tensor.matmul(ps[0:HID, 5, :], W2[:], FR[0:HID, :], start=True, stop=True).then_inc(f_out, 1)
                for n in range(4, 8):
                    hyena_in(n)
                pe.wait_ge(f_sin, 2)
                for s in range(NB):
                    if s >= 2:
                        pe.wait_ge(hs_ready, s - 1)
                    for i in range(2):
                        last = nc.tensor.matmul(ps[:, 4 + 2 * (s % 2) + i, :], FR[:, s * P:(s + 1) * P],
                                                W3[:, i * HW:(i + 1) * HW], start=True, stop=True)
                    last.then_inc(h3_out, 1)
                for n in range(8, 12):
                    hyena_in(n)
                need_tile(pe, T_FWD)
                ft = WR[:, T_FWD % RING, :].rearrange("p (s r f) -> p s r f", s=NB, r=2)
                pe.wait_ge(hs_ready, NB)
                pe.wait_ge(hy_copied, NHY)
                for f in range(HC):
                    for r in range(2):
                        n = 2 * f + r
                        if n >= 4:
                            pe.wait_ge(kf_copied, n - 3)
                        for s in range(NB):
                            last = nc.tensor.matmul(ps[:, n % 4, :], ft[:, s, r, f * P:(f + 1) * P], HS[:, r, s, :],
                                                    start=(s == 0), stop=(s == NB - 1))
                        last.then_inc(kf_out, 1)
                pe.wait_ge(z_ready, HC)
                for s in range(NB):
                    for c in range(HC):
                        last = nc.tensor.transpose(ps[:, 4 + s, c * P:(c + 1) * P], ZT[:, c, s * P:(s + 1) * P], ident)
                    last.then_inc(z_turned, 1)
                pe.wait_ge(ztok_ready, NB)
                pe.wait_ge(kf_copied, 2 * HC)
                for f in range(HC):
                    if f >= 2:
                        pe.wait_ge(zf_used, f - 1)
                    for r in range(2):
                        for s in range(NB):
                            last = nc.tensor.matmul(ps[:, 2 * (f % 2) + r, :], ft[:, s, r, f * P:(f + 1) * P],
                                                    ZTOK[:, s, :], start=(s == 0), stop=(s == NB - 1))
                    last.then_inc(zf_out, 1)
                need_tile(pe, T_INV)
                vt = WR[:, T_INV % RING, :].rearrange("p (f r t) -> p f r t", f=HC, r=2)
                pe.wait_ge(yf_ready, HC)
                for c in range(HC):
                    for f in range(HC):
                        for r in range(2):
                            last = nc.tensor.matmul(ps[:, 4 + c, :], YF[:, r, f, c * P:(c + 1) * P], vt[:, f, r, :],
                                                    start=(f == 0 and r == 0), stop=(f == HC - 1 and r == 1))
                    last.then_inc(y_out, 1)
                arrive(pe)

                all_at(pe, 2)
                for n in range(KC):
                    t = T_BR + n
                    need_tile(pe, t)
                    if n >= 2:
                        pe.wait_ge(br_used, n - 1)
                    w = WR[:, t % RING, 0:24 * P].rearrange("p (k n) -> p k n", n=P)
                    for bank, k0, nk, src in ((0, 16, 4, ATT), (1, 0, 8, XNT), (2, 20, 4, YH), (3, 8, 8, XNT)):
                        for k in range(nk):
                            last = nc.tensor.matmul(ps[:, 4 * (n % 2) + bank, :], w[:, k0 + k, :], src[:, k, :],
                                                    start=(k == 0), stop=(k == nk - 1))
                    last.then_inc(br_out, 1)
                pe.wait_ge(mrg_ready, KC)
                for half in range(2):
                    t = T_OUT + half
                    need_tile(pe, t)
                    w = WR[:, t % RING, :].rearrange("p (k n) -> p k n", n=512)
                    for b in range(NB):
                        n = half * NB + b
                        if n >= 4:
                            pe.wait_ge(wo_added, n - 3)
                        for k in range(KC):
                            last = nc.tensor.matmul(ps[:, n % 4, :], MRG[:, k, b * P:(b + 1) * P], w[:, k, :],
                                                    start=(k == 0), stop=(k == KC - 1))
                        last.then_inc(wo_out, 1)
                arrive(pe)

                all_at(pe, 3)
                turn_norm(NB, XS2)
                pe.wait_ge(xnt_ready, 4 * NB)
                for n in range(HP):
                    t = T_PQ + n // 4
                    if n % 4 == 0:
                        need_tile(pe, t)
                    if n >= 4:
                        pe.wait_ge(pq_copied, n - 3)
                    w = WR[:, t % RING, :].rearrange("p (k n) -> p k n", n=512)
                    for k in range(KC):
                        last = nc.tensor.matmul(ps[:, n % 4, :], w[:, k, (n % 4) * P:(n % 4 + 1) * P], XN2[:, k, :],
                                                start=(k == 0), stop=(k == KC - 1))
                    last.then_inc(pq_out, 1)
                pe.wait_ge(params, P_D)
                pe.wait_ge(pq_copied, HP)

                def expert_scores(b):
                    for n in range(HP):
                        if n % 4 == 0 and b >= 1:
                            pe.wait_ge(ps_copied, 4 * (b - 1) + n // 4 + 1)
                        last = nc.tensor.matmul(ps[:, 4 + n // 4, (n % 4) * NK:(n % 4 + 1) * NK],
                                                PQT[:, n, b * P:(b + 1) * P], KEY[:, n % 2, :], start=True, stop=True)
                        if n % 4 == 3:
                            last.then_inc(ps_out, 1)

                expert_scores(0)
                for b in range(NB):
                    if b + 1 < NB:
                        expert_scores(b + 1)
                    pe.wait_ge(sel_ready, b + 1)
                    for i in range(3):
                        last = nc.tensor.transpose(ps[:, b, i * P:(i + 1) * P], SEL[:, i, :], ident)
                    last.then_inc(sel_turned, 1)
                arrive(pe)

                all_at(pe, 4)
                pe.nop().then_inc(g_out, 4)
                with pe.Fori(0, SEQ // TOK_IT) as it:
                    for q in range(TOK_IT // OH):
                        pe.wait_ge(oh_ready, it * 8 + q + 1)
                        for s in range(OH // 4):
                            n = q * 4 + s
                            pe.wait_ge(g_bank_free, it * 32 + n + 1)
                            for k in range(4):
                                last = nc.tensor.matmul(ps[:, n % 8, k * NK:(k + 1) * NK], OHA[:, q % 2, 4 * s + k, :],
                                                        OHB[:, q % 2, 4 * s + k, :], start=True, stop=True)
                            last.then_inc(g_out, 1)
                arrive(pe)

                all_at(pe, 5)

                def up(j, jj):
                    pe.wait_ge(u_split, j + 1)
                    if not isinstance(j, int) or j >= 2:
                        pe.wait_ge(act_ready, j - 1)
                    parts = [(UHI, XHI), (UHI, XLO), (ULO, XHI)]
                    for i, (a, c) in enumerate(parts):
                        for k in range(KC):
                            last = nc.tensor.matmul(ps[:, jj % 2, :], a[:, jj, k, :], c[:, k, :],
                                                    start=(i == 0 and k == 0), stop=(i == 2 and k == KC - 1))
                    last.then_inc(u_done, 1)

                def down(g, par):
                    pe.wait_ge(w_ready, g * 4 + 4)
                    pe.wait_ge(v_split, g * 4 + 4)
                    for o in range(NOUT):
                        dh, b = divmod(o, NB)
                        pe.wait_ge(out_free, g * NOUT + o + 1)
                        n = 0
                        for a, c in ((WHI, VHI), (WHI, VLO), (WLO, VHI)):
                            for jj in range(JG):
                                last = nc.tensor.matmul(ps[:, 2 + o % 4, :], a[:, par, jj, b * P:(b + 1) * P],
                                                        c[:, jj, dh * 512:(dh + 1) * 512],
                                                        start=(n == 0), stop=(n == 3 * JG - 1))
                                n += 1
                        last.then_inc(v_out, 1)

                for jj in range(JG):
                    up(jj, jj)

                def step(g, par):
                    for jj in range(JG):
                        up(g * 4 + 4 + jj, jj)
                    down(g, par)

                with pe.Fori(0, (NG - 2) // 2) as it:
                    step(it * 2, 0)
                    step(it * 2 + 1, 1)
                step(NG - 2, 0)
                down(NG - 1, 1)
                end_layer(pe, l)

        @block.scalar
        def _(act):
            act.wait_ge(pre_steps, SINCOS_ARGS)
            nc.scalar.activation(SINCOS[:], SINCOS[:], ACT.Sin).then_inc(pre_sin, 1)
            act.wait_ge(x_loaded, 16)

            def squares(n, xs):
                for b in range(NB):
                    nc.scalar.activation(xs[:, 0, :], X[:, b, :], ACT.Square,
                                         accum_out=SS[:, b:b + 1]).then_inc(sumsq, 1)
                    act.wait_ge(sumsq, n + b + 1)
                act.wait_ge(var_ready, n // NB + 1)
                nc.scalar.activation(SR, SV, ACT.Sqrt).then_inc(root_ready, 1)

            with act.Fori(0, DEPTH) as l:
                squares(0, XS)
                for b in range(NB):
                    for o, n, c0 in ((0, AW, 0), (1, 2 * KVW, AW)):
                        act.wait_ge(qkv_out, 2 * b + o + 1)
                        nc.scalar.copy(QKV[:, b, c0:c0 + n], ps[:, 4 + 2 * (b % 2) + o, 0:n]).then_inc(qkv_copied, 1)
                for c in range(4 + KVH):
                    act.wait_ge(qk_turned, c + 1)
                    dst = QT[:, c, :] if c < 4 else KT[:, c - 4, :]
                    nc.scalar.copy(dst, ps[:, c, :]).then_inc(qk_copied, 1)
                units = [(b, g) for b in range(NB) for g in range(KVH)]
                kbs = [0]

                def probs(u):
                    b, g = units[u]
                    n = (min(NB, b + 2) - max(0, b - 1)) * P
                    act.wait_ge(mx_ready, u + 1)
                    for h in range(GROUP):
                        nc.scalar.activation(SC[:, u % 2, h, 0:n], SC[:, u % 2, h, 0:n], ACT.Exp,
                                             bias=MX[:, 4 * (u % 2) + h:4 * (u % 2) + h + 1],
                                             accum_out=DEN[:, 4 * (u % 2) + h:4 * (u % 2) + h + 1])
                    nc.scalar.activation(DSK[:, 4 * (u % 2):4 * (u % 2) + 4], DSK[:, 4 * (u % 2):4 * (u % 2) + 4],
                                         ACT.Exp).then_inc(exp_done, 1)

                def copies(u):
                    b, g = units[u]
                    for i in range(min(NB, b + 2) - max(0, b - 1)):
                        act.wait_ge(probs_turned, kbs[0] + 1)
                        nc.scalar.copy(PT[:, u % 2, i, :], ps[:, 4 + i, :]).then_inc(pt_copied, 1)
                        kbs[0] += 1
                    act.wait_ge(o_out, u + 1)
                    nc.scalar.copy(ATT[:, 2 * g:2 * g + 2, b * P:(b + 1) * P],
                                   ps[:, 7, 0:2 * P].rearrange("p (a q) -> p a q", q=P)).then_inc(o_copied, 1)

                probs(0)
                for u in range(len(units)):
                    if u + 1 < len(units):
                        probs(u + 1)
                    copies(u)
                arrive(act)

                all_at(act, 1)
                act.wait_ge(pads_zero, 3)
                act.wait_ge(f_arg, 1)
                nc.scalar.activation(FR[0:HID, :], FA[:], ACT.Sin).then_inc(f_sin, 1)

                def hyena_copy(n):
                    act.wait_ge(hy_out, n + 1)
                    nc.scalar.copy(HYT[:, n, 1:SEQ + 1], ps[:, n % 4, :]).then_inc(hy_copied, 1)

                for n in range(4):
                    hyena_copy(n)
                act.wait_ge(f_arg, 2)
                nc.scalar.activation(FR[0:HID, :], FA[:], ACT.Sin).then_inc(f_sin, 1)
                for n in range(4, 8):
                    hyena_copy(n)
                for s in range(NB):
                    act.wait_ge(h3_out, s + 1)
                    if s >= 1:
                        act.wait_ge(hs_ready, s)
                    nc.scalar.copy(VT[:, 0, :], ps[:, 4 + 2 * (s % 2) + 1, :]).then_inc(h3_copied, 1)
                for n in range(8, 12):
                    hyena_copy(n)
                for n in range(2 * HC):
                    act.wait_ge(kf_out, n + 1)
                    nc.scalar.copy(KF[:, n % 2, n // 2, :], ps[:, n % 4, :]).then_inc(kf_copied, 1)
                for s in range(NB):
                    act.wait_ge(z_turned, s + 1)
                    nc.scalar.copy(ZTOK[:, s, :], ps[:, 4 + s, :]).then_inc(ztok_ready, 1)
                arrive(act)

                all_at(act, 2)
                for n in range(KC):
                    act.wait_ge(br_out, n + 1)
                    if n >= 2:
                        act.wait_ge(br_used, n - 1)
                    for i in range(2):
                        last = nc.scalar.activation(SG[:, n % 2, i, :], ps[:, 4 * (n % 2) + 2 * i + 1, :], ACT.Sigmoid)
                    last.then_inc(sg_ready, 1)
                arrive(act)

                all_at(act, 3)
                squares(NB, XS2)
                for n in range(2 * NB):
                    act.wait_ge(xnt_ready, 2 * NB + n + 1)
                    b, half = divmod(n, 2)
                    part = (slice(None), slice(4 * half, 4 * half + 4), slice(b * P, (b + 1) * P))
                    nc.scalar.copy(XHI[part], XN2[part]).then_inc(xhi_ready, 1)
                for n in range(HP):
                    act.wait_ge(pq_out, n + 1)
                    nc.scalar.copy(PQT[:, n, :], ps[:, n % 4, :]).then_inc(pq_copied, 1)
                for b in range(NB):
                    if b >= 1:
                        act.wait_ge(ps_free, b)
                    for i in range(4):
                        act.wait_ge(ps_out, 4 * b + i + 1)
                        nc.scalar.copy(PS[:, 4 * i:4 * i + 4, :].rearrange("p a k -> p (a k)"),
                                       ps[:, 4 + i, :]).then_inc(ps_copied, 1)
                    act.wait_ge(bmax_ready, b + 1)
                    nc.scalar.activation(SEL[:, 2, :], SEL[:, 2, :], ACT.Exp).then_inc(bexp_ready, 1)
                    act.wait_ge(sel_turned, b + 1)
                    nc.scalar.copy(IDXT[:, :, b * P:(b + 1) * P],
                                   ps[:, b, 0:3 * P].rearrange("p (a c) -> p a c", a=3)).then_inc(idx_copied, 1)
                arrive(act)

                all_at(act, 4)
                act.nop().then_inc(g_bank_free, 8)
                with act.Fori(0, SEQ // TOK_IT) as it:
                    for n in range(TOK_IT // 4):
                        s, c = divmod(4 * n, CB)
                        act.wait_ge(g_out, it * 32 + n + 5)
                        if c == 0:
                            act.wait_ge(g_stored[s], it * 16)
                        nc.scalar.copy(GST[:, s, :, c:c + 4].rearrange("p j c -> p c j"),
                                       ps[:, n % 8, :].rearrange("p (c j) -> p c j", c=4)).then_inc(g_bank_free, 1)
                arrive(act)

                all_at(act, 5)

                def split_u(g, jj):
                    j = g * 4 + jj
                    act.wait_ge(u_loaded[jj // 2], g * 16 + 16)
                    if not isinstance(j, int) or j >= JG:
                        act.wait_ge(u_done, j - 3)
                    nc.scalar.copy(UHI[:, jj].rearrange("p k i -> p (k i)"), URAW[:, jj // 2, jj % 2, :]).then_inc(u_hi, 1)

                def split_v(g, jj):
                    act.wait_ge(v_loaded[jj // 2], g * 16 + 16)
                    act.wait_ge(v_out, g * NOUT)
                    nc.scalar.copy(VHI[:, jj, :], VRAW[:, jj // 2, jj % 2, :]).then_inc(v_hi, 1)

                def gelu(j, jj):
                    act.wait_ge(u_done, j + 1)
                    if not isinstance(j, int) or j >= 2:
                        act.wait_ge(w_ready, j - 1)
                    nc.scalar.activation(AC[:, jj % 2, :], ps[:, jj % 2, :], ACT.Gelu).then_inc(act_ready, 1)

                def step(g, last=False):
                    for jj in range(JG):
                        if not last or jj < 2:
                            split_u(g + 1 + (2 + jj) // 4, (2 + jj) % 4)
                        split_v(g, jj)
                        gelu(g * 4 + 3 + jj, (3 + jj) % 4)

                for j in range(2):
                    split_u(0, j)
                for jj in range(JG):
                    split_u((jj + 2) // 4, (jj + 2) % 4)
                    if jj >= 1:
                        gelu(jj - 1, jj - 1)
                with act.Fori(0, NG - 2) as g:
                    step(g)
                step(NG - 2, last=True)
                gelu(NK - 1, 3)
                for jj in range(JG):
                    split_v(NG - 1, jj)
                end_layer(act, l)
            for b in range(NB):
                nc.scalar.activation(OUTB[:, 0, :], X[:, b, :], ACT.Square,
                                     accum_out=SS[:, b:b + 1]).then_inc(pre_sin, 1)
                act.wait_ge(pre_sin, 2 + b)
            act.wait_ge(pre_steps, FINAL_VAR)
            nc.scalar.activation(SR, SV, ACT.Sqrt).then_inc(pre_sin, 1)

        @block.vector
        def _(dve):
            pre = Steps(pre_steps)

            def reduce_angle(steps, r, a, k, quarter, shift):
                steps.did(nc.vector.tensor_scalar(k, a, 1.0 / (2 * math.pi), quarter, ALU.mult, ALU.add))
                steps.then(dve)
                steps.did(nc.vector.tensor_scalar(k, k, ROUND, ROUND, ALU.add, ALU.subtract))
                steps.then(dve)
                for i, c in enumerate((TWO_PI_HI, TWO_PI_MID, TWO_PI_LO)):
                    steps.did(nc.vector.scalar_tensor_tensor(r, k, -c, a if i == 0 else r, ALU.mult, ALU.add))
                    steps.then(dve)
                if shift:
                    steps.did(nc.vector.tensor_scalar(r, r, shift, None, ALU.add))
                    steps.then(dve)
                steps.did(nc.vector.tensor_scalar(r, r, PI_IN, -PI_IN, ALU.min, ALU.max))
                steps.then(dve)

            dve.wait_ge(x_loaded, 16)
            dve.wait_ge(pos_loaded, 16)
            dve.wait_ge(first_loads, 16)
            ang, kk = RT[:, 0, :, 0, :], RT[:, 1, :, 0, :]
            pre.did(nc.vector.tensor_copy(SV, POSF[:].bitcast(I32)))
            pre.then(dve)
            pre.did(nc.vector.tensor_tensor(ang, SV.unsqueeze(2).to_broadcast([P, NB, ROT]),
                                            CST[:, C_FREQ:C_FREQ + ROT].unsqueeze(1).to_broadcast([P, NB, ROT]), ALU.mult))
            pre.then(dve)
            reduce_angle(pre, SINCOS[:, 0], ang, kk, 0.0, 0.0)
            reduce_angle(pre, SINCOS[:, 1], ang, kk, 0.25, math.pi / 2)
            assert pre.n == SINCOS_ARGS
            dve.wait_ge(pre_sin, 1)

            def inverse_root(steps, n):
                steps.did(nc.vector.reciprocal(SR, SR))
                steps.then(dve)
                steps.did(nc.vector.tensor_tensor(ST, SR, SR, ALU.mult))
                steps.then(dve)
                steps.did(nc.vector.tensor_tensor(ST, ST, SV, ALU.mult))
                steps.then(dve)
                steps.did(nc.vector.tensor_scalar(ST, ST, -0.5, 1.5, ALU.mult, ALU.add))
                steps.then(dve)
                steps.did(nc.vector.tensor_tensor(SR, SR, ST, ALU.mult))
                steps.then(dve)

            def norm(steps, first, xs, xnt, gcol):
                dve.wait_ge(sumsq, first + NB)
                nc.vector.tensor_scalar(SV, SS, 1.0 / DM, EPS, ALU.mult, ALU.add).then_inc(var_ready, 1)
                dve.wait_ge(var_ready, first // NB + 1)
                dve.wait_ge(root_ready, first // NB + 1)
                inverse_root(steps, NB)
                scaled = lambda b: nc.vector.tensor_scalar(xs[:, b % 2, :], X[:, b, :], SR[:, b:b + 1], None,
                                                           ALU.mult).then_inc(xs_ready, 1)
                for b in range(NB + 1):
                    if b < NB:
                        if b >= 2:
                            dve.wait_ge(xs_turned, 2 * first + 2 * (b - 1))
                        scaled(b)
                    if b >= 1:
                        for half in range(2):
                            n = 2 * (b - 1) + half
                            dve.wait_ge(xs_turned, 2 * first + n + 1)
                            nc.vector.tensor_tensor(
                                xnt[:, 4 * half:4 * half + 4, (b - 1) * P:b * P],
                                ps[:, n % 4, :].rearrange("p (k c) -> p k c", k=4),
                                COL[:, gcol + 4 * half:gcol + 4 * half + 4].unsqueeze(2).to_broadcast([P, 4, P]),
                                ALU.mult).then_inc(xnt_ready, 1)

            with dve.Fori(0, DEPTH) as l:
                st = Steps(dve_steps)
                dve.wait_ge(params, P_A)
                norm(st, 0, XS, XNT, L_GMIX)
                dve.wait_ge(qkv_copied, 2 * NB)
                heads = QKV[:, :, 0:AW + KVW].rearrange("p b (h d) -> p b h d", d=HD)
                shape = [P, NB, QH + KVH, ROT]
                t1, t2 = heads[:, :, :, 0:ROT], heads[:, :, :, ROT:2 * ROT]
                sin, cos = (SINCOS[:, i].unsqueeze(2).to_broadcast(shape) for i in range(2))
                for i, (a, c) in enumerate(((t1, cos), (t2, sin), (t2, cos), (t1, sin))):
                    st.did(nc.vector.tensor_tensor(RT[:, i], a, c, ALU.mult))
                st.then(dve)
                nc.vector.tensor_tensor(t1, RT[:, 0], RT[:, 1], ALU.subtract)
                nc.vector.tensor_tensor(t2, RT[:, 2], RT[:, 3], ALU.add).then_inc(roped, 1)
                dve.wait_ge(roped, 1)
                for r in range(2):
                    nc.vector.tensor_copy(KREP[:, :, :, r, :], QKV[:, :, AW:AW + KVW].rearrange("p b (g d) -> p b g d", d=HD)
                                          ).then_inc(roped, 1)

                units = [(b, g) for b in range(NB) for g in range(KVH)]

                def take_scores(u):
                    b, g = units[u]
                    k0, k1 = max(0, b - 1), min(NB, b + 2)
                    n = (k1 - k0) * P
                    m0 = (k0 - (b - 1)) * P
                    m = MX[:, 4 * (u % 2):4 * (u % 2) + 4]
                    dve.wait_ge(sc_out, u + 1)
                    if u >= 2:
                        dve.wait_ge(probs_turned, kb_done[u - 2])
                    mask = CST[:, C_MASK + m0:C_MASK + m0 + n].unsqueeze(1).to_broadcast([P, GROUP, n])
                    nc.vector.scalar_tensor_tensor(SC[:, u % 2, :, 0:n], ps[:, 0:GROUP, 0:n], HD ** -0.5, mask,
                                                   ALU.mult, ALU.add).then_inc(sc_copied, 1)
                    dve.wait_ge(sc_copied, u + 1)
                    st.did(nc.vector.tensor_reduce(m, SC[:, u % 2, :, 0:n], axis=AX, op=ALU.max))
                    st.then(dve)
                    sink4 = SINK[:, GROUP * g:GROUP * g + 4]
                    st.did(nc.vector.tensor_tensor(m, m, sink4, ALU.max))
                    st.then(dve)
                    st.did(nc.vector.tensor_tensor(DSK[:, 4 * (u % 2):4 * (u % 2) + 4], sink4, m, ALU.subtract))
                    nc.vector.tensor_scalar(m, m, -1.0, None, ALU.mult).then_inc(mx_ready, 1)

                def normalise(u):
                    b, g = units[u]
                    n = (min(NB, b + 2) - max(0, b - 1)) * P
                    den = DEN[:, 4 * (u % 2):4 * (u % 2) + 4]
                    dve.wait_ge(exp_done, u + 1)
                    st.did(nc.vector.tensor_tensor(den, den, DSK[:, 4 * (u % 2):4 * (u % 2) + 4], ALU.add))
                    st.then(dve)
                    st.did(nc.vector.reciprocal(den, den))
                    st.then(dve)
                    for h in range(GROUP):
                        last = nc.vector.tensor_scalar(SC[:, u % 2, h, 0:n], SC[:, u % 2, h, 0:n], den[:, h:h + 1], None,
                                                       ALU.mult)
                    last.then_inc(probs_ready, 1)

                kb_done, total = [], 0
                for b, g in units:
                    total += min(NB, b + 2) - max(0, b - 1)
                    kb_done.append(total)
                take_scores(0)
                for u in range(len(units)):
                    if u + 1 < len(units):
                        take_scores(u + 1)
                    normalise(u)
                arrive(dve)

                all_at(dve, 1)
                dve.wait_ge(params, P_B)

                def short_conv(i, dst):
                    for c in range(HC):
                        n = HC * i + c
                        if c == 0:
                            dve.wait_ge(hy_copied, n + HC)
                        st.did(nc.vector.tensor_scalar(dst[:, c, :], HYT[:, n, 0:SEQ], COL[:, L_CONVW + 3 * n:L_CONVW + 3 * n + 1],
                                                       COL[:, L_CONVB + n:L_CONVB + n + 1], ALU.mult, ALU.add))
                    for tap in (1, 2):
                        st.then(dve)
                        for c in range(HC):
                            n = HC * i + c
                            w = COL[:, L_CONVW + 3 * n + tap:L_CONVW + 3 * n + tap + 1]
                            st.did(nc.vector.scalar_tensor_tensor(dst[:, c, :], HYT[:, n, tap:tap + SEQ], w, dst[:, c, :],
                                                                  ALU.mult, ALU.add))
                    st.then(dve)

                dve.wait_ge(pads_zero, 3)
                for i in range(2):
                    dve.wait_ge(f_out, i + 1)
                    if i == 1:
                        dve.wait_ge(f_sin, 1)
                    st.did(nc.vector.tensor_scalar(FA[:], ps[0:HID, 4 + i, :], FCOL[:, 2 * i:2 * i + 1],
                                                   FCOL[:, 2 * i + 1:2 * i + 2], ALU.add, ALU.mult))
                    st.then(dve)
                    reduce_angle(st, FA[:], FA[:], FK[:], 0.0, 0.0)
                    dve.nop().then_inc(f_arg, 1)
                    if i == 0:
                        short_conv(0, X0)
                dve.wait_ge(dec_loaded, 16)
                for s in range(NB):
                    f, b = ps[:, 4 + 2 * (s % 2), :], VT[:, 0, :]
                    dve.wait_ge(h3_copied, s + 1)
                    st.did(nc.vector.tensor_tensor(HS[:, 0, s, :], f, b, ALU.add))
                    st.did(nc.vector.tensor_tensor(HS[:, 1, s, :], f, b, ALU.subtract))
                    st.then(dve)
                    nc.vector.tensor_tensor(HS[:, 0, s, :], HS[:, 0, s, :], DEC[:, s, :], ALU.mult)
                    nc.vector.tensor_tensor(HS[:, 1, s, :], HS[:, 1, s, :], DEC[:, s, :], ALU.mult).then_inc(hs_ready, 1)
                short_conv(1, ZT)
                dve.wait_ge(hs_ready, NB)
                short_conv(2, VT)
                for c in range(HC):
                    nc.vector.tensor_tensor(ZT[:, c, :], ZT[:, c, :], VT[:, c, :], ALU.mult).then_inc(z_ready, 1)
                dve.wait_ge(kf_copied, 2 * HC)
                dve.wait_ge(z_ready, HC)
                for f in range(HC):
                    zr, zs = ps[:, 2 * (f % 2), :], ps[:, 2 * (f % 2) + 1, :]
                    kr, ks = KF[:, 0, f, :], KF[:, 1, f, :]
                    dve.wait_ge(zf_out, f + 1)
                    if f:
                        dve.wait_ge(yf_ready, f)
                    st.did(nc.vector.tensor_tensor(VT[:, 0, :], zr, kr, ALU.mult))
                    st.did(nc.vector.tensor_tensor(VT[:, 1, :], zs, ks, ALU.mult))
                    st.did(nc.vector.tensor_tensor(VT[:, 2, :], zr, ks, ALU.mult))
                    nc.vector.tensor_tensor(VT[:, 3, :], zs, kr, ALU.mult).then_inc(zf_used, 1)
                    dve.wait_ge(zf_used, f + 1)
                    nc.vector.tensor_tensor(YF[:, 0, f, :], VT[:, 0, :], VT[:, 1, :], ALU.subtract)
                    nc.vector.tensor_tensor(YF[:, 1, f, :], VT[:, 2, :], VT[:, 3, :], ALU.add).then_inc(yf_ready, 1)
                dve.wait_ge(yf_ready, HC)
                for c in range(HC):
                    dve.wait_ge(y_out, c + 1)
                    st.did(nc.vector.scalar_tensor_tensor(VT[:, c, :], ZT[:, c, :], COL[:, L_SKIP + c:L_SKIP + c + 1],
                                                          ps[:, 4 + c, :], ALU.mult, ALU.add))
                    st.then(dve)
                    nc.vector.tensor_tensor(YH[:, c, :], VT[:, c, :], X0[:, c, :], ALU.mult).then_inc(y_used, 1)
                arrive(dve)

                all_at(dve, 2)
                for n in range(KC):
                    dve.wait_ge(sg_ready, n + 1)
                    if n >= 2:
                        dve.wait_ge(mrg_ready, n - 1)
                    st.did(nc.vector.tensor_tensor(MP[:, n % 2, 0, :], ps[:, 4 * (n % 2), :], SG[:, n % 2, 0, :], ALU.mult))
                    nc.vector.tensor_tensor(MP[:, n % 2, 1, :], ps[:, 4 * (n % 2) + 2, :], SG[:, n % 2, 1, :],
                                            ALU.mult).then_inc(br_used, 1)
                    dve.wait_ge(br_used, n + 1)
                    nc.vector.tensor_tensor(MRG[:, n, :], MP[:, n % 2, 0, :], MP[:, n % 2, 1, :],
                                            ALU.add).then_inc(mrg_ready, 1)
                for n in range(2 * NB):
                    half, b = divmod(n, NB)
                    dve.wait_ge(wo_out, n + 1)
                    xb = X[:, b, 512 * half:512 * half + 512]
                    nc.vector.tensor_tensor(xb, ps[:, n % 4, :], xb, ALU.add).then_inc(wo_added, 1)
                arrive(dve)

                all_at(dve, 3)
                norm(st, NB, XS2, XN2, L_GFFN)
                for n in range(2 * NB):
                    b, half = divmod(n, 2)
                    part = (slice(None), slice(4 * half, 4 * half + 4), slice(b * P, (b + 1) * P))
                    dve.wait_ge(xhi_ready, n + 1)
                    dve.wait_ge(xnt_ready, 2 * NB + n + 1)
                    nc.vector.tensor_tensor(XLO[part], XN2[part], XHI[part].bitcast(F32), ALU.subtract)
                for b in range(NB):
                    if b >= 1:
                        st.then(dve)
                    for n in range(HP):
                        if n % 4 == 0:
                            dve.wait_ge(ps_copied, 4 * b + n // 4 + 1)
                        st.did(nc.vector.max(TV[:, n, 0:8], PS[:, n, :]))
                    st.then(dve)
                    for n in range(HP):
                        st.did(nc.vector.max_index(TI[:, n, 0:8], TV[:, n, 0:8], PS[:, n, :]))
                    st.then(dve)
                    for n in range(HP):
                        st.did(nc.vector.match_replace(PS[:, n, :], TV[:, n, 0:8], PS[:, n, :], NEG))
                    st.then(dve)
                    for n in range(HP):
                        st.did(nc.vector.max(TV[:, n, 8:16], PS[:, n, :]))
                    st.then(dve)
                    for n in range(HP):
                        last = nc.vector.max_index(TI[:, n, 8:16], TV[:, n, 8:16], PS[:, n, :])
                        if n < HP - 1:
                            st.did(last)
                    last.then_inc(ps_free, 1)
                    dve.wait_ge(ps_free, b + 1)
                    tv = TV[:].rearrange("p (h s) k -> p h s k", s=2)
                    st.did(nc.vector.tensor_tensor(CD[:], tv[:, :, 0, :].unsqueeze(3).to_broadcast([P, PH, TOPK, TOPK]),
                                                   tv[:, :, 1, :].unsqueeze(2).to_broadcast([P, PH, TOPK, TOPK]), ALU.add))
                    st.did(nc.vector.tensor_copy(TIF[:], TI[:]))
                    st.then(dve)
                    cd = [CD[:, h].rearrange("p a b -> p (a b)") for h in range(PH)]
                    for h in range(PH):
                        st.did(nc.vector.max(BV[:, h, 0:8], cd[h]))
                    st.then(dve)
                    for h in range(PH):
                        st.did(nc.vector.max_index(BP[:, h, 0:8], BV[:, h, 0:8], cd[h]))
                    st.then(dve)
                    for h in range(PH):
                        st.did(nc.vector.match_replace(cd[h], BV[:, h, 0:8], cd[h], NEG))
                    st.then(dve)
                    for h in range(PH):
                        st.did(nc.vector.max(BV[:, h, 8:16], cd[h]))
                    st.then(dve)
                    for h in range(PH):
                        st.did(nc.vector.max_index(BP[:, h, 8:16], BV[:, h, 8:16], cd[h]))
                    st.then(dve)
                    if b >= 1:
                        dve.wait_ge(sel_turned, b)
                    sel = [SEL[:, i, :].rearrange("p (h m) -> p h m", m=TOPK) for i in range(3)]
                    wide = [P, PH, TOPK]
                    nc.vector.tensor_tensor(sel[2], BV[:], BV[:, :, 0:1].to_broadcast(wide),
                                            ALU.subtract).then_inc(bmax_ready, 1)
                    bp = BP[:].rearrange("p h m -> p (h m)")
                    st.did(nc.vector.tensor_scalar(BA[:, 0, :], bp, 4, None, ALU.logical_shift_right))
                    st.did(nc.vector.tensor_scalar(BA[:, 1, :], bp, TOPK - 1, None, ALU.bitwise_and))
                    st.then(dve)
                    st.did(nc.vector.tensor_copy(BAF[:], BA[:]))
                    st.then(dve)
                    tif = TIF[:].rearrange("p (h s) k -> p h s k", s=2)
                    for i in range(2):
                        st.did(nc.vector.tensor_tensor(
                            EQ[:], BAF[:, i, :].unsqueeze(2).to_broadcast([P, PH * TOPK, TOPK]),
                            CST[:, C_IOTA16:C_IOTA16 + TOPK].unsqueeze(1).to_broadcast([P, PH * TOPK, TOPK]), ALU.is_equal))
                        st.then(dve)
                        eq = EQ[:].rearrange("p (h m) a -> p h m a", m=TOPK)
                        st.did(nc.vector.tensor_tensor(
                            eq, eq, tif[:, :, i, :].unsqueeze(2).to_broadcast([P, PH, TOPK, TOPK]), ALU.mult))
                        st.then(dve)
                        st.did(nc.vector.tensor_reduce(SEL[:, i, :], EQ[:], axis=AX, op=ALU.add))
                        st.then(dve)
                    dve.wait_ge(bexp_ready, b + 1)
                    st.did(nc.vector.tensor_reduce(GSUM, sel[2], axis=AX, op=ALU.add))
                    st.then(dve)
                    st.did(nc.vector.reciprocal(GSUM, GSUM))
                    st.then(dve)
                    nc.vector.tensor_tensor(sel[2], sel[2], GSUM.unsqueeze(2).to_broadcast(wide),
                                            ALU.mult).then_inc(sel_ready, 1)
                arrive(dve)

                all_at(dve, 4)
                with dve.Fori(0, SEQ // TOK_IT) as it:
                    src = IDXT[:, :, bass.ds(it * TOK_IT, TOK_IT)]
                    dve.wait_ge(oh_ready, it * 8)
                    nc.vector.tensor_copy(IST[:], src).then_inc(ist_steps, 1)
                    dve.wait_ge(ist_steps, it + 1)
                    for q in range(TOK_IT // OH):
                        dve.wait_ge(g_out, it * 32 + 4 * q)
                        for k in range(OH):
                            c = q * OH + k
                            nc.vector.tensor_scalar(OHA[:, q % 2, k, :], iota, IST[:, 0, c:c + 1], None, ALU.is_equal)
                            last = nc.vector.tensor_scalar(OHB[:, q % 2, k, :], iota, IST[:, 1, c:c + 1],
                                                           IST[:, 2, c:c + 1], ALU.is_equal, ALU.mult)
                        last.then_inc(oh_ready, 1)
                arrive(dve)

                all_at(dve, 5)
                dve.nop().then_inc(out_free, 4)

                def split_u(j, jj):
                    dve.wait_ge(u_hi, j + 1)
                    nc.vector.tensor_tensor(ULO[:, jj].rearrange("p k i -> p (k i)"), URAW[:, jj // 2, jj % 2, :],
                                            UHI[:, jj].rearrange("p k i -> p (k i)").bitcast(F32),
                                            ALU.subtract).then_inc(u_split, 1)

                def split_v(g, jj):
                    dve.wait_ge(v_hi, g * 4 + jj + 1)
                    nc.vector.tensor_tensor(VLO[:, jj, :], VRAW[:, jj // 2, jj % 2, :], VHI[:, jj, :].bitcast(F32),
                                            ALU.subtract).then_inc(v_split, 1)

                def weigh(j, jj, par, use):
                    blocks = "p (b c) -> p b c"
                    dve.wait_ge(act_ready, j + 1)
                    dve.wait_ge(g_loaded[par], use)
                    nc.vector.tensor_tensor(WF[:, jj % 2, :].rearrange(blocks, c=CB),
                                            AC[:, jj % 2, :].rearrange(blocks, c=CB), GT[:, par, :, jj, :],
                                            ALU.mult).then_inc(wf_ready, 1)
                    dve.wait_ge(wf_ready, j + 1)
                    nc.vector.tensor_copy(WHI[:, par, jj, :], WF[:, jj % 2, :]).then_inc(whi_ready, 1)
                    dve.wait_ge(whi_ready, j + 1)
                    nc.vector.tensor_tensor(WLO[:, par, jj, :], WF[:, jj % 2, :], WHI[:, par, jj, :].bitcast(F32),
                                            ALU.subtract).then_inc(w_ready, 1)

                def add_outputs(g):
                    for o in range(NOUT):
                        dh, b = divmod(o, NB)
                        xb = X[:, b, 512 * dh:512 * dh + 512]
                        dve.wait_ge(v_out, g * NOUT + o + 1)
                        nc.vector.tensor_tensor(xb, ps[:, 2 + o % 4, :], xb, ALU.add).then_inc(out_free, 1)

                def step(g, par, use, last=False):
                    for jj in range(JG):
                        if not last or jj < 2:
                            split_u(g * 4 + 6 + jj, (2 + jj) % 4)
                        split_v(g, jj)
                        if jj == 0:
                            weigh(g * 4 + 3, 3, par, use + 16)
                        else:
                            weigh(g * 4 + 3 + jj, jj - 1, 1 - par, use + 16 + 16 * par)
                    add_outputs(g)

                for j in range(2):
                    split_u(j, j)
                for jj in range(JG):
                    split_u(jj + 2, (jj + 2) % 4)
                    if jj >= 1:
                        weigh(jj - 1, jj - 1, 0, 16)
                with dve.Fori(0, (NG - 2) // 2) as it:
                    step(it * 2, 0, it * 16)
                    step(it * 2 + 1, 1, it * 16)
                step(NG - 2, 0, 8 * (NG - 2), last=True)
                weigh(NK - 1, 3, 1, 8 * NG)
                for jj in range(JG):
                    split_v(NG - 1, jj)
                add_outputs(NG - 1)
                end_layer(dve, l)

            dve.wait_ge(pre_sin, 1 + NB)
            pre.did(nc.vector.tensor_scalar(SV, SS, 1.0 / DM, EPS, ALU.mult, ALU.add))
            assert pre.n == FINAL_VAR
            dve.wait_ge(pre_sin, 2 + NB)
            inverse_root(pre, NB)
            dve.wait_ge(first_loads, 32)
            for b in range(NB):
                pre.did(nc.vector.tensor_scalar(OUTB[:, b, :], X[:, b, :], SR[:, b:b + 1], None, ALU.mult))
            pre.then(dve)
            assert pre.n == FINAL0
            for b in range(NB):
                pre.did(nc.vector.tensor_tensor(OUTB[:, b, :], OUTB[:, b, :], GFIN[:], ALU.mult))


def shape_tables():
    f4 = np.float32
    const = np.zeros((P, NCONST), f4)
    const[:, C_ID:C_ID + P] = np.eye(P)
    const[:, C_IOTA:C_IOTA + NK] = np.arange(NK)
    q, k = np.arange(P)[:, None], np.arange(3 * P)[None, :] - P
    const[:, C_MASK:C_MASK + 3 * P] = np.where(np.abs(q - k) <= P, 0.0, -1e30)
    const[:, C_IOTA16:C_IOTA16 + TOPK] = np.arange(TOPK)
    const[:, C_FREQ:C_FREQ + ROT] = f4(500000.0) ** (-np.arange(0, 2 * ROT, 2, dtype=f4) / f4(2 * ROT))
    t = np.linspace(0.0, 1.0, SEQ, dtype=f4)[:, None]
    bands = (EMB - 1) // 2
    w = f4(2.0 * math.pi) * np.arange(SEQ, dtype=f4)[:, None] / f4(SEQ)
    f = np.linspace(1e-4, bands - 1, bands, dtype=f4)[None, :]
    fw = (f * w).astype(f4)
    zemb = np.concatenate([t, np.cos(fw), -np.sin(fw)], axis=1).astype(f4).T
    lo, hi = math.log(1e-2) / 1.5, math.log(1e-2) / 0.3
    deltas = np.abs(np.linspace(lo, hi, HW, dtype=f4))[None, :]
    decay = np.exp(-t * deltas).astype(f4).reshape(NB, P, HW).transpose(1, 0, 2)
    ang = (2 * math.pi / (2 * SEQ)) * np.outer(np.arange(SEQ), np.arange(SEQ) + 0.5)
    both = np.stack([np.cos(ang), np.sin(ang)], axis=1)
    fwd = both.reshape(NB, P, 2, SEQ).transpose(1, 0, 2, 3).reshape(P, -1)
    inv = (both / SEQ).transpose(2, 1, 0).reshape(NB, P, 2, SEQ).transpose(1, 0, 2, 3).reshape(P, -1)
    return [np.ascontiguousarray(a, dtype=f4) for a in (const, zemb, decay, fwd, inv)]


def kernel(x, positions, norm_mix, w_in, conv_w, conv_b, filt_w1, filt_b1, filt_freq1, filt_w2, filt_b2, filt_freq2,
           filt_w3, filt_b3, hyena_skip, attn_sink, w_attn_branch, w_hyena_branch, w_out, norm_ffn, w_query, sub_keys,
           expert_u, expert_v, norm_final):
    import concourse.bacc as bacc
    from concourse.bass_utils import run_bass_kernel_spmd

    def chunks(a, n):
        return np.asarray(a).reshape(DEPTH, n, P).transpose(0, 2, 1)

    const, zemb, decay, fwd, inv = shape_tables()
    conv = np.asarray(conv_w).reshape(DEPTH, 3, NHY, P).transpose(0, 3, 2, 1).reshape(DEPTH, P, 3 * NHY)
    cols = np.concatenate([chunks(norm_mix, KC), chunks(norm_ffn, KC), conv, chunks(conv_b, NHY), chunks(hyena_skip, HC)], axis=2)
    fcols = np.stack([np.asarray(a) for a in (filt_b1, filt_freq1, filt_b2, filt_freq2)], axis=2)
    w3 = np.concatenate([np.asarray(filt_w3), np.asarray(filt_b3)[:, None, :]], axis=1)
    ut = (np.asarray(expert_u).reshape(DEPTH, NK, NK // 2, 2, KC, P).transpose(0, 2, 5, 3, 4, 1)
          .reshape(DEPTH, NK // 2, P, 2, KC * P))
    v = np.asarray(expert_v).reshape(DEPTH, NK, NK // 2, 2, DM).transpose(0, 2, 1, 3, 4)
    given = {
        "x": np.asarray(x).reshape(SEQ, DM), "positions": np.asarray(positions).reshape(SEQ), "consts": const,
        "gfinal": np.asarray(norm_final), "cols": cols, "fcols": fcols, "sink": np.asarray(attn_sink),
        "w1": np.asarray(filt_w1), "w2": np.asarray(filt_w2), "w3": w3, "zemb": zemb, "decay": decay,
        "fwd": fwd, "inv": inv, "w_in": np.asarray(w_in), "w_ab": np.asarray(w_attn_branch),
        "w_hb": np.asarray(w_hyena_branch), "w_out": np.asarray(w_out), "w_q": np.asarray(w_query),
        "keys": np.asarray(sub_keys).transpose(0, 3, 1, 2), "ut": ut, "v": v,
    }
    nc = bacc.Bacc("TRN2", target_bir_lowering=False, num_devices=1)
    arrays, args = {}, []
    for name, a in given.items():
        a = np.ascontiguousarray(a)
        arrays[f"{name}_dram"] = a
        args.append(nc.dram_tensor(f"{name}_dram", a.shape, mybir.dt.from_np(a.dtype), kind="ExternalInput").ap())
    args.append(nc.dram_tensor("out_dram", (SEQ, DM), F32, kind="ExternalOutput").ap())
    encoder(nc, *args)
    got = run_bass_kernel_spmd(nc, [arrays], core_ids=[0]).results[0]["out_dram"]
    return got.reshape(1, SEQ, DM)
```

```python
import math
from contextlib import ExitStack

import numpy as np
import concourse.bass as bass
from concourse import mybir

F32 = mybir.dt.float32
F32R = mybir.dt.float32r
I32 = mybir.dt.int32
U32 = mybir.dt.uint32
ACT = mybir.ActivationFunctionType
ALU = mybir.AluOpType
AX = mybir.AxisListType.X

P = 128
DEPTH, SEQ, DM = 2, 512, 1024
NB = SEQ // P
KC = DM // P
QH, KVH, HD = 8, 2, 64
GROUP = QH // KVH
ROT = HD // 8
AW, KVW = QH * HD, KVH * HD
HW = 512
HC = HW // P
NHY = 3 * HC
EMB, HID = 33, 64
HY0 = AW + 2 * KVW
GA0 = HY0 + 3 * HW
GH0 = GA0 + DM
NK, PH, TOPK = 128, 8, 16
HP = 2 * PH
QG = 4
HG = QG // 2
NGRP = HP // QG
CAND = TOPK * TOPK
EPS = 1e-6
NEG = -3.0e38
TWO_PI_HI = 6.28125
TWO_PI_MID = float(np.float32(0.0019350051879882812))
TWO_PI_LO = float(np.float32(2 * math.pi - TWO_PI_HI - TWO_PI_MID))
PI_IN = 3.1415925
ROUND = 1.5 * 2 ** 23

C_ID, C_IOTA, C_MASK, C_IOTA16, C_FREQ = 0, 128, 256, 640, 656
NCONST = C_FREQ + ROT
L_GMIX, L_GFFN, L_CONVW, L_CONVB, L_SKIP = 0, 8, 16, 16 + 3 * NHY, 16 + 4 * NHY
NCOL = L_SKIP + HC + 1
L_BASE = NCOL - 1

T_Q, T_KV, T_HY, T_FWD, T_INV, T_BR, T_OUT, T_PQ = 0, 1, 2, 5, 6, 7, 15, 17
NTILES = T_PQ + 4
RING = 3

NPAR = 9
TOK_IT = 128
CB = 64
OH, OHR = 8, 4
OHN = TOK_IT // OH
JG = 4
NG = NK // JG
DB = 3
DT = DB * P
NOUT = 2 * DB
PICKS = PH * TOPK
GR, GS = 4, 8
GSTEPS = PICKS // GS
SLOTS = [range(i * NOUT // JG, (i + 1) * NOUT // JG) for i in range(JG)]


class Steps:

    def __init__(self, sem):
        self.sem, self.n = sem, 0

    def did(self, ins):
        ins.then_inc(self.sem, 1)
        self.n += 1
        return self.n

    def then(self, eng, n=None):
        eng.wait_ge(self.sem, self.n if n is None else n)


def tile_uses():
    parts = [1] * NTILES
    for n in range(KC):
        parts[T_BR + n] = 4
    got, out = [0] * RING, []
    for t in range(NTILES):
        got[t % RING] += 16 * parts[t]
        out.append((t % RING, got[t % RING]))
    return out


def encoder(nc, x, positions, consts, gfinal, gffn, cols, fcols, sink, w1, w2, w3, zemb, decay, fwd, inv,
            w_in, w_ab, w_hb, w_out, w_q, keys, ut, v,
            u_rows, v_rows, out):
    ctx = ExitStack()
    at = [16512]

    def sb(name, shape, dt=F32, offset=None):
        size = 4 * int(np.prod(shape[1:]))
        size = (size + 31) // 32 * 32
        if offset is None:
            offset = at[0]
            at[0] += size
        t = nc.alloc_sbuf_tensor_at(name, shape, dt, offset=offset)
        return t, offset

    def sem(name):
        return nc.alloc_semaphore(name)

    X, _ = sb("X", [P, NB, DM])
    CST, _ = sb("CST", [P, NCONST])
    COL, _ = sb("COL", [P, NCOL])
    FCOL, _ = sb("FCOL", [HID, 4])
    SINK, _ = sb("SINK", [P, QH])
    SINCOS, _ = sb("SINCOS", [P, 2, NB, ROT])
    SMALL, _ = sb("SMALL", [P, 64])
    WR, wr_at = sb("WR", [P, RING, 4096])
    phase_at = at[0]
    ident = CST[:, C_ID:C_ID + P]
    iota = CST[:, C_IOTA:C_IOTA + NK]

    XNT, _ = sb("XNT", [P, KC, SEQ])
    MRG, mrg_at = sb("MRG", [P, KC, SEQ])
    ATT, _ = sb("ATT", [P, 4, SEQ])
    YH, yh_at = sb("YH", [P, HC, SEQ])
    abc_at = at[0]
    KF, _ = sb("KF", [P, 2, HC, HW], offset=mrg_at)
    DEC, _ = sb("DEC", [P, NB, HW], offset=yh_at)
    XS, xs_at = sb("XS", [P, 2, DM])
    QKV, _ = sb("QKV", [P, NB, HY0])
    KREP, _ = sb("KREP", [P, NB, KVH, 2, HD])
    QT, _ = sb("QT", [P, 4, SEQ])
    KT, _ = sb("KT", [P, KVH, SEQ])
    SC, _ = sb("SC", [P, 2, GROUP, 3 * P])
    PT, _ = sb("PT", [P, 2, 3, GROUP * P])
    RT, _ = sb("RT", [P, 4, NB, QH + KVH, ROT])
    end_a = at[0]
    at[0] = abc_at
    HYT, _ = sb("HYT", [P, NHY, SEQ + 2])
    X0, _ = sb("X0", [P, HC, SEQ])
    ZT, _ = sb("ZT", [P, HC, SEQ])
    VT, _ = sb("VT", [P, HC, SEQ])
    ZTOK, _ = sb("ZTOK", [P, NB, HW])
    HS, hs_at = sb("HS", [P, 2, NB, HW])
    YF, _ = sb("YF", [P, 2, HC, HW], offset=hs_at)
    FA, _ = sb("FA", [HID, SEQ])
    FK, _ = sb("FK", [HID, SEQ])
    FR, _ = sb("FR", [HID + 1, SEQ])
    W1, _ = sb("W1", [EMB, HID])
    W2, _ = sb("W2", [HID, HID])
    W3, w3_at = sb("W3", [HID + 1, 2 * HW])
    ZE, _ = sb("ZE", [EMB, SEQ])
    end_b = at[0]
    at[0] = abc_at
    SG, _ = sb("SG", [P, 2, 2, SEQ])
    MP, _ = sb("MP", [P, 2, 2, SEQ])
    at[0] = phase_at
    XHI, _ = sb("XHI", [P, KC, DT], F32R)
    XLO, _ = sb("XLO", [P, KC, DT], F32R)
    XG, _ = sb("XG", [P, DM])
    GI, _ = sb("GI", [P, PICKS], I32)
    GG, _ = sb("GG", [P, PICKS])
    IDXT, idxt_at = sb("IDXT", [P, 3, DT])
    def_at = at[0]
    XN2, _ = sb("XN2", [P, KC, SEQ])
    XS2, _ = sb("XS2", [P, 2, DM])
    KEY, _ = sb("KEY", [P, 2, NK])
    GF, _ = sb("GF", [P, DM])
    GIF, _ = sb("GIF", [P, PICKS])
    PQT, _ = sb("PQT", [P, 2, QG, SEQ])
    PS, _ = sb("PS", [P, 2, NB, QG, NK])
    CD, _ = sb("CD", [P, NB * HG, TOPK, TOPK])
    EQ, _ = sb("EQ", [P, NB * HG * TOPK, TOPK])
    TV, _ = sb("TV", [P, NB * QG, TOPK])
    TI, _ = sb("TI", [P, NB * QG, TOPK], U32)
    TIF, _ = sb("TIF", [P, NB * QG, TOPK])
    BV, _ = sb("BV", [P, NB * HG, TOPK])
    BP, _ = sb("BP", [P, NB * HG, TOPK], U32)
    BA, _ = sb("BA", [P, 2, NB * HG * TOPK], U32)
    BAF, _ = sb("BAF", [P, 2, NB * HG * TOPK])
    SELG, _ = sb("SELG", [P, 2, NB * HG, TOPK])
    BE, _ = sb("BE", [P, 2, NB * HG, TOPK])
    SEL, _ = sb("SEL", [P, 3, NB, PH, TOPK])
    end_d = at[0]
    at[0] = def_at
    OHS, _ = sb("OHS", [P, OHR, 2, OH, NK])
    GST, _ = sb("GST", [P, 2, NK, CB])
    end_e = at[0]
    URAW, _ = sb("URAW", [P, 2, 2, DM], offset=wr_at)
    VRAW, _ = sb("VRAW", [P, 2, JG, 512], offset=wr_at + 16384)
    GT, _ = sb("GT", [P, 2, DT // CB, JG, CB], offset=wr_at + 32768)
    at[0] = idxt_at
    UHI, _ = sb("UHI", [P, JG, KC, P], F32R)
    ULO, _ = sb("ULO", [P, JG, KC, P], F32R)
    VHI, _ = sb("VHI", [P, 2, JG, 512], F32R)
    VLO, _ = sb("VLO", [P, 2, JG, 512], F32R)
    WHI, _ = sb("WHI", [P, 2, JG, DT], F32R)
    WLO, _ = sb("WLO", [P, 2, JG, DT], F32R)
    AC, _ = sb("AC", [P, 2, DT])
    WF, _ = sb("WF", [P, 2, DT])
    ROWS, _ = sb("ROWS", [P, GR, DM])
    GIS, _ = sb("GIS", [P, 2, GS], I32)
    DOT, _ = sb("DOT", [P, PICKS])
    GW, _ = sb("GW", [P, PICKS])
    STG, _ = sb("STG", [P, 2, GS])
    end_f = at[0]
    OUTB, _ = sb("OUTB", [P, NB, DM], offset=phase_at)
    GFIN, _ = sb("GFIN", [P, DM], offset=phase_at + 16384)
    assert max(end_a, end_b, end_d, end_e, end_f) <= nc.sbuf_usable_end, (end_a, end_b, end_d, end_e, end_f)

    ps = nc.alloc_psum_tensor("ps", [P, 8, 512], F32)
    gd = nc.dram_tensor("g_table", (DT // CB, P, NK, CB), F32, kind="Internal").ap()

    SS, SV, SR, ST = SMALL[:, 0:4], SMALL[:, 4:8], SMALL[:, 8:12], SMALL[:, 12:16]
    MX, DSK, DEN, POSF = SMALL[:, 16:24], SMALL[:, 24:32], SMALL[:, 32:40], SMALL[:, 40:44]
    GMX, GSUM = SMALL[:, 44:52], SMALL[:, 52:60]

    first_loads, x_loaded, pos_loaded = sem("first_loads"), sem("x_loaded"), sem("pos_loaded")
    pre_steps, out_stored, next_layer = sem("pre_steps"), sem("out_stored"), sem("next_layer")
    pre_sin = sem("pre_sin")
    went_on = sem("went_on")
    layer_sems = []

    def lsem(name):
        layer_sems.append(sem(name))
        return layer_sems[-1]

    engines_done = lsem("engines_done")
    phase = lsem("phase")
    params = lsem("params")
    w_loaded = [lsem(f"w_loaded{i}") for i in range(RING)]
    act_steps, dve_steps = lsem("act_steps"), lsem("dve_steps")
    sumsq, var_ready, root_ready = lsem("sumsq"), lsem("var_ready"), lsem("root_ready")
    xs_ready, xs_turned, xnt_ready = lsem("xs_ready"), lsem("xs_turned"), lsem("xnt_ready")
    qkv_out, qkv_copied, roped = lsem("qkv_out"), lsem("qkv_copied"), lsem("roped")
    qk_turned, qk_copied = lsem("qk_turned"), lsem("qk_copied")
    sc_out, sc_copied, mx_ready, exp_done = lsem("sc_out"), lsem("sc_copied"), lsem("mx_ready"), lsem("exp_done")
    probs_ready, probs_turned, pt_copied = lsem("probs_ready"), lsem("probs_turned"), lsem("pt_copied")
    o_out, o_copied = lsem("o_out"), lsem("o_copied")
    pads_zero, hy_out, hy_copied = lsem("pads_zero"), lsem("hy_out"), lsem("hy_copied")
    f_out, f_arg, f_sin = lsem("f_out"), lsem("f_arg"), lsem("f_sin")
    h3_out, h3_copied, hs_ready, dec_loaded = lsem("h3_out"), lsem("h3_copied"), lsem("hs_ready"), lsem("dec_loaded")
    kf_out, kf_copied = lsem("kf_out"), lsem("kf_copied")
    z_ready, z_turned, ztok_ready = lsem("z_ready"), lsem("z_turned"), lsem("ztok_ready")
    zf_out, zf_used, yf_ready = lsem("zf_out"), lsem("zf_used"), lsem("yf_ready")
    y_out, y_used = lsem("y_out"), lsem("y_used")
    br_out, sg_ready, br_used, mrg_ready = lsem("br_out"), lsem("sg_ready"), lsem("br_used"), lsem("mrg_ready")
    wo_out, wo_added = lsem("wo_out"), lsem("wo_added")
    xhi_ready = lsem("xhi_ready")
    pq_out, pq_copied, ps_out, ps_copied, ps_free = lsem("pq_out"), lsem("pq_copied"), lsem("ps_out"), lsem("ps_copied"), lsem("ps_free")
    bmax_ready, bexp_ready = lsem("bmax_ready"), lsem("bexp_ready")
    sel_ready, sel_turned, idx_copied = lsem("sel_ready"), lsem("sel_turned"), lsem("idx_copied")
    oh_made = lsem("oh_made")
    oh_ready, g_out, g_bank_free = lsem("oh_ready"), lsem("g_out"), lsem("g_bank_free")
    gst_free = lsem("gst_free")
    g_stored = [lsem(f"g_stored{i}") for i in range(2)]
    u_loaded = [lsem(f"u_loaded{i}") for i in range(2)]
    v_loaded = [lsem(f"v_loaded{i}") for i in range(2)]
    g_loaded = [lsem(f"g_loaded{i}") for i in range(2)]
    u_hi, u_split, u_done = lsem("u_hi"), lsem("u_split"), lsem("u_done")
    v_hi, v_split = lsem("v_hi"), lsem("v_split")
    stg_ready, dots_done, gelu_done, gw_ready = lsem("stg_ready"), lsem("dots_done"), lsem("gelu_done"), lsem("gw_ready")
    rows_used, gis_ready, pool_went = lsem("rows_used"), lsem("gis_ready"), lsem("pool_went")
    rows_loaded = [sem(f"rows_loaded{i}") for i in range(GR)]
    ROWS_LAYER = 16 * 2 * PICKS // GR
    act_ready, wf_ready, whi_ready, w_ready = lsem("act_ready"), lsem("wf_ready"), lsem("whi_ready"), lsem("w_ready")
    v_out, out_free = lsem("v_out"), lsem("out_free")

    TILE = tile_uses()

    tile_done = ([(qkv_out, 2 * NB)] * 2 + [(hy_out, 4 * i + 4) for i in range(3)] + [(zf_out, HC), (y_out, HC)]
                 + [(br_out, n + 1) for n in range(KC)] + [(wo_out, NB * i + NB) for i in range(2)]
                 + [(pq_out, 4 * i + 4) for i in range(4)])
    assert len(tile_done) == NTILES

    def need_tile(e, t):
        e.wait_ge(w_loaded[TILE[t][0]], TILE[t][1])

    def arrive(e):
        e.drain().then_inc(phase, 1)

    def all_at(e, n):
        e.wait_ge(phase, 3 * n)

    def end_layer(e, l):
        e.drain().then_inc(engines_done, 1)
        e.wait_ge(next_layer, l + 1)
        e.nop().then_inc(went_on, 1)

    SINCOS_ARGS, FINAL_VAR, FINAL0 = 15, 16, 25

    with nc.Block() as block:

        @block.sync
        def _(sp):
            sp.dma_start(X[:], x.rearrange("(b p) d -> p b d", p=P)).then_inc(x_loaded, 16)
            sp.dma_start(CST[:], consts).then_inc(first_loads, 16)
            with sp.Fori(0, DEPTH) as l:
                loaded = [0]

                def weights(parts):
                    t = loaded[0]
                    loaded[0] += 1
                    if t >= RING:
                        sp.wait_ge(*tile_done[t - RING])
                    for dst, src in parts:
                        sp.dma_start(dst(WR[:, t % RING, :]), src).then_inc(w_loaded[t % RING], 16)

                def cols_of(w, c0, n, kc=KC):
                    return w[l, :, c0:c0 + n].rearrange("(k p) n -> p k n", p=P)

                def at_cols(o, kc, n):
                    return lambda s: s[:, o:o + kc * n].rearrange("p (k n) -> p k n", n=n)

                sp.dma_start(COL[:], cols[l]).then_inc(params, 16)
                sp.dma_start(SINK[:], sink[l].partition_broadcast(P)).then_inc(params, 16)
                sp.dma_start(FCOL[:], fcols[l]).then_inc(params, 16)
                weights([(at_cols(0, KC, AW), cols_of(w_in, 0, AW))])
                weights([(at_cols(0, KC, 2 * KVW), cols_of(w_in, AW, 2 * KVW))])
                for i in range(3):
                    weights([(at_cols(0, KC, 512), cols_of(w_in, HY0 + 512 * i, 512))])
                all_at(sp, 1)
                sp.dma_start(W1[:], w1[l]).then_inc(params, 16)
                sp.dma_start(W2[:], w2[l]).then_inc(params, 16)
                sp.dma_start(W3[:], w3[l]).then_inc(params, 16)
                sp.dma_start(ZE[:], zemb).then_inc(params, 16)
                sp.dma_start(DEC[:], decay).then_inc(dec_loaded, 16)
                weights([(lambda s: s, fwd)])
                weights([(lambda s: s, inv)])
                for n in range(KC):
                    weights([(at_cols(0, KC, P), cols_of(w_in, GA0 + P * n, P)),
                             (at_cols(KC * P, KC, P), cols_of(w_in, GH0 + P * n, P)),
                             (at_cols(2 * KC * P, 4, P), cols_of(w_ab, P * n, P)),
                             (at_cols((2 * KC + 4) * P, 4, P), cols_of(w_hb, P * n, P))])
                for i in range(2):
                    weights([(at_cols(0, KC, 512), cols_of(w_out, 512 * i, 512))])
                for i in range(4):
                    if i == 3:
                        all_at(sp, 3)
                        sp.dma_start(KEY[:], keys[l]).then_inc(params, 16)
                        sp.dma_start(GF[:], gffn[l].partition_broadcast(P)).then_inc(params, 16)
                    weights([(at_cols(0, KC, 512), cols_of(w_q, 512 * i, 512))])
                all_at(sp, 4)
                sp.nop().then_inc(gst_free, 2)
                with sp.Fori(0, DT // TOK_IT) as it:
                    for s in range(2):
                        dst = gd[it * 2 + s].rearrange("i j c -> i (j c)")
                        sp.wait_ge(g_bank_free, it * 32 + 16 * (s + 1) + 8)
                        sp.dma_start(dst, GST[:, s].rearrange("p j c -> p (j c)")).then_inc(g_stored[s], 16)
                    for s in range(2):
                        sp.wait_ge(g_stored[s], it * 16 + 16)
                        sp.nop().then_inc(gst_free, 1)
                for s in range(2):
                    sp.wait_ge(g_stored[s], 16 * (DT // TOK_IT))
                all_at(sp, 5)

                def load_u(jp, slot):
                    sp.dma_start(URAW[:, slot], ut[l, jp]).then_inc(u_loaded[slot], 16)

                def load_v(g, dh):
                    sp.dma_start(VRAW[:, dh], v[l, g, dh]).then_inc(v_loaded[dh], 16)

                def load_g(g, slot):
                    src = gd[:, :, bass.ds(g * JG, JG), :].rearrange("b i j c -> i b (j c)")
                    sp.dma_start(GT[:, slot].rearrange("p b j c -> p b (j c)"), src).then_inc(g_loaded[slot], 16)

                def step(g, par, last=False):
                    sp.wait_ge(u_split, g * 4 + 4)
                    load_u(g * 2 + 3, 1)
                    sp.wait_ge(v_split, g * 8 + 4)
                    load_v(g + 1, 0)
                    if not last:
                        sp.wait_ge(w_ready, g * 4 + 4)
                        load_g(g + 2, par)
                        sp.wait_ge(u_split, g * 4 + 6)
                        load_u(g * 2 + 4, 0)
                    sp.wait_ge(v_split, g * 8 + 8)
                    load_v(g + 1, 1)

                load_u(0, 0)
                load_g(0, 0)
                load_u(1, 1)
                load_v(0, 0)
                sp.wait_ge(u_split, 2)
                load_u(2, 0)
                load_v(0, 1)
                load_g(1, 1)
                with sp.Fori(0, (NG - 2) // 2) as it:
                    step(it * 2, 0)
                    step(it * 2 + 1, 1)
                step(NG - 2, 0, last=True)
                end_layer(sp, l)
            sp.dma_start(GFIN[:], gfinal.partition_broadcast(P)).then_inc(first_loads, 16)
            for b in range(NB):
                sp.wait_ge(pre_steps, FINAL0 + b + 1)
                sp.dma_start(out[b * P:(b + 1) * P, :], OUTB[:, b, :]).then_inc(out_stored, 16)
            sp.wait_ge(out_stored, 16 * NB)

        @block.gpsimd
        def _(pool):
            with nc.allow_non_contiguous_dma("positions and sinks are a few words"):
                pool.dma_start(POSF[:].bitcast(I32), positions.rearrange("(b p) -> p b", p=P)).then_inc(pos_loaded, 16)
            with pool.Fori(0, DEPTH) as l:
                all_at(pool, 1)
                pool.memset(HYT[:, :, 0:1], 0.0).then_inc(pads_zero, 1)
                pool.memset(HYT[:, :, SEQ + 1:SEQ + 2], 0.0).then_inc(pads_zero, 1)
                pool.wait_ge(pads_zero, 2)
                pool.memset(FR[HID:HID + 1, :], 1.0).then_inc(pads_zero, 1)
                all_at(pool, 4)
                with pool.Fori(0, DT // TOK_IT) as it:
                    for q in range(TOK_IT // OH):
                        gates = IDXT[:, 2, bass.ds(it * TOK_IT + q * OH, OH)]
                        pool.wait_ge(oh_made, it * OHN + q + 1)
                        nc.gpsimd.tensor_tensor(OHS[:, q % OHR, 1], OHS[:, q % OHR, 1],
                                                gates.unsqueeze(2).to_broadcast([P, OH, NK]), ALU.mult).then_inc(oh_ready, 1)
                all_at(pool, 5)

                def rows(table, it, par, before):
                    s = it * 2 + par
                    nc.gpsimd.tensor_copy(GIS[:, par, :], GI[:, bass.ds(s * GS, GS)]).then_inc(gis_ready, 1)
                    pool.wait_ge(gis_ready, s + (before + 1))
                    pool.nop().then_inc(pool_went, 1)
                    for k in range(GS):
                        pool.wait_ge(rows_used, s * GS + (before * GS + k + 1))
                        pool.nop().then_inc(pool_went, 1)
                        pool.indirect_dma_start(out=ROWS[:, k % GR, :], out_offset=None, in_=table,
                                                in_offset=bass.IndirectOffsetOnAxis(ap=GIS[:, par, k:k + 1], axis=0)
                                                ).then_inc(rows_loaded[k % GR], 16)

                for table, before in ((u_rows, 0), (v_rows, GSTEPS)):
                    with pool.Fori(0, GSTEPS // 2) as it:
                        rows(table, it, 0, before)
                        rows(table, it, 1, before)
                pool.wait_ge(engines_done, 4)
                for s in layer_sems:
                    pool.sem_clear(s)
                pool.nop().then_inc(next_layer, 1)

        P_A, P_B, P_D = 16 * 3, 16 * 7, 16 * 9

        @block.tensor
        def _(pe):
            pe.wait_ge(first_loads, 16)

            def turn_norm(first, xs):
                for b in range(NB):
                    pe.wait_ge(xs_ready, first + b + 1)
                    for half in range(2):
                        n = 2 * b + half
                        if n >= 4:
                            pe.wait_ge(xnt_ready, 2 * first + n - 3)
                        for k in range(4):
                            last = nc.tensor.transpose(ps[:, n % 4, k * P:(k + 1) * P],
                                                       xs[:, b % 2, (half * 4 + k) * P:(half * 4 + k + 1) * P], ident)
                        last.then_inc(xs_turned, 1)

            with pe.Fori(0, DEPTH) as l:
                turn_norm(0, XS)
                need_tile(pe, T_Q)
                need_tile(pe, T_KV)
                wq = WR[:, T_Q % RING, :].rearrange("p (k n) -> p k n", n=AW)
                wkv = WR[:, T_KV % RING, 0:KC * 2 * KVW].rearrange("p (k n) -> p k n", n=2 * KVW)
                for b in range(NB):
                    pe.wait_ge(xnt_ready, 2 * b + 2)
                    if b >= 2:
                        pe.wait_ge(qkv_copied, 2 * (b - 1))
                    for (w, n, o) in ((wq, AW, 0), (wkv, 2 * KVW, 1)):
                        for k in range(KC):
                            last = nc.tensor.matmul(ps[:, 4 + 2 * (b % 2) + o, 0:n], XNT[:, k, b * P:(b + 1) * P],
                                                    w[:, k, :], start=(k == 0), stop=(k == KC - 1))
                        last.then_inc(qkv_out, 1)
                pe.wait_ge(roped, 3)
                pe.wait_ge(qkv_copied, 2 * NB)
                for c in range(4 + KVH):
                    for b in range(NB):
                        src = (QKV[:, b, c * P:(c + 1) * P] if c < 4 else
                               KREP[:, b, c - 4].rearrange("p r d -> p (r d)"))
                        last = nc.tensor.transpose(ps[:, c, b * P:(b + 1) * P], src, ident)
                    last.then_inc(qk_turned, 1)
                pe.wait_ge(qk_copied, 4 + KVH)

                units = [(b, g) for b in range(NB) for g in range(KVH)]

                def keys_of(b):
                    return max(0, b - 1), min(NB, b + 2)

                def scores(u):
                    b, g = units[u]
                    k0, k1 = keys_of(b)
                    if u >= 1:
                        pe.wait_ge(sc_copied, u)
                    for h in range(GROUP):
                        head = GROUP * g + h
                        rows = slice(HD * (head % 2), HD * (head % 2) + HD)
                        last = nc.tensor.matmul(ps[:, h, 0:(k1 - k0) * P], QT[rows, head // 2, b * P:(b + 1) * P],
                                                KT[rows, g, k0 * P:k1 * P], start=True, stop=True)
                    last.then_inc(sc_out, 1)

                scores(0)
                kbs = 0
                for u, (b, g) in enumerate(units):
                    if u + 1 < len(units):
                        scores(u + 1)
                    k0, k1 = keys_of(b)
                    pe.wait_ge(probs_ready, u + 1)
                    if u >= 1:
                        pe.wait_ge(pt_copied, kbs)
                    for i in range(k1 - k0):
                        for h in range(GROUP):
                            last = nc.tensor.transpose(ps[:, 4 + i, h * P:(h + 1) * P],
                                                       SC[:, u % 2, h, i * P:(i + 1) * P], ident)
                        last.then_inc(probs_turned, 1)
                    kbs += k1 - k0
                    pe.wait_ge(pt_copied, kbs)
                    if u >= 1:
                        pe.wait_ge(o_copied, u)
                    for odd in range(2):
                        for i in range(k1 - k0):
                            pt = PT[:, u % 2, i, :].rearrange("p (a b q) -> p b a q", b=2, q=P)
                            last = nc.tensor.matmul(
                                ps[HD * odd:HD * odd + HD, 7, 0:2 * P].rearrange("p (a q) -> p a q", q=P),
                                QKV[:, k0 + i, AW + KVW + g * HD:AW + KVW + (g + 1) * HD],
                                pt[:, odd], start=(i == 0), stop=(i == k1 - k0 - 1))
                    last.then_inc(o_out, 1)
                arrive(pe)

                all_at(pe, 1)
                pe.wait_ge(params, P_B)
                pe.wait_ge(pads_zero, 3)
                nc.tensor.matmul(ps[0:HID, 4, :], W1[:], ZE[:], start=True, stop=True).then_inc(f_out, 1)

                def hyena_in(n):
                    t = T_HY + n // 4
                    if n % 4 == 0:
                        need_tile(pe, t)
                    if n >= 4:
                        pe.wait_ge(hy_copied, n - 3)
                    w = WR[:, t % RING, :].rearrange("p (k n) -> p k n", n=512)
                    for k in range(KC):
                        last = nc.tensor.matmul(ps[:, n % 4, :], w[:, k, (n % 4) * P:(n % 4 + 1) * P], XNT[:, k, :],
                                                start=(k == 0), stop=(k == KC - 1))
                    last.then_inc(hy_out, 1)

                for n in range(4):
                    hyena_in(n)
                pe.wait_ge(f_sin, 1)
                nc.tensor.matmul(ps[0:HID, 5, :], W2[:], FR[0:HID, :], start=True, stop=True).then_inc(f_out, 1)
                for n in range(4, 8):
                    hyena_in(n)
                pe.wait_ge(f_sin, 2)
                for s in range(NB):
                    if s >= 2:
                        pe.wait_ge(hs_ready, s - 1)
                    for i in range(2):
                        last = nc.tensor.matmul(ps[:, 4 + 2 * (s % 2) + i, :], FR[:, s * P:(s + 1) * P],
                                                W3[:, i * HW:(i + 1) * HW], start=True, stop=True)
                    last.then_inc(h3_out, 1)
                for n in range(8, 12):
                    hyena_in(n)
                need_tile(pe, T_FWD)
                ft = WR[:, T_FWD % RING, :].rearrange("p (s r f) -> p s r f", s=NB, r=2)
                pe.wait_ge(hs_ready, NB)
                pe.wait_ge(hy_copied, NHY)
                for f in range(HC):
                    for r in range(2):
                        n = 2 * f + r
                        if n >= 4:
                            pe.wait_ge(kf_copied, n - 3)
                        for s in range(NB):
                            last = nc.tensor.matmul(ps[:, n % 4, :], ft[:, s, r, f * P:(f + 1) * P], HS[:, r, s, :],
                                                    start=(s == 0), stop=(s == NB - 1))
                        last.then_inc(kf_out, 1)
                pe.wait_ge(z_ready, HC)
                for s in range(NB):
                    for c in range(HC):
                        last = nc.tensor.transpose(ps[:, 4 + s, c * P:(c + 1) * P], ZT[:, c, s * P:(s + 1) * P], ident)
                    last.then_inc(z_turned, 1)
                pe.wait_ge(ztok_ready, NB)
                pe.wait_ge(kf_copied, 2 * HC)
                for f in range(HC):
                    if f >= 2:
                        pe.wait_ge(zf_used, f - 1)
                    for r in range(2):
                        for s in range(NB):
                            last = nc.tensor.matmul(ps[:, 2 * (f % 2) + r, :], ft[:, s, r, f * P:(f + 1) * P],
                                                    ZTOK[:, s, :], start=(s == 0), stop=(s == NB - 1))
                    last.then_inc(zf_out, 1)
                need_tile(pe, T_INV)
                vt = WR[:, T_INV % RING, :].rearrange("p (f r t) -> p f r t", f=HC, r=2)
                pe.wait_ge(yf_ready, HC)
                for c in range(HC):
                    for f in range(HC):
                        for r in range(2):
                            last = nc.tensor.matmul(ps[:, 4 + c, :], YF[:, r, f, c * P:(c + 1) * P], vt[:, f, r, :],
                                                    start=(f == 0 and r == 0), stop=(f == HC - 1 and r == 1))
                    last.then_inc(y_out, 1)
                arrive(pe)

                all_at(pe, 2)
                for n in range(KC):
                    t = T_BR + n
                    need_tile(pe, t)
                    if n >= 2:
                        pe.wait_ge(br_used, n - 1)
                    w = WR[:, t % RING, 0:24 * P].rearrange("p (k n) -> p k n", n=P)
                    for bank, k0, nk, src in ((0, 16, 4, ATT), (1, 0, 8, XNT), (2, 20, 4, YH), (3, 8, 8, XNT)):
                        for k in range(nk):
                            last = nc.tensor.matmul(ps[:, 4 * (n % 2) + bank, :], w[:, k0 + k, :], src[:, k, :],
                                                    start=(k == 0), stop=(k == nk - 1))
                    last.then_inc(br_out, 1)
                pe.wait_ge(mrg_ready, KC)
                for half in range(2):
                    t = T_OUT + half
                    need_tile(pe, t)
                    w = WR[:, t % RING, :].rearrange("p (k n) -> p k n", n=512)
                    for b in range(NB):
                        n = half * NB + b
                        if n >= 4:
                            pe.wait_ge(wo_added, n - 3)
                        for k in range(KC):
                            last = nc.tensor.matmul(ps[:, n % 4, :], MRG[:, k, b * P:(b + 1) * P], w[:, k, :],
                                                    start=(k == 0), stop=(k == KC - 1))
                        last.then_inc(wo_out, 1)
                arrive(pe)

                all_at(pe, 3)
                turn_norm(NB, XS2)
                pe.wait_ge(xnt_ready, 4 * NB)
                pe.wait_ge(params, P_D)

                def queries(i):
                    need_tile(pe, T_PQ + i)
                    w = WR[:, (T_PQ + i) % RING, :].rearrange("p (k n) -> p k n", n=512)
                    for m in range(QG):
                        n = QG * i + m
                        if n >= 4:
                            pe.wait_ge(pq_copied, n - 3)
                        for k in range(KC):
                            last = nc.tensor.matmul(ps[:, m, :], w[:, k, m * P:(m + 1) * P], XN2[:, k, :],
                                                    start=(k == 0), stop=(k == KC - 1))
                        last.then_inc(pq_out, 1)

                def expert_scores(i):
                    pe.wait_ge(pq_copied, QG * (i + 1))
                    for b in range(NB):
                        if i >= 1:
                            pe.wait_ge(ps_copied, NB * (i - 1) + b + 1)
                        for m in range(QG):
                            last = nc.tensor.matmul(ps[:, 4 + b, m * NK:(m + 1) * NK], PQT[:, i % 2, m, b * P:(b + 1) * P],
                                                    KEY[:, m % 2, :], start=True, stop=True)
                        last.then_inc(ps_out, 1)

                queries(0)
                for i in range(NGRP):
                    expert_scores(i)
                    if i + 1 < NGRP:
                        queries(i + 1)
                pe.wait_ge(sel_ready, NGRP)
                for b in range(DB):
                    for i in range(3):
                        last = nc.tensor.transpose(ps[:, b, i * P:(i + 1) * P],
                                                   SEL[:, i, b].rearrange("p h m -> p (h m)"), ident)
                    last.then_inc(sel_turned, 1)
                arrive(pe)

                all_at(pe, 4)
                pe.nop().then_inc(g_out, OHR * (OH // 4))
                with pe.Fori(0, DT // TOK_IT) as it:
                    for q in range(TOK_IT // OH):
                        pe.wait_ge(oh_ready, it * OHN + q + 1)
                        for s in range(OH // 4):
                            n = q * (OH // 4) + s
                            pe.wait_ge(g_bank_free, it * 32 + n + 1)
                            for k in range(4):
                                last = nc.tensor.matmul(ps[:, n % 8, k * NK:(k + 1) * NK], OHS[:, q % OHR, 0, 4 * s + k, :],
                                                        OHS[:, q % OHR, 1, 4 * s + k, :], start=True, stop=True)
                            last.then_inc(g_out, 1)
                arrive(pe)

                all_at(pe, 5)

                pe.nop().then_inc(v_out, 1)

                def up(j, jj):
                    pe.wait_ge(u_split, j + 1)
                    if not isinstance(j, int) or j >= JG:
                        pe.wait_ge(act_ready, j - 3)
                    parts = [(UHI, XHI), (UHI, XLO), (ULO, XHI)]
                    for i, (a, c) in enumerate(parts):
                        for k in range(KC):
                            last = nc.tensor.matmul(ps[:, jj, 0:DT], a[:, jj, k, :], c[:, k, :],
                                                    start=(i == 0 and k == 0), stop=(i == 2 and k == KC - 1))
                    last.then_inc(u_done, 1)

                def down(g, par, o):
                    dh, b = divmod(o, DB)
                    if o == 0:
                        pe.wait_ge(w_ready, g * 4 + 4)
                    if b == 0:
                        pe.wait_ge(v_split, g * 8 + 4 * dh + 4)
                    pe.wait_ge(out_free, g * NOUT + o + 1)
                    n, g0 = 0, par * NOUT
                    for a, c in ((WHI, VHI), (WHI, VLO), (WLO, VHI)):
                        for jj in range(JG):
                            last = nc.tensor.matmul(ps[:, 4 + (g0 + o) % 4, :], a[:, par, jj, b * P:(b + 1) * P],
                                                    c[:, dh, jj, :], start=(n == 0), stop=(n == 3 * JG - 1))
                            n += 1
                    last.then_inc(v_out, 1)

                def step(g, par, more=True):
                    for jj in range(JG):
                        if more:
                            up(g * 4 + 4 + jj, jj)
                        for o in SLOTS[jj]:
                            down(g, par, o)

                for jj in range(JG):
                    up(jj, jj)
                with pe.Fori(0, (NG - 2) // 2) as it:
                    step(it * 2, 0)
                    step(it * 2 + 1, 1)
                step(NG - 2, 0)
                step(NG - 1, 1, more=False)
                end_layer(pe, l)

        @block.scalar
        def _(act):
            act.wait_ge(pre_steps, SINCOS_ARGS)
            nc.scalar.activation(SINCOS[:], SINCOS[:], ACT.Sin).then_inc(pre_sin, 1)
            act.wait_ge(x_loaded, 16)

            def squares(n, xs):
                for b in range(NB):
                    nc.scalar.activation(xs[:, 0, :], X[:, b, :], ACT.Square,
                                         accum_out=SS[:, b:b + 1]).then_inc(sumsq, 1)
                    act.wait_ge(sumsq, n + b + 1)
                act.wait_ge(var_ready, n // NB + 1)
                nc.scalar.activation(SR, SV, ACT.Sqrt).then_inc(root_ready, 1)

            with act.Fori(0, DEPTH) as l:
                squares(0, XS)
                for b in range(NB):
                    for o, n, c0 in ((0, AW, 0), (1, 2 * KVW, AW)):
                        act.wait_ge(qkv_out, 2 * b + o + 1)
                        nc.scalar.copy(QKV[:, b, c0:c0 + n], ps[:, 4 + 2 * (b % 2) + o, 0:n]).then_inc(qkv_copied, 1)
                for c in range(4 + KVH):
                    act.wait_ge(qk_turned, c + 1)
                    dst = QT[:, c, :] if c < 4 else KT[:, c - 4, :]
                    nc.scalar.copy(dst, ps[:, c, :]).then_inc(qk_copied, 1)
                units = [(b, g) for b in range(NB) for g in range(KVH)]
                kbs = [0]

                def probs(u):
                    b, g = units[u]
                    n = (min(NB, b + 2) - max(0, b - 1)) * P
                    act.wait_ge(mx_ready, u + 1)
                    for h in range(GROUP):
                        nc.scalar.activation(SC[:, u % 2, h, 0:n], SC[:, u % 2, h, 0:n], ACT.Exp,
                                             bias=MX[:, 4 * (u % 2) + h:4 * (u % 2) + h + 1],
                                             accum_out=DEN[:, 4 * (u % 2) + h:4 * (u % 2) + h + 1])
                    nc.scalar.activation(DSK[:, 4 * (u % 2):4 * (u % 2) + 4], DSK[:, 4 * (u % 2):4 * (u % 2) + 4],
                                         ACT.Exp).then_inc(exp_done, 1)

                def copies(u):
                    b, g = units[u]
                    for i in range(min(NB, b + 2) - max(0, b - 1)):
                        act.wait_ge(probs_turned, kbs[0] + 1)
                        nc.scalar.copy(PT[:, u % 2, i, :], ps[:, 4 + i, :]).then_inc(pt_copied, 1)
                        kbs[0] += 1
                    act.wait_ge(o_out, u + 1)
                    nc.scalar.copy(ATT[:, 2 * g:2 * g + 2, b * P:(b + 1) * P],
                                   ps[:, 7, 0:2 * P].rearrange("p (a q) -> p a q", q=P)).then_inc(o_copied, 1)

                probs(0)
                for u in range(len(units)):
                    if u + 1 < len(units):
                        probs(u + 1)
                    copies(u)
                arrive(act)

                all_at(act, 1)
                act.wait_ge(pads_zero, 3)
                act.wait_ge(f_arg, 1)
                nc.scalar.activation(FR[0:HID, :], FA[:], ACT.Sin).then_inc(f_sin, 1)

                def hyena_copy(n):
                    act.wait_ge(hy_out, n + 1)
                    nc.scalar.copy(HYT[:, n, 1:SEQ + 1], ps[:, n % 4, :]).then_inc(hy_copied, 1)

                for n in range(4):
                    hyena_copy(n)
                act.wait_ge(f_arg, 2)
                nc.scalar.activation(FR[0:HID, :], FA[:], ACT.Sin).then_inc(f_sin, 1)
                for n in range(4, 8):
                    hyena_copy(n)
                for s in range(NB):
                    act.wait_ge(h3_out, s + 1)
                    if s >= 1:
                        act.wait_ge(hs_ready, s)
                    nc.scalar.copy(VT[:, 0, :], ps[:, 4 + 2 * (s % 2) + 1, :]).then_inc(h3_copied, 1)
                for n in range(8, 12):
                    hyena_copy(n)
                for n in range(2 * HC):
                    act.wait_ge(kf_out, n + 1)
                    nc.scalar.copy(KF[:, n % 2, n // 2, :], ps[:, n % 4, :]).then_inc(kf_copied, 1)
                for s in range(NB):
                    act.wait_ge(z_turned, s + 1)
                    nc.scalar.copy(ZTOK[:, s, :], ps[:, 4 + s, :]).then_inc(ztok_ready, 1)
                arrive(act)

                all_at(act, 2)
                for n in range(KC):
                    act.wait_ge(br_out, n + 1)
                    if n >= 2:
                        act.wait_ge(br_used, n - 1)
                    for i in range(2):
                        last = nc.scalar.activation(SG[:, n % 2, i, :], ps[:, 4 * (n % 2) + 2 * i + 1, :], ACT.Sigmoid)
                    last.then_inc(sg_ready, 1)
                arrive(act)

                all_at(act, 3)
                squares(NB, XS2)
                for n in range(2 * DB):
                    act.wait_ge(xnt_ready, 2 * NB + n + 1)
                    b, half = divmod(n, 2)
                    part = (slice(None), slice(4 * half, 4 * half + 4), slice(b * P, (b + 1) * P))
                    nc.scalar.copy(XHI[part], XN2[part]).then_inc(xhi_ready, 1)
                for i in range(NGRP + 1):
                    if i < NGRP:
                        for m in range(QG):
                            n = QG * i + m
                            act.wait_ge(pq_out, n + 1)
                            if m == 0 and i >= 2:
                                act.wait_ge(ps_out, NB * (i - 1))
                            nc.scalar.copy(PQT[:, i % 2, m, :], ps[:, m, :]).then_inc(pq_copied, 1)
                        if i >= 2:
                            act.wait_ge(ps_free, i - 1)
                        for b in range(NB):
                            act.wait_ge(ps_out, NB * i + b + 1)
                            nc.scalar.copy(PS[:, i % 2, b].rearrange("p m k -> p (m k)"),
                                           ps[:, 4 + b, :]).then_inc(ps_copied, 1)
                    if i >= 1:
                        act.wait_ge(bmax_ready, i)
                        nc.scalar.activation(BE[:, (i - 1) % 2], BE[:, (i - 1) % 2], ACT.Exp).then_inc(bexp_ready, 1)
                for b in range(DB):
                    act.wait_ge(sel_turned, b + 1)
                    nc.scalar.copy(IDXT[:, :, b * P:(b + 1) * P],
                                   ps[:, b, 0:3 * P].rearrange("p (a c) -> p a c", a=3)).then_inc(idx_copied, 1)
                arrive(act)

                all_at(act, 4)
                act.nop().then_inc(g_bank_free, 8)
                with act.Fori(0, DT // TOK_IT) as it:
                    for n in range(TOK_IT // 4):
                        s, c = divmod(4 * n, CB)
                        act.wait_ge(g_out, it * 32 + n + 1 + OHR * (OH // 4))
                        if c == 0:
                            act.wait_ge(gst_free, it * 2 + s + 1)
                        nc.scalar.copy(GST[:, s, :, c:c + 4].rearrange("p j c -> p c j"),
                                       ps[:, n % 8, :].rearrange("p (c j) -> p c j", c=4)).then_inc(g_bank_free, 1)
                arrive(act)

                all_at(act, 5)

                def split_u(g, jj):
                    j = g * 4 + jj
                    act.wait_ge(u_loaded[jj // 2], g * 16 + 16)
                    if not isinstance(j, int) or j >= JG:
                        act.wait_ge(u_done, j - 3)
                    nc.scalar.copy(UHI[:, jj].rearrange("p k i -> p (k i)"), URAW[:, jj // 2, jj % 2, :]).then_inc(u_hi, 1)

                def split_v(g, dh, pair):
                    if pair == 0:
                        act.wait_ge(v_loaded[dh], g * 16 + 16)
                        if dh == 1:
                            act.wait_ge(v_out, g * NOUT + 1)
                        elif not isinstance(g, int) or g >= 1:
                            act.wait_ge(v_out, g * NOUT - (NOUT // 2 - 1))
                    for jj in (2 * pair, 2 * pair + 1):
                        nc.scalar.copy(VHI[:, dh, jj, :], VRAW[:, dh, jj, :]).then_inc(v_hi, 1)

                def gelu(j, jj):
                    act.wait_ge(u_done, j + 1)
                    if not isinstance(j, int) or j >= 2:
                        act.wait_ge(w_ready, j - 1)
                    nc.scalar.activation(AC[:, jj % 2, :], ps[:, jj, 0:DT], ACT.Gelu).then_inc(act_ready, 1)

                def step(g, columns=True, first=False, ahead=JG):
                    for jj in range(JG):
                        if columns and jj < ahead:
                            split_u(g + 1 + (2 + jj) // 4, (2 + jj) % 4)
                        if jj < 2 and not first:
                            split_v(g, 1, jj)
                        if jj >= 2 and columns:
                            split_v(g + 1, 0, jj - 2)
                        if columns:
                            gelu(g * 4 + 4 + jj, jj)

                split_u(0, 0)
                split_u(0, 1)
                step(-1, first=True)
                with act.Fori(0, GSTEPS) as g:
                    step(g)
                act.wait_ge(dots_done, GSTEPS)
                nc.scalar.activation(DOT[:], DOT[:], ACT.Gelu).then_inc(gelu_done, 1)
                with act.Fori(GSTEPS, NG - 2) as g:
                    step(g)
                step(NG - 2, ahead=2)
                step(NG - 1, columns=False)
                end_layer(act, l)
            for b in range(NB):
                nc.scalar.activation(OUTB[:, 0, :], X[:, b, :], ACT.Square,
                                     accum_out=SS[:, b:b + 1]).then_inc(pre_sin, 1)
                act.wait_ge(pre_sin, 2 + b)
            act.wait_ge(pre_steps, FINAL_VAR)
            nc.scalar.activation(SR, SV, ACT.Sqrt).then_inc(pre_sin, 1)

        @block.vector
        def _(dve):
            pre = Steps(pre_steps)

            def reduce_angle(steps, r, a, k, quarter, shift):
                steps.did(nc.vector.tensor_scalar(k, a, 1.0 / (2 * math.pi), quarter, ALU.mult, ALU.add))
                steps.then(dve)
                steps.did(nc.vector.tensor_scalar(k, k, ROUND, ROUND, ALU.add, ALU.subtract))
                steps.then(dve)
                for i, c in enumerate((TWO_PI_HI, TWO_PI_MID, TWO_PI_LO)):
                    steps.did(nc.vector.scalar_tensor_tensor(r, k, -c, a if i == 0 else r, ALU.mult, ALU.add))
                    steps.then(dve)
                if shift:
                    steps.did(nc.vector.tensor_scalar(r, r, shift, None, ALU.add))
                    steps.then(dve)
                steps.did(nc.vector.tensor_scalar(r, r, PI_IN, -PI_IN, ALU.min, ALU.max))
                steps.then(dve)

            dve.wait_ge(x_loaded, 16)
            dve.wait_ge(pos_loaded, 16)
            dve.wait_ge(first_loads, 16)
            ang, kk = RT[:, 0, :, 0, :], RT[:, 1, :, 0, :]
            pre.did(nc.vector.tensor_copy(SV, POSF[:].bitcast(I32)))
            pre.then(dve)
            pre.did(nc.vector.tensor_tensor(ang, SV.unsqueeze(2).to_broadcast([P, NB, ROT]),
                                            CST[:, C_FREQ:C_FREQ + ROT].unsqueeze(1).to_broadcast([P, NB, ROT]), ALU.mult))
            pre.then(dve)
            reduce_angle(pre, SINCOS[:, 0], ang, kk, 0.0, 0.0)
            reduce_angle(pre, SINCOS[:, 1], ang, kk, 0.25, math.pi / 2)
            assert pre.n == SINCOS_ARGS
            dve.wait_ge(pre_sin, 1)

            def inverse_root(steps, n):
                steps.did(nc.vector.reciprocal(SR, SR))
                steps.then(dve)
                steps.did(nc.vector.tensor_tensor(ST, SR, SR, ALU.mult))
                steps.then(dve)
                steps.did(nc.vector.tensor_tensor(ST, ST, SV, ALU.mult))
                steps.then(dve)
                steps.did(nc.vector.tensor_scalar(ST, ST, -0.5, 1.5, ALU.mult, ALU.add))
                steps.then(dve)
                steps.did(nc.vector.tensor_tensor(SR, SR, ST, ALU.mult))
                steps.then(dve)

            def norm(steps, first, xs, xnt, gcol):
                dve.wait_ge(sumsq, first + NB)
                nc.vector.tensor_scalar(SV, SS, 1.0 / DM, EPS, ALU.mult, ALU.add).then_inc(var_ready, 1)
                dve.wait_ge(var_ready, first // NB + 1)
                dve.wait_ge(root_ready, first // NB + 1)
                inverse_root(steps, NB)
                scaled = lambda b: nc.vector.tensor_scalar(xs[:, b % 2, :], X[:, b, :], SR[:, b:b + 1], None,
                                                           ALU.mult).then_inc(xs_ready, 1)
                for b in range(NB + 1):
                    if b < NB:
                        if b >= 2:
                            dve.wait_ge(xs_turned, 2 * first + 2 * (b - 1))
                        scaled(b)
                    if b >= 1:
                        for half in range(2):
                            n = 2 * (b - 1) + half
                            dve.wait_ge(xs_turned, 2 * first + n + 1)
                            nc.vector.tensor_tensor(
                                xnt[:, 4 * half:4 * half + 4, (b - 1) * P:b * P],
                                ps[:, n % 4, :].rearrange("p (k c) -> p k c", k=4),
                                COL[:, gcol + 4 * half:gcol + 4 * half + 4].unsqueeze(2).to_broadcast([P, 4, P]),
                                ALU.mult).then_inc(xnt_ready, 1)

            with dve.Fori(0, DEPTH) as l:
                st = Steps(dve_steps)
                dve.wait_ge(params, P_A)
                norm(st, 0, XS, XNT, L_GMIX)
                dve.wait_ge(qkv_copied, 2 * NB)
                heads = QKV[:, :, 0:AW + KVW].rearrange("p b (h d) -> p b h d", d=HD)
                shape = [P, NB, QH + KVH, ROT]
                t1, t2 = heads[:, :, :, 0:ROT], heads[:, :, :, ROT:2 * ROT]
                sin, cos = (SINCOS[:, i].unsqueeze(2).to_broadcast(shape) for i in range(2))
                for i, (a, c) in enumerate(((t1, cos), (t2, sin), (t2, cos), (t1, sin))):
                    st.did(nc.vector.tensor_tensor(RT[:, i], a, c, ALU.mult))
                st.then(dve)
                nc.vector.tensor_tensor(t1, RT[:, 0], RT[:, 1], ALU.subtract)
                nc.vector.tensor_tensor(t2, RT[:, 2], RT[:, 3], ALU.add).then_inc(roped, 1)
                dve.wait_ge(roped, 1)
                for r in range(2):
                    nc.vector.tensor_copy(KREP[:, :, :, r, :], QKV[:, :, AW:AW + KVW].rearrange("p b (g d) -> p b g d", d=HD)
                                          ).then_inc(roped, 1)

                units = [(b, g) for b in range(NB) for g in range(KVH)]

                def take_scores(u):
                    b, g = units[u]
                    k0, k1 = max(0, b - 1), min(NB, b + 2)
                    n = (k1 - k0) * P
                    m0 = (k0 - (b - 1)) * P
                    m = MX[:, 4 * (u % 2):4 * (u % 2) + 4]
                    dve.wait_ge(sc_out, u + 1)
                    if u >= 2:
                        dve.wait_ge(probs_turned, kb_done[u - 2])
                    mask = CST[:, C_MASK + m0:C_MASK + m0 + n].unsqueeze(1).to_broadcast([P, GROUP, n])
                    nc.vector.scalar_tensor_tensor(SC[:, u % 2, :, 0:n], ps[:, 0:GROUP, 0:n], HD ** -0.5, mask,
                                                   ALU.mult, ALU.add).then_inc(sc_copied, 1)
                    dve.wait_ge(sc_copied, u + 1)
                    st.did(nc.vector.tensor_reduce(m, SC[:, u % 2, :, 0:n], axis=AX, op=ALU.max))
                    st.then(dve)
                    sink4 = SINK[:, GROUP * g:GROUP * g + 4]
                    st.did(nc.vector.tensor_tensor(m, m, sink4, ALU.max))
                    st.then(dve)
                    st.did(nc.vector.tensor_tensor(DSK[:, 4 * (u % 2):4 * (u % 2) + 4], sink4, m, ALU.subtract))
                    nc.vector.tensor_scalar(m, m, -1.0, None, ALU.mult).then_inc(mx_ready, 1)

                def normalise(u):
                    b, g = units[u]
                    n = (min(NB, b + 2) - max(0, b - 1)) * P
                    den = DEN[:, 4 * (u % 2):4 * (u % 2) + 4]
                    dve.wait_ge(exp_done, u + 1)
                    st.did(nc.vector.tensor_tensor(den, den, DSK[:, 4 * (u % 2):4 * (u % 2) + 4], ALU.add))
                    st.then(dve)
                    st.did(nc.vector.reciprocal(den, den))
                    st.then(dve)
                    for h in range(GROUP):
                        last = nc.vector.tensor_scalar(SC[:, u % 2, h, 0:n], SC[:, u % 2, h, 0:n], den[:, h:h + 1], None,
                                                       ALU.mult)
                    last.then_inc(probs_ready, 1)

                kb_done, total = [], 0
                for b, g in units:
                    total += min(NB, b + 2) - max(0, b - 1)
                    kb_done.append(total)
                take_scores(0)
                for u in range(len(units)):
                    if u + 1 < len(units):
                        take_scores(u + 1)
                    normalise(u)
                arrive(dve)

                all_at(dve, 1)
                dve.wait_ge(params, P_B)

                def short_conv(i, dst):
                    for c in range(HC):
                        n = HC * i + c
                        if c == 0:
                            dve.wait_ge(hy_copied, n + HC)
                        st.did(nc.vector.tensor_scalar(dst[:, c, :], HYT[:, n, 0:SEQ], COL[:, L_CONVW + 3 * n:L_CONVW + 3 * n + 1],
                                                       COL[:, L_CONVB + n:L_CONVB + n + 1], ALU.mult, ALU.add))
                    for tap in (1, 2):
                        st.then(dve)
                        for c in range(HC):
                            n = HC * i + c
                            w = COL[:, L_CONVW + 3 * n + tap:L_CONVW + 3 * n + tap + 1]
                            st.did(nc.vector.scalar_tensor_tensor(dst[:, c, :], HYT[:, n, tap:tap + SEQ], w, dst[:, c, :],
                                                                  ALU.mult, ALU.add))
                    st.then(dve)

                dve.wait_ge(pads_zero, 3)
                for i in range(2):
                    dve.wait_ge(f_out, i + 1)
                    if i == 1:
                        dve.wait_ge(f_sin, 1)
                    st.did(nc.vector.tensor_scalar(FA[:], ps[0:HID, 4 + i, :], FCOL[:, 2 * i:2 * i + 1],
                                                   FCOL[:, 2 * i + 1:2 * i + 2], ALU.add, ALU.mult))
                    st.then(dve)
                    reduce_angle(st, FA[:], FA[:], FK[:], 0.0, 0.0)
                    dve.nop().then_inc(f_arg, 1)
                    if i == 0:
                        short_conv(0, X0)
                dve.wait_ge(dec_loaded, 16)
                for s in range(NB):
                    f, b = ps[:, 4 + 2 * (s % 2), :], VT[:, 0, :]
                    dve.wait_ge(h3_copied, s + 1)
                    st.did(nc.vector.tensor_tensor(HS[:, 0, s, :], f, b, ALU.add))
                    st.did(nc.vector.tensor_tensor(HS[:, 1, s, :], f, b, ALU.subtract))
                    st.then(dve)
                    nc.vector.tensor_tensor(HS[:, 0, s, :], HS[:, 0, s, :], DEC[:, s, :], ALU.mult)
                    nc.vector.tensor_tensor(HS[:, 1, s, :], HS[:, 1, s, :], DEC[:, s, :], ALU.mult).then_inc(hs_ready, 1)
                short_conv(1, ZT)
                dve.wait_ge(hs_ready, NB)
                short_conv(2, VT)
                for c in range(HC):
                    nc.vector.tensor_tensor(ZT[:, c, :], ZT[:, c, :], VT[:, c, :], ALU.mult).then_inc(z_ready, 1)
                dve.wait_ge(kf_copied, 2 * HC)
                dve.wait_ge(z_ready, HC)
                for f in range(HC):
                    zr, zs = ps[:, 2 * (f % 2), :], ps[:, 2 * (f % 2) + 1, :]
                    kr, ks = KF[:, 0, f, :], KF[:, 1, f, :]
                    dve.wait_ge(zf_out, f + 1)
                    if f:
                        dve.wait_ge(yf_ready, f)
                    st.did(nc.vector.tensor_tensor(VT[:, 0, :], zr, kr, ALU.mult))
                    st.did(nc.vector.tensor_tensor(VT[:, 1, :], zs, ks, ALU.mult))
                    st.did(nc.vector.tensor_tensor(VT[:, 2, :], zr, ks, ALU.mult))
                    nc.vector.tensor_tensor(VT[:, 3, :], zs, kr, ALU.mult).then_inc(zf_used, 1)
                    dve.wait_ge(zf_used, f + 1)
                    nc.vector.tensor_tensor(YF[:, 0, f, :], VT[:, 0, :], VT[:, 1, :], ALU.subtract)
                    nc.vector.tensor_tensor(YF[:, 1, f, :], VT[:, 2, :], VT[:, 3, :], ALU.add).then_inc(yf_ready, 1)
                dve.wait_ge(yf_ready, HC)
                for c in range(HC):
                    dve.wait_ge(y_out, c + 1)
                    st.did(nc.vector.scalar_tensor_tensor(VT[:, c, :], ZT[:, c, :], COL[:, L_SKIP + c:L_SKIP + c + 1],
                                                          ps[:, 4 + c, :], ALU.mult, ALU.add))
                    st.then(dve)
                    nc.vector.tensor_tensor(YH[:, c, :], VT[:, c, :], X0[:, c, :], ALU.mult).then_inc(y_used, 1)
                arrive(dve)

                all_at(dve, 2)
                for n in range(KC):
                    dve.wait_ge(sg_ready, n + 1)
                    if n >= 2:
                        dve.wait_ge(mrg_ready, n - 1)
                    st.did(nc.vector.tensor_tensor(MP[:, n % 2, 0, :], ps[:, 4 * (n % 2), :], SG[:, n % 2, 0, :], ALU.mult))
                    nc.vector.tensor_tensor(MP[:, n % 2, 1, :], ps[:, 4 * (n % 2) + 2, :], SG[:, n % 2, 1, :],
                                            ALU.mult).then_inc(br_used, 1)
                    dve.wait_ge(br_used, n + 1)
                    nc.vector.tensor_tensor(MRG[:, n, :], MP[:, n % 2, 0, :], MP[:, n % 2, 1, :],
                                            ALU.add).then_inc(mrg_ready, 1)
                for n in range(2 * NB):
                    half, b = divmod(n, NB)
                    dve.wait_ge(wo_out, n + 1)
                    xb = X[:, b, 512 * half:512 * half + 512]
                    nc.vector.tensor_tensor(xb, ps[:, n % 4, :], xb, ALU.add).then_inc(wo_added, 1)
                arrive(dve)

                all_at(dve, 3)
                norm(st, NB, XS2, XN2, L_GFFN)
                dve.wait_ge(params, P_D)
                nc.vector.tensor_tensor(XG[:], XS2[:, (NB - 1) % 2, :], GF[:], ALU.mult)
                for n in range(2 * DB):
                    b, half = divmod(n, 2)
                    part = (slice(None), slice(4 * half, 4 * half + 4), slice(b * P, (b + 1) * P))
                    dve.wait_ge(xhi_ready, n + 1)
                    dve.wait_ge(xnt_ready, 2 * NB + n + 1)
                    nc.vector.tensor_tensor(XLO[part], XN2[part], XHI[part].bitcast(F32), ALU.subtract)
                NV, NS = NB * QG, NB * HG

                def finish_group(i):
                    dve.wait_ge(bexp_ready, i + 1)
                    be = BE[:, i % 2]
                    st.did(nc.vector.tensor_reduce(GSUM, be, axis=AX, op=ALU.add))
                    st.then(dve)
                    st.did(nc.vector.reciprocal(GSUM, GSUM))
                    st.then(dve)
                    st.did(nc.vector.tensor_tensor(be, be, GSUM.unsqueeze(2).to_broadcast([P, NS, TOPK]), ALU.mult))
                    st.then(dve)
                    place = [SEL[:, k, :, HG * i:HG * i + HG, :].rearrange("p b h m -> p b (h m)") for k in range(3)]
                    flat = "p (b h) m -> p b (h m)"
                    st.did(nc.vector.tensor_copy(place[0], SELG[:, 0].rearrange(flat, b=NB)))
                    st.did(nc.vector.tensor_copy(place[1], SELG[:, 1].rearrange(flat, b=NB)))
                    nc.vector.tensor_copy(place[2], be.rearrange(flat, b=NB)).then_inc(sel_ready, 1)

                for i in range(NGRP):
                    scores = [PS[:, i % 2, b, m, :] for b in range(NB) for m in range(QG)]
                    for n in range(NV):
                        if n % QG == 0:
                            dve.wait_ge(ps_copied, NB * i + n // QG + 1)
                        st.did(nc.vector.max(TV[:, n, 0:8], scores[n]))
                    st.then(dve)
                    for n in range(NV):
                        st.did(nc.vector.max_index(TI[:, n, 0:8], TV[:, n, 0:8], scores[n]))
                    st.then(dve)
                    for n in range(NV):
                        st.did(nc.vector.match_replace(scores[n], TV[:, n, 0:8], scores[n], NEG))
                    st.then(dve)
                    for n in range(NV):
                        st.did(nc.vector.max(TV[:, n, 8:16], scores[n]))
                    st.then(dve)
                    for n in range(NV):
                        last = nc.vector.max_index(TI[:, n, 8:16], TV[:, n, 8:16], scores[n])
                        if n < NV - 1:
                            st.did(last)
                    last.then_inc(ps_free, 1)
                    dve.wait_ge(ps_free, i + 1)
                    tv = TV[:].rearrange("p (h s) k -> p h s k", s=2)
                    st.did(nc.vector.tensor_tensor(CD[:], tv[:, :, 0, :].unsqueeze(3).to_broadcast([P, NS, TOPK, TOPK]),
                                                   tv[:, :, 1, :].unsqueeze(2).to_broadcast([P, NS, TOPK, TOPK]), ALU.add))
                    st.did(nc.vector.tensor_copy(TIF[:], TI[:]))
                    st.then(dve)
                    cd = [CD[:, h].rearrange("p a b -> p (a b)") for h in range(NS)]
                    for h in range(NS):
                        st.did(nc.vector.max(BV[:, h, 0:8], cd[h]))
                    st.then(dve)
                    for h in range(NS):
                        st.did(nc.vector.max_index(BP[:, h, 0:8], BV[:, h, 0:8], cd[h]))
                    st.then(dve)
                    for h in range(NS):
                        st.did(nc.vector.match_replace(cd[h], BV[:, h, 0:8], cd[h], NEG))
                    st.then(dve)
                    for h in range(NS):
                        st.did(nc.vector.max(BV[:, h, 8:16], cd[h]))
                    st.then(dve)
                    for h in range(NS):
                        st.did(nc.vector.max_index(BP[:, h, 8:16], BV[:, h, 8:16], cd[h]))
                    st.then(dve)
                    nc.vector.tensor_tensor(BE[:, i % 2], BV[:], BV[:, :, 0:1].to_broadcast([P, NS, TOPK]),
                                            ALU.subtract).then_inc(bmax_ready, 1)
                    bp = BP[:].rearrange("p h m -> p (h m)")
                    st.did(nc.vector.tensor_scalar(BA[:, 0, :], bp, 4, None, ALU.logical_shift_right))
                    st.did(nc.vector.tensor_scalar(BA[:, 1, :], bp, TOPK - 1, None, ALU.bitwise_and))
                    st.then(dve)
                    st.did(nc.vector.tensor_copy(BAF[:], BA[:]))
                    st.then(dve)
                    tif = TIF[:].rearrange("p (h s) k -> p h s k", s=2)
                    for k in range(2):
                        st.did(nc.vector.tensor_tensor(
                            EQ[:], BAF[:, k, :].unsqueeze(2).to_broadcast([P, NS * TOPK, TOPK]),
                            CST[:, C_IOTA16:C_IOTA16 + TOPK].unsqueeze(1).to_broadcast([P, NS * TOPK, TOPK]), ALU.is_equal))
                        st.then(dve)
                        eq = EQ[:].rearrange("p (h m) a -> p h m a", m=TOPK)
                        st.did(nc.vector.tensor_tensor(
                            eq, eq, tif[:, :, k, :].unsqueeze(2).to_broadcast([P, NS, TOPK, TOPK]), ALU.mult))
                        st.then(dve)
                        st.did(nc.vector.tensor_reduce(SELG[:, k].rearrange("p h m -> p (h m)"), EQ[:], axis=AX, op=ALU.add))
                        st.then(dve)
                    finish_group(i)
                dve.wait_ge(sel_ready, NGRP)
                picks = [SEL[:, k, NB - 1].rearrange("p h m -> p (h m)") for k in range(3)]
                nc.vector.tensor_copy(GG[:], picks[2])
                st.did(nc.vector.scalar_tensor_tensor(GIF[:], picks[0], float(NK), picks[1], ALU.mult, ALU.add))
                st.then(dve)
                st.did(nc.vector.tensor_scalar(GIF[:], GIF[:], COL[:, L_BASE:L_BASE + 1], None, ALU.add))
                st.then(dve)
                nc.vector.tensor_copy(GI[:], GIF[:])
                arrive(dve)

                all_at(dve, 4)
                with dve.Fori(0, DT // TOK_IT) as it:
                    for q in range(TOK_IT // OH):
                        picks = IDXT[:, 0:2, bass.ds(it * TOK_IT + q * OH, OH)]
                        dve.wait_ge(g_out, it * 32 + OH // 4 * (q + 1))
                        nc.vector.tensor_tensor(OHS[:, q % OHR], picks.unsqueeze(3).to_broadcast([P, 2, OH, NK]),
                                                CST[:, C_IOTA:C_IOTA + NK].unsqueeze(1).unsqueeze(1).to_broadcast([P, 2, OH, NK]),
                                                ALU.is_equal).then_inc(oh_made, 1)
                arrive(dve)

                all_at(dve, 5)
                dve.nop().then_inc(out_free, 4)

                def split_u(j, jj):
                    dve.wait_ge(u_hi, j + 1)
                    nc.vector.tensor_tensor(ULO[:, jj].rearrange("p k i -> p (k i)"), URAW[:, jj // 2, jj % 2, :],
                                            UHI[:, jj].rearrange("p k i -> p (k i)").bitcast(F32),
                                            ALU.subtract).then_inc(u_split, 1)

                def split_v(g, dh, pair):
                    for jj in (2 * pair, 2 * pair + 1):
                        dve.wait_ge(v_hi, g * 8 + 4 * dh + jj + 1)
                        nc.vector.tensor_tensor(VLO[:, dh, jj, :], VRAW[:, dh, jj, :], VHI[:, dh, jj, :].bitcast(F32),
                                                ALU.subtract).then_inc(v_split, 1)

                def weigh(j, jj, par, use):
                    blocks = "p (b c) -> p b c"
                    dve.wait_ge(act_ready, j + 1)
                    dve.wait_ge(g_loaded[par], use)
                    nc.vector.tensor_tensor(WF[:, jj % 2, :].rearrange(blocks, c=CB),
                                            AC[:, jj % 2, :].rearrange(blocks, c=CB), GT[:, par, :, jj, :],
                                            ALU.mult).then_inc(wf_ready, 1)
                    dve.wait_ge(wf_ready, j + 1)
                    nc.vector.tensor_copy(WHI[:, par, jj, :], WF[:, jj % 2, :]).then_inc(whi_ready, 1)
                    dve.wait_ge(whi_ready, j + 1)
                    nc.vector.tensor_tensor(WLO[:, par, jj, :], WF[:, jj % 2, :], WHI[:, par, jj, :].bitcast(F32),
                                            ALU.subtract).then_inc(w_ready, 1)

                def dot(s, par, k):
                    dve.wait_ge(rows_loaded[k % GR], l * ROWS_LAYER + s * (16 * GS // GR) + 16 * (k // GR + 1))
                    nc.vector.tensor_tensor_reduce(ROWS[:, k % GR, :], ROWS[:, k % GR, :], XG[:], 1.0, 0.0, ALU.mult, ALU.add,
                                                   accum_out=STG[:, par, k:k + 1]).then_inc(rows_used, 1)

                def keep_dots(s, par):
                    dve.wait_ge(rows_used, s * GS + (GR + GS))
                    nc.vector.tensor_copy(DOT[:, bass.ds(s * GS, GS)], STG[:, par, :]).then_inc(dots_done, 1)

                def stage_weights(s, par):
                    nc.vector.tensor_copy(STG[:, par, :], GW[:, bass.ds((s - GSTEPS) * GS, GS)]).then_inc(stg_ready, 1)

                def add_row(s, par, k):
                    dve.wait_ge(rows_loaded[k % GR], l * ROWS_LAYER + s * (16 * GS // GR) + 16 * (k // GR + 1))
                    if k == 0:
                        dve.wait_ge(stg_ready, s - (GSTEPS - 1))
                    dve.wait_ge(rows_used, s * GS + (GR + k))
                    nc.vector.scalar_tensor_tensor(X[:, NB - 1, :], ROWS[:, k % GR, :], STG[:, par, k:k + 1],
                                                   X[:, NB - 1, :], ALU.mult, ALU.add).then_inc(rows_used, 1)

                def add_output(g, par, o):
                    dh, b = divmod(o, DB)
                    xb = X[:, b, 512 * dh:512 * dh + 512]
                    dve.wait_ge(v_out, g * NOUT + o + 2)
                    nc.vector.tensor_tensor(xb, ps[:, 4 + (par * NOUT + o) % 4, :], xb, ALU.add).then_inc(out_free, 1)

                def step(g, par, use, columns=True, first=False, ahead=JG, rows=None):
                    if rows is add_row:
                        stage_weights(g, 1 - par)
                    for jj in range(JG):
                        if columns and jj < ahead:
                            split_u(g * 4 + 6 + jj, (2 + jj) % 4)
                        if jj < 2 and not first:
                            split_v(g, 1, jj)
                        if jj >= 2 and columns:
                            split_v(g + 1, 0, jj - 2)
                        if columns:
                            weigh(g * 4 + 4 + jj, jj, par, use)
                        if rows:
                            rows(g, 1 - par, 2 * jj)
                        if not first:
                            for o in SLOTS[jj]:
                                add_output(g, 1 - par, o)
                        if rows:
                            rows(g, 1 - par, 2 * jj + 1)
                    if rows is dot:
                        keep_dots(g, 1 - par)

                split_u(0, 0)
                split_u(1, 1)
                step(-1, 0, 16, first=True)
                dve.nop().then_inc(rows_used, GR)
                with dve.Fori(0, GSTEPS // 2) as it:
                    step(it * 2, 1, it * 16 + 16, rows=dot)
                    step(it * 2 + 1, 0, it * 16 + 32, rows=dot)
                dve.wait_ge(gelu_done, 1)
                nc.vector.tensor_tensor(GW[:], DOT[:], GG[:], ALU.mult).then_inc(gw_ready, 1)
                dve.wait_ge(gw_ready, 1)
                with dve.Fori(GSTEPS // 2, (NG - 2) // 2) as it:
                    step(it * 2, 1, it * 16 + 16, rows=add_row)
                    step(it * 2 + 1, 0, it * 16 + 32, rows=add_row)
                step(NG - 2, 1, 8 * NG, ahead=2, rows=add_row)
                step(NG - 1, 0, 0, columns=False, rows=add_row)
                end_layer(dve, l)

            dve.wait_ge(pre_sin, 1 + NB)
            pre.did(nc.vector.tensor_scalar(SV, SS, 1.0 / DM, EPS, ALU.mult, ALU.add))
            assert pre.n == FINAL_VAR
            dve.wait_ge(pre_sin, 2 + NB)
            inverse_root(pre, NB)
            dve.wait_ge(first_loads, 32)
            for b in range(NB):
                pre.did(nc.vector.tensor_scalar(OUTB[:, b, :], X[:, b, :], SR[:, b:b + 1], None, ALU.mult))
            pre.then(dve)
            assert pre.n == FINAL0
            for b in range(NB):
                pre.did(nc.vector.tensor_tensor(OUTB[:, b, :], OUTB[:, b, :], GFIN[:], ALU.mult))


def shape_tables():
    f4 = np.float32
    const = np.zeros((P, NCONST), f4)
    const[:, C_ID:C_ID + P] = np.eye(P)
    const[:, C_IOTA:C_IOTA + NK] = np.arange(NK)
    q, k = np.arange(P)[:, None], np.arange(3 * P)[None, :] - P
    const[:, C_MASK:C_MASK + 3 * P] = np.where(np.abs(q - k) <= P, 0.0, -1e30)
    const[:, C_IOTA16:C_IOTA16 + TOPK] = np.arange(TOPK)
    const[:, C_FREQ:C_FREQ + ROT] = f4(500000.0) ** (-np.arange(0, 2 * ROT, 2, dtype=f4) / f4(2 * ROT))
    t = np.linspace(0.0, 1.0, SEQ, dtype=f4)[:, None]
    bands = (EMB - 1) // 2
    w = f4(2.0 * math.pi) * np.arange(SEQ, dtype=f4)[:, None] / f4(SEQ)
    f = np.linspace(1e-4, bands - 1, bands, dtype=f4)[None, :]
    fw = (f * w).astype(f4)
    zemb = np.concatenate([t, np.cos(fw), -np.sin(fw)], axis=1).astype(f4).T
    lo, hi = math.log(1e-2) / 1.5, math.log(1e-2) / 0.3
    deltas = np.abs(np.linspace(lo, hi, HW, dtype=f4))[None, :]
    decay = np.exp(-t * deltas).astype(f4).reshape(NB, P, HW).transpose(1, 0, 2)
    ang = (2 * math.pi / (2 * SEQ)) * np.outer(np.arange(SEQ), np.arange(SEQ) + 0.5)
    both = np.stack([np.cos(ang), np.sin(ang)], axis=1)
    fwd = both.reshape(NB, P, 2, SEQ).transpose(1, 0, 2, 3).reshape(P, -1)
    inv = (both / SEQ).transpose(2, 1, 0).reshape(NB, P, 2, SEQ).transpose(1, 0, 2, 3).reshape(P, -1)
    return [np.ascontiguousarray(a, dtype=f4) for a in (const, zemb, decay, fwd, inv)]


def kernel(x, positions, norm_mix, w_in, conv_w, conv_b, filt_w1, filt_b1, filt_freq1, filt_w2, filt_b2, filt_freq2,
           filt_w3, filt_b3, hyena_skip, attn_sink, w_attn_branch, w_hyena_branch, w_out, norm_ffn, w_query, sub_keys,
           expert_u, expert_v, norm_final):
    import concourse.bacc as bacc
    from concourse.bass_utils import run_bass_kernel_spmd

    def chunks(a, n):
        return np.asarray(a).reshape(DEPTH, n, P).transpose(0, 2, 1)

    const, zemb, decay, fwd, inv = shape_tables()
    conv = np.asarray(conv_w).reshape(DEPTH, 3, NHY, P).transpose(0, 3, 2, 1).reshape(DEPTH, P, 3 * NHY)
    cols = np.concatenate([chunks(norm_mix, KC), chunks(norm_ffn, KC), conv, chunks(conv_b, NHY), chunks(hyena_skip, HC),
                           np.broadcast_to((np.arange(DEPTH, dtype=np.float32) * NK * NK)[:, None, None], (DEPTH, P, 1))], axis=2)
    fcols = np.stack([np.asarray(a) for a in (filt_b1, filt_freq1, filt_b2, filt_freq2)], axis=2)
    w3 = np.concatenate([np.asarray(filt_w3), np.asarray(filt_b3)[:, None, :]], axis=1)
    ut = (np.asarray(expert_u).reshape(DEPTH, NK, NK // 2, 2, KC, P).transpose(0, 2, 5, 3, 4, 1)
          .reshape(DEPTH, NK // 2, P, 2, KC * P))
    v = np.asarray(expert_v).reshape(DEPTH, NK, NG, JG, 2, DM // 2).transpose(0, 2, 4, 1, 3, 5)
    given = {
        "x": np.asarray(x).reshape(SEQ, DM), "positions": np.asarray(positions).reshape(SEQ), "consts": const,
        "gfinal": np.asarray(norm_final), "gffn": np.asarray(norm_ffn), "cols": cols, "fcols": fcols, "sink": np.asarray(attn_sink),
        "w1": np.asarray(filt_w1), "w2": np.asarray(filt_w2), "w3": w3, "zemb": zemb, "decay": decay,
        "fwd": fwd, "inv": inv, "w_in": np.asarray(w_in), "w_ab": np.asarray(w_attn_branch),
        "w_hb": np.asarray(w_hyena_branch), "w_out": np.asarray(w_out), "w_q": np.asarray(w_query),
        "keys": np.asarray(sub_keys).transpose(0, 3, 1, 2), "ut": ut, "v": v,
        "u_rows": np.asarray(expert_u).reshape(DEPTH * NK * NK, DM),
        "v_rows": np.asarray(expert_v).reshape(DEPTH * NK * NK, DM),
    }
    nc = bacc.Bacc("TRN2", target_bir_lowering=False, num_devices=1)
    arrays, args = {}, []
    for name, a in given.items():
        a = np.ascontiguousarray(a)
        arrays[f"{name}_dram"] = a
        args.append(nc.dram_tensor(f"{name}_dram", a.shape, mybir.dt.from_np(a.dtype), kind="ExternalInput").ap())
    args.append(nc.dram_tensor("out_dram", (SEQ, DM), F32, kind="ExternalOutput").ap())
    encoder(nc, *args)
    got = run_bass_kernel_spmd(nc, [arrays], core_ids=[0]).results[0]["out_dram"]
    return got.reshape(1, SEQ, DM)
```

```python
import math
from contextlib import ExitStack

import numpy as np
import concourse.bass as bass
from concourse import mybir

F32 = mybir.dt.float32
F32R = mybir.dt.float32r
I32 = mybir.dt.int32
U32 = mybir.dt.uint32
ACT = mybir.ActivationFunctionType
ALU = mybir.AluOpType
AX = mybir.AxisListType.X

P = 128
DEPTH, SEQ, DM = 2, 512, 1024
NB = SEQ // P
KC = DM // P
QH, KVH, HD = 8, 2, 64
GROUP = QH // KVH
ROT = HD // 8
AW, KVW = QH * HD, KVH * HD
HW = 512
HC = HW // P
NHY = 3 * HC
EMB, HID = 33, 64
HY0 = AW + 2 * KVW
GA0 = HY0 + 3 * HW
GH0 = GA0 + DM
NK, PH, TOPK = 128, 8, 16
HP = 2 * PH
QG = 4
HG = QG // 2
NGRP = HP // QG
FULL, NARROW = 4, 4
CFULL = FULL * TOPK
CAND = CFULL + (TOPK - FULL) * NARROW
assert (FULL + 1) * (NARROW + 1) > TOPK and NARROW == 4 and TOPK == 16
EPS = 1e-6
NEG = -3.0e38
TWO_PI_HI = 6.28125
TWO_PI_MID = float(np.float32(0.0019350051879882812))
TWO_PI_LO = float(np.float32(2 * math.pi - TWO_PI_HI - TWO_PI_MID))
PI_IN = 3.1415925
ROUND = 1.5 * 2 ** 23

C_ID, C_IOTA, C_MASK, C_IOTA16, C_FREQ = 0, 128, 256, 640, 656
NCONST = C_FREQ + ROT
L_GMIX, L_GFFN, L_CONVW, L_CONVB, L_SKIP = 0, 8, 16, 16 + 3 * NHY, 16 + 4 * NHY
NCOL = L_SKIP + HC + 1
L_BASE = NCOL - 1

T_Q, T_KV, T_HY, T_FWD, T_INV, T_BR, T_OUT, T_PQ = 0, 1, 2, 5, 6, 7, 15, 17
NTILES = T_PQ + 4
RING = 3

HY_ROPE, HY_A = 2, 9
TOK_IT = 128
CB = 64
OH, OHR = 8, 4
OHN = TOK_IT // OH
JG = 4
NG = NK // JG
DB = 3
DT = DB * P
NOUT = 2 * DB
PICKS = PH * TOPK
GR, GS = 4, 8
GSTEPS = PICKS // GS
SLOTS = [range(i * NOUT // JG, (i + 1) * NOUT // JG) for i in range(JG)]


class Steps:

    def __init__(self, sem):
        self.sem, self.n = sem, 0

    def did(self, ins):
        ins.then_inc(self.sem, 1)
        self.n += 1
        return self.n

    def then(self, eng, n=None):
        eng.wait_ge(self.sem, self.n if n is None else n)


def tile_uses():
    parts = [1] * NTILES
    for n in range(KC):
        parts[T_BR + n] = 4
    got, out = [0] * RING, []
    for t in range(NTILES):
        got[t % RING] += 16 * parts[t]
        out.append((t % RING, got[t % RING]))
    return out


def hy_bank(n):
    return 2 + n if n < HY_ROPE else 6 if n < HY_A else n % 4


def encoder(nc, x, positions, consts, gfinal, gffn, cols, fcols, sink, w1, w2, w3, zemb, decay, fwd, inv,
            w_in, w_ab, w_hb, w_out, w_q, keys, ut, v,
            u_rows, v_rows, out):
    ctx = ExitStack()
    at = [16512]

    def sb(name, shape, dt=F32, offset=None):
        size = 4 * int(np.prod(shape[1:]))
        size = (size + 31) // 32 * 32
        if offset is None:
            offset = at[0]
            at[0] += size
        t = nc.alloc_sbuf_tensor_at(name, shape, dt, offset=offset)
        return t, offset

    def sem(name):
        return nc.alloc_semaphore(name)

    X, _ = sb("X", [P, NB, DM])
    CST, _ = sb("CST", [P, NCONST])
    COL, _ = sb("COL", [P, NCOL])
    FCOL, _ = sb("FCOL", [HID, 4])
    SINK, _ = sb("SINK", [P, QH])
    SINCOS, _ = sb("SINCOS", [P, 2, NB, ROT])
    SMALL, _ = sb("SMALL", [P, 64])
    WR, wr_at = sb("WR", [P, RING, 4096])
    phase_at = at[0]
    ident = CST[:, C_ID:C_ID + P]
    iota = CST[:, C_IOTA:C_IOTA + NK]

    XNT, xnt_at = sb("XNT", [P, KC, SEQ])
    MRG, mrg_at = sb("MRG", [P, KC, SEQ])
    ATT, att_at = sb("ATT", [P, 4, SEQ])
    YH, yh_at = sb("YH", [P, HC, SEQ])
    abc_at = at[0]
    KF, _ = sb("KF", [P, 2, HC, HW], offset=mrg_at)
    DEC, _ = sb("DEC", [P, NB, HW], offset=yh_at)
    XS, xs_at = sb("XS", [P, 2, DM])
    QKV, _ = sb("QKV", [P, NB, HY0])
    KREP, _ = sb("KREP", [P, NB, KVH, 2, HD])
    QT, _ = sb("QT", [P, 4, SEQ])
    KT, _ = sb("KT", [P, KVH, SEQ])
    SC, _ = sb("SC", [P, 2, GROUP, 3 * P])
    PT, _ = sb("PT", [P, 2, 3, GROUP * P])
    RT, _ = sb("RT", [P, 4, NB, QH + KVH, ROT])
    HYT, hyt_at = sb("HYT", [P, NHY, SEQ + 2])
    end_a = at[0]
    at[0] = abc_at
    X0, _ = sb("X0", [P, HC, SEQ])
    ZT, _ = sb("ZT", [P, HC, SEQ])
    VT, _ = sb("VT", [P, HC, SEQ])
    ZTOK, _ = sb("ZTOK", [P, NB, HW])
    HS, hs_at = sb("HS", [P, 2, NB, HW])
    YF, _ = sb("YF", [P, 2, HC, HW], offset=hs_at)
    FA, _ = sb("FA", [HID, SEQ])
    FK, _ = sb("FK", [HID, SEQ])
    FR, _ = sb("FR", [HID + 1, SEQ])
    W1, _ = sb("W1", [EMB, HID])
    W2, _ = sb("W2", [HID, HID])
    W3, w3_at = sb("W3", [HID + 1, 2 * HW])
    ZE, _ = sb("ZE", [EMB, SEQ])
    end_b = at[0]
    assert end_b <= hyt_at
    at[0] = abc_at
    SG, _ = sb("SG", [P, 2, 2, SEQ])
    MP, _ = sb("MP", [P, 2, 2, SEQ])
    XL, _ = sb("XL", [P, KC, SEQ], F32R, offset=xnt_at)
    ATTL, _ = sb("ATTL", [P, 4, SEQ], F32R, offset=att_at)
    YHL, _ = sb("YHL", [P, HC, SEQ], F32R, offset=yh_at)
    MRGL, _ = sb("MRGL", [P, KC, SEQ], F32R, offset=mrg_at)
    WRL, _ = sb("WRL", [P, RING, 4096], F32R, offset=wr_at)
    XH, xh_at = sb("XH", [P, KC, SEQ], F32R)
    ATTH, _ = sb("ATTH", [P, 4, SEQ], F32R)
    YHH, _ = sb("YHH", [P, HC, SEQ], F32R)
    MRGH, _ = sb("MRGH", [P, KC, SEQ], F32R)
    woh_at = at[0]
    at[0] += 4096
    WCH, _ = sb("WCH", [P, 2, 3, 8 * P], F32R)
    end_c = at[0]
    WOH = [sb(f"WOH{i}", [P, 4, 2 * 512], F32R, offset=o)[0] for i, o in enumerate((woh_at, xh_at))]
    at[0] = phase_at
    XHI, _ = sb("XHI", [P, KC, DT], F32R)
    XLO, _ = sb("XLO", [P, KC, DT], F32R)
    XG, _ = sb("XG", [P, DM])
    GI, _ = sb("GI", [P, PICKS], I32)
    GG, _ = sb("GG", [P, PICKS])
    IDXT, idxt_at = sb("IDXT", [P, 3, DT])
    def_at = at[0]
    XN2, _ = sb("XN2", [P, KC, SEQ])
    XS2, _ = sb("XS2", [P, 2, DM])
    KEY, _ = sb("KEY", [P, 2, NK])
    GF, _ = sb("GF", [P, DM])
    GIF, _ = sb("GIF", [P, PICKS])
    PQT, _ = sb("PQT", [P, 2, QG, SEQ])
    PS, _ = sb("PS", [P, 2, QG, NB, NK])
    CD, _ = sb("CD", [P, NB * HG, CAND])
    EQ, _ = sb("EQ", [P, 2, NB * HG * TOPK, TOPK])
    TV, _ = sb("TV", [P, NB * QG, TOPK])
    TI, _ = sb("TI", [P, NB * QG, TOPK], U32)
    TIF, _ = sb("TIF", [P, 2, NB * QG, TOPK])
    BV, _ = sb("BV", [P, NB * HG, TOPK])
    BP, _ = sb("BP", [P, NB * HG, TOPK], U32)
    BA, _ = sb("BA", [P, 4, NB * HG * TOPK], U32)
    BAF, _ = sb("BAF", [P, 4, NB * HG * TOPK])
    NARW, _ = sb("NARW", [P, NB * HG * TOPK])
    BE, _ = sb("BE", [P, 2, NB * HG, TOPK])
    SEL, _ = sb("SEL", [P, 3, NB, PH, TOPK])
    end_d = at[0]
    at[0] = def_at
    OHS, _ = sb("OHS", [P, OHR, 2, OH, NK])
    GST, _ = sb("GST", [P, 2, NK, CB])
    end_e = at[0]
    URAW, _ = sb("URAW", [P, 2, 2, DM], offset=wr_at)
    VRAW, _ = sb("VRAW", [P, 2, JG, 512], offset=wr_at + 16384)
    GT, _ = sb("GT", [P, 2, DT // CB, JG, CB], offset=wr_at + 32768)
    at[0] = idxt_at
    UHI, _ = sb("UHI", [P, JG, KC, P], F32R)
    ULO, _ = sb("ULO", [P, JG, KC, P], F32R)
    VHI, _ = sb("VHI", [P, 2, JG, 512], F32R)
    VLO, _ = sb("VLO", [P, 2, JG, 512], F32R)
    WHI, _ = sb("WHI", [P, 2, JG, DT], F32R)
    WLO, _ = sb("WLO", [P, 2, JG, DT], F32R)
    AC, _ = sb("AC", [P, 2, DT])
    WF, _ = sb("WF", [P, 2, DT])
    ROWS, _ = sb("ROWS", [P, GR, DM])
    GIS, _ = sb("GIS", [P, 2, GS], I32)
    DOT, _ = sb("DOT", [P, PICKS])
    GW, _ = sb("GW", [P, PICKS])
    STG, _ = sb("STG", [P, 2, GS])
    end_f = at[0]
    OUTB, _ = sb("OUTB", [P, NB, DM], offset=phase_at)
    GFIN, _ = sb("GFIN", [P, DM], offset=phase_at + 16384)
    assert max(end_a, end_b, end_c, end_d, end_e, end_f) <= nc.sbuf_usable_end, (end_a, end_b, end_c, end_d, end_e, end_f)

    ps = nc.alloc_psum_tensor("ps", [P, 8, 512], F32)
    gd = nc.dram_tensor("g_table", (DT // CB, P, NK, CB), F32, kind="Internal").ap()

    SS, SV, SR, ST = SMALL[:, 0:4], SMALL[:, 4:8], SMALL[:, 8:12], SMALL[:, 12:16]
    MX, DSK, DEN, POSF = SMALL[:, 16:24], SMALL[:, 24:32], SMALL[:, 32:40], SMALL[:, 40:44]
    GMX, GSUM = SMALL[:, 44:52], SMALL[:, 52:60]

    first_loads, x_loaded, pos_loaded = sem("first_loads"), sem("x_loaded"), sem("pos_loaded")
    pre_steps, out_stored, next_layer = sem("pre_steps"), sem("out_stored"), sem("next_layer")
    pre_sin = sem("pre_sin")
    went_on = sem("went_on")
    layer_sems = []

    def lsem(name):
        layer_sems.append(sem(name))
        return layer_sems[-1]

    engines_done = lsem("engines_done")
    phase = lsem("phase")
    late_sems = layer_sems[:]
    params = lsem("params")
    w_loaded = [lsem(f"w_loaded{i}") for i in range(RING)]
    act_steps, dve_steps = lsem("act_steps"), lsem("dve_steps")
    sumsq, var_ready, root_ready = lsem("sumsq"), lsem("var_ready"), lsem("root_ready")
    xs_ready, xs_turned, xnt_ready = lsem("xs_ready"), lsem("xs_turned"), lsem("xnt_ready")
    qkv_out, qkv_copied, roped = lsem("qkv_out"), lsem("qkv_copied"), lsem("roped")
    qk_turned, qk_copied = lsem("qk_turned"), lsem("qk_copied")
    sc_out, sc_copied, mx_ready, exp_done = lsem("sc_out"), lsem("sc_copied"), lsem("mx_ready"), lsem("exp_done")
    probs_ready, probs_turned, pt_copied = lsem("probs_ready"), lsem("probs_turned"), lsem("pt_copied")
    o_out, o_copied = lsem("o_out"), lsem("o_copied")
    pads_zero, hy_out, hy_copied = lsem("pads_zero"), lsem("hy_out"), lsem("hy_copied")
    f_out, f_arg, f_sin = lsem("f_out"), lsem("f_arg"), lsem("f_sin")
    h3_out, h3_copied, hs_ready, dec_loaded = lsem("h3_out"), lsem("h3_copied"), lsem("hs_ready"), lsem("dec_loaded")
    kf_out, kf_copied = lsem("kf_out"), lsem("kf_copied")
    z_ready, z_turned, ztok_ready = lsem("z_ready"), lsem("z_turned"), lsem("ztok_ready")
    zf_out, zf_used, yf_ready = lsem("zf_out"), lsem("zf_used"), lsem("yf_ready")
    y_out, y_used = lsem("y_out"), lsem("y_used")
    br_out, sg_ready, br_used, mrg_ready = lsem("br_out"), lsem("sg_ready"), lsem("br_used"), lsem("mrg_ready")
    in_hi, in_split, wb_hi, wb_split = lsem("in_hi"), lsem("in_split"), lsem("wb_hi"), lsem("wb_split")
    mrg_hi, mrg_split, wo_hi, wo_split = lsem("mrg_hi"), lsem("mrg_split"), lsem("wo_hi"), lsem("wo_split")
    wo_out, wo_added = lsem("wo_out"), lsem("wo_added")
    xhi_ready = lsem("xhi_ready")
    pq_out, pq_copied, ps_out, ps_copied, ps_free = lsem("pq_out"), lsem("pq_copied"), lsem("ps_out"), lsem("ps_copied"), lsem("ps_free")
    bmax_ready, bexp_ready = lsem("bmax_ready"), lsem("bexp_ready")
    rows_apart, rows_abs, rows_ready = lsem("rows_apart"), lsem("rows_abs"), lsem("rows_ready")
    places_ready, keys_found = lsem("places_ready"), lsem("keys_found")
    pool_steps = lsem("pool_steps")
    sel_ready, sel_turned, idx_copied = lsem("sel_ready"), lsem("sel_turned"), lsem("idx_copied")
    oh_made = lsem("oh_made")
    oh_ready, g_out, g_bank_free = lsem("oh_ready"), lsem("g_out"), lsem("g_bank_free")
    gst_free = lsem("gst_free")
    g_stored = [lsem(f"g_stored{i}") for i in range(2)]
    before_late = len(layer_sems) - 2
    u_loaded = [lsem(f"u_loaded{i}") for i in range(2)]
    v_loaded = [lsem(f"v_loaded{i}") for i in range(2)]
    g_loaded = [lsem(f"g_loaded{i}") for i in range(2)]
    u_hi, u_split, u_done = lsem("u_hi"), lsem("u_split"), lsem("u_done")
    v_hi, v_split = lsem("v_hi"), lsem("v_split")
    stg_ready, dots_done, gelu_done, gw_ready = lsem("stg_ready"), lsem("dots_done"), lsem("gelu_done"), lsem("gw_ready")
    rows_used, gis_ready, pool_went = lsem("rows_used"), lsem("gis_ready"), lsem("pool_went")
    rows_loaded = [sem(f"rows_loaded{i}") for i in range(GR)]
    ROWS_LAYER = 16 * 2 * PICKS // GR
    act_ready, wf_ready, whi_ready, w_ready = lsem("act_ready"), lsem("wf_ready"), lsem("whi_ready"), lsem("w_ready")
    v_out, out_free = lsem("v_out"), lsem("out_free")

    sp_at_f = lsem("sp_at_f")
    late_sems += layer_sems[before_late:]
    early_sems = [s for s in layer_sems if s not in late_sems]

    TILE = tile_uses()

    tile_done = ([(qkv_out, 2 * NB)] * 2 + [(hy_out, 4 * i + 4) for i in range(3)] + [(zf_out, HC), (y_out, HC)]
                 + [(br_out, n + 1) for n in range(KC)] + [(wo_out, NB * i + NB) for i in range(2)]
                 + [(pq_out, 4 * i + 4) for i in range(4)])
    assert len(tile_done) == NTILES

    def need_tile(e, t):
        e.wait_ge(w_loaded[TILE[t][0]], TILE[t][1])

    def arrive(e):
        e.drain().then_inc(phase, 1)

    def all_at(e, n):
        e.wait_ge(phase, 3 * n)

    def g_all_stored(e):
        for s in range(2):
            e.wait_ge(g_stored[s], 16 * (DT // TOK_IT))

    def end_layer(e, l):
        e.drain().then_inc(engines_done, 1)
        e.wait_ge(next_layer, l + 1)
        e.nop().then_inc(went_on, 1)

    SINCOS_ARGS, FINAL_VAR, FINAL0 = 15, 16, 25

    def places_and_columns(k):
        n = NB * HG * TOPK
        return (BAF[:, k, :].unsqueeze(2).to_broadcast([P, n, TOPK]),
                CST[:, C_IOTA16:C_IOTA16 + TOPK].unsqueeze(1).to_broadcast([P, n, TOPK]))

    def times_keys(e, i, k):
        eq = EQ[:, k].rearrange("p (h m) a -> p h m a", m=TOPK)
        tif = TIF[:, i % 2].rearrange("p (h s) k -> p h s k", s=2)[:, :, k, :]
        return e.tensor_tensor(eq, eq, tif.unsqueeze(2).to_broadcast([P, NB * HG, TOPK, TOPK]), ALU.mult)

    C_IN = [(ATT[:], ATTH[:], ATTL[:]), (YH[:], YHH[:], YHL[:])] + [
        tuple(t[:, 4 * i:4 * i + 4] for t in (XNT, XH, XL)) for i in range(2)]

    def branch_weights(n, i):
        part = (slice(None), (T_BR + n) % RING, slice((16, 0, 8)[i] * P, ((16, 0, 8)[i] + 8) * P))
        return WR[part], WCH[:, n % 2, i, :], WRL[part]

    def out_weights(half, i):
        part = (slice(None), (T_OUT + half) % RING, slice(i * 1024, (i + 1) * 1024))
        return WR[part], WOH[half][:, i, :], WRL[part]

    def high(x, hi, lo):
        return nc.scalar.copy(hi, x)

    def low(x, hi, lo):
        return nc.vector.tensor_tensor(lo, x, hi.bitcast(F32), ALU.subtract)

    with nc.Block() as block:

        @block.sync
        def _(sp):
            sp.dma_start(X[:], x.rearrange("(b p) d -> p b d", p=P)).then_inc(x_loaded, 16)
            sp.dma_start(CST[:], consts).then_inc(first_loads, 16)
            with sp.Fori(0, DEPTH) as l:
                loaded = [0]

                def weights(parts):
                    t = loaded[0]
                    loaded[0] += 1
                    if t >= RING:
                        sp.wait_ge(*tile_done[t - RING])
                    for dst, src in parts:
                        sp.dma_start(dst(WR[:, t % RING, :]), src).then_inc(w_loaded[t % RING], 16)

                def cols_of(w, c0, n, kc=KC):
                    return w[l, :, c0:c0 + n].rearrange("(k p) n -> p k n", p=P)

                def at_cols(o, kc, n):
                    return lambda s: s[:, o:o + kc * n].rearrange("p (k n) -> p k n", n=n)

                sp.dma_start(COL[:], cols[l]).then_inc(params, 16)
                sp.dma_start(SINK[:], sink[l].partition_broadcast(P)).then_inc(params, 16)
                sp.dma_start(FCOL[:], fcols[l]).then_inc(params, 16)
                weights([(at_cols(0, KC, AW), cols_of(w_in, 0, AW))])
                weights([(at_cols(0, KC, 2 * KVW), cols_of(w_in, AW, 2 * KVW))])
                for i in range(3):
                    weights([(at_cols(0, KC, 512), cols_of(w_in, HY0 + 512 * i, 512))])
                all_at(sp, 1)
                sp.dma_start(W1[:], w1[l]).then_inc(params, 16)
                sp.dma_start(W2[:], w2[l]).then_inc(params, 16)
                sp.dma_start(W3[:], w3[l]).then_inc(params, 16)
                sp.dma_start(ZE[:], zemb).then_inc(params, 16)
                sp.dma_start(DEC[:], decay).then_inc(dec_loaded, 16)
                weights([(lambda s: s, fwd)])
                weights([(lambda s: s, inv)])
                for n in range(KC):
                    weights([(at_cols(0, KC, P), cols_of(w_in, GA0 + P * n, P)),
                             (at_cols(KC * P, KC, P), cols_of(w_in, GH0 + P * n, P)),
                             (at_cols(2 * KC * P, 4, P), cols_of(w_ab, P * n, P)),
                             (at_cols((2 * KC + 4) * P, 4, P), cols_of(w_hb, P * n, P))])
                for i in range(2):
                    weights([(at_cols(0, KC, 512), cols_of(w_out, 512 * i, 512))])
                for i in range(4):
                    if i == 3:
                        all_at(sp, 3)
                        sp.dma_start(KEY[:], keys[l]).then_inc(params, 16)
                        sp.dma_start(GF[:], gffn[l].partition_broadcast(P)).then_inc(params, 16)
                    weights([(at_cols(0, KC, 512), cols_of(w_q, 512 * i, 512))])
                def load_u(jp, slot):
                    sp.dma_start(URAW[:, slot], ut[l, jp]).then_inc(u_loaded[slot], 16)

                def load_v(g, dh):
                    sp.dma_start(VRAW[:, dh], v[l, g, dh]).then_inc(v_loaded[dh], 16)

                def load_g(g, slot):
                    src = gd[:, :, bass.ds(g * JG, JG), :].rearrange("b i j c -> i b (j c)")
                    sp.dma_start(GT[:, slot].rearrange("p b j c -> p b (j c)"), src).then_inc(g_loaded[slot], 16)

                all_at(sp, 4)
                load_u(0, 0)
                load_u(1, 1)
                load_v(0, 0)
                load_v(0, 1)
                sp.nop().then_inc(gst_free, 2)
                with sp.Fori(0, DT // TOK_IT) as it:
                    for s in range(2):
                        dst = gd[it * 2 + s].rearrange("i j c -> i (j c)")
                        sp.wait_ge(g_bank_free, it * 32 + 16 * (s + 1) + 8)
                        sp.dma_start(dst, GST[:, s].rearrange("p j c -> p (j c)")).then_inc(g_stored[s], 16)
                    for s in range(2):
                        sp.wait_ge(g_stored[s], it * 16 + 16)
                        sp.nop().then_inc(gst_free, 1)
                g_all_stored(sp)
                all_at(sp, 5)
                sp.nop().then_inc(sp_at_f, 1)

                def step(g, par, last=False):
                    sp.wait_ge(u_split, g * 4 + 4)
                    load_u(g * 2 + 3, 1)
                    sp.wait_ge(v_split, g * 8 + 4)
                    load_v(g + 1, 0)
                    if not last:
                        sp.wait_ge(w_ready, g * 4 + 4)
                        load_g(g + 2, par)
                        sp.wait_ge(u_split, g * 4 + 6)
                        load_u(g * 2 + 4, 0)
                    sp.wait_ge(v_split, g * 8 + 8)
                    load_v(g + 1, 1)

                load_g(0, 0)
                load_g(1, 1)
                sp.wait_ge(u_split, 2)
                load_u(2, 0)
                with sp.Fori(0, (NG - 2) // 2) as it:
                    step(it * 2, 0)
                    step(it * 2 + 1, 1)
                step(NG - 2, 0, last=True)
                end_layer(sp, l)
            sp.dma_start(GFIN[:], gfinal.partition_broadcast(P)).then_inc(first_loads, 16)
            for b in range(NB):
                sp.wait_ge(pre_steps, FINAL0 + b + 1)
                sp.dma_start(out[b * P:(b + 1) * P, :], OUTB[:, b, :]).then_inc(out_stored, 16)
            sp.wait_ge(out_stored, 16 * NB)

        @block.gpsimd
        def _(pool):
            with nc.allow_non_contiguous_dma("positions and sinks are a few words"):
                pool.dma_start(POSF[:].bitcast(I32), positions.rearrange("(b p) -> p b", p=P)).then_inc(pos_loaded, 16)
            with pool.Fori(0, DEPTH) as l:
                all_at(pool, 1)
                pool.memset(HYT[:, :, 0:1], 0.0).then_inc(pads_zero, 1)
                pool.memset(HYT[:, :, SEQ + 1:SEQ + 2], 0.0).then_inc(pads_zero, 1)
                pool.wait_ge(pads_zero, 2)
                pool.memset(FR[HID:HID + 1, :], 1.0).then_inc(pads_zero, 1)
                all_at(pool, 3)
                tree = 0
                for i in range(NGRP):
                    pool.wait_ge(places_ready, i + 1)
                    for k in (1, 0) if i < NGRP - 1 else ():
                        nc.gpsimd.tensor_tensor(EQ[:, k], *places_and_columns(k), ALU.subtract).then_inc(rows_apart, 1)
                    for k in (1, 0):
                        if (i, k) != (NGRP - 1, 0):
                            pool.wait_ge(rows_ready, 2 * i + 2 - k)
                            if i == NGRP - 1:
                                times_keys(nc.gpsimd, i, k).then_inc(keys_found, 1)
                                continue
                            times_keys(nc.gpsimd, i, k).then_inc(pool_steps, 1)
                            n = TOPK // 2
                            while n:
                                tree += 1
                                pool.wait_ge(pool_steps, tree)
                                nc.gpsimd.tensor_tensor(EQ[:, k, :, 0:n], EQ[:, k, :, 0:n], EQ[:, k, :, n:2 * n],
                                                        ALU.add).then_inc(pool_steps if n > 1 else keys_found, 1)
                                n //= 2
                all_at(pool, 4)
                with pool.Fori(0, DT // TOK_IT) as it:
                    for q in range(TOK_IT // OH):
                        gates = IDXT[:, 2, bass.ds(it * TOK_IT + q * OH, OH)]
                        pool.wait_ge(oh_made, it * OHN + q + 1)
                        nc.gpsimd.tensor_tensor(OHS[:, q % OHR, 1], OHS[:, q % OHR, 1],
                                                gates.unsqueeze(2).to_broadcast([P, OH, NK]), ALU.mult).then_inc(oh_ready, 1)
                all_at(pool, 5)
                g_all_stored(pool)

                def rows(table, it, par, before):
                    s = it * 2 + par
                    nc.gpsimd.tensor_copy(GIS[:, par, :], GI[:, bass.ds(s * GS, GS)]).then_inc(gis_ready, 1)
                    pool.wait_ge(gis_ready, s + (before + 1))
                    pool.nop().then_inc(pool_went, 1)
                    for k in range(GS):
                        pool.wait_ge(rows_used, s * GS + (before * GS + k + 1))
                        pool.nop().then_inc(pool_went, 1)
                        pool.indirect_dma_start(out=ROWS[:, k % GR, :], out_offset=None, in_=table,
                                                in_offset=bass.IndirectOffsetOnAxis(ap=GIS[:, par, k:k + 1], axis=0)
                                                ).then_inc(rows_loaded[k % GR], 16)

                for table, before in ((u_rows, 0), (v_rows, GSTEPS)):
                    with pool.Fori(0, GSTEPS // 2) as it:
                        rows(table, it, 0, before)
                        rows(table, it, 1, before)
                pool.wait_ge(sp_at_f, 1)
                for s in early_sems:
                    pool.sem_clear(s)
                pool.wait_ge(engines_done, 4)
                for s in late_sems:
                    pool.sem_clear(s)
                pool.nop().then_inc(next_layer, 1)

        P_A, P_B, P_D = 16 * 3, 16 * 7, 16 * 9

        @block.tensor
        def _(pe):
            pe.wait_ge(first_loads, 16)

            def turn_norm(first, xs):
                for b in range(NB):
                    pe.wait_ge(xs_ready, first + b + 1)
                    for half in range(2):
                        n = 2 * b + half
                        if n >= 4:
                            pe.wait_ge(xnt_ready, 2 * first + n - 3)
                        for k in range(4):
                            last = nc.tensor.transpose(ps[:, n % 4, k * P:(k + 1) * P],
                                                       xs[:, b % 2, (half * 4 + k) * P:(half * 4 + k + 1) * P], ident)
                        last.then_inc(xs_turned, 1)

            with pe.Fori(0, DEPTH) as l:
                turn_norm(0, XS)
                need_tile(pe, T_Q)
                need_tile(pe, T_KV)
                wq = WR[:, T_Q % RING, :].rearrange("p (k n) -> p k n", n=AW)
                wkv = WR[:, T_KV % RING, 0:KC * 2 * KVW].rearrange("p (k n) -> p k n", n=2 * KVW)
                for b in range(NB):
                    pe.wait_ge(xnt_ready, 2 * b + 2)
                    if b >= 2:
                        pe.wait_ge(qkv_copied, 2 * (b - 1))
                    for (w, n, o) in ((wq, AW, 0), (wkv, 2 * KVW, 1)):
                        for k in range(KC):
                            last = nc.tensor.matmul(ps[:, 4 + 2 * (b % 2) + o, 0:n], XNT[:, k, b * P:(b + 1) * P],
                                                    w[:, k, :], start=(k == 0), stop=(k == KC - 1))
                        last.then_inc(qkv_out, 1)
                def hyena_in(n):
                    t, bank = T_HY + n // 4, hy_bank(n)
                    if n % 4 == 0:
                        need_tile(pe, t)
                    before = [m for m in range(n) if hy_bank(m) == bank]
                    if before:
                        pe.wait_ge(hy_copied, before[-1] + 1)
                    w = WR[:, t % RING, :].rearrange("p (k n) -> p k n", n=512)
                    for k in range(KC):
                        last = nc.tensor.matmul(ps[:, bank, :], w[:, k, (n % 4) * P:(n % 4 + 1) * P], XNT[:, k, :],
                                                start=(k == 0), stop=(k == KC - 1))
                    last.then_inc(hy_out, 1)

                for n in range(HY_ROPE):
                    hyena_in(n)
                pe.wait_ge(roped, 3)
                pe.wait_ge(qkv_copied, 2 * NB)
                pe.wait_ge(hy_copied, HY_ROPE)
                for c in range(4 + KVH):
                    for b in range(NB):
                        src = (QKV[:, b, c * P:(c + 1) * P] if c < 4 else
                               KREP[:, b, c - 4].rearrange("p r d -> p (r d)"))
                        last = nc.tensor.transpose(ps[:, c, b * P:(b + 1) * P], src, ident)
                    last.then_inc(qk_turned, 1)
                pe.wait_ge(qk_copied, 4 + KVH)

                units = [(b, g) for b in range(NB) for g in range(KVH)]

                def keys_of(b):
                    return max(0, b - 1), min(NB, b + 2)

                def scores(u):
                    b, g = units[u]
                    k0, k1 = keys_of(b)
                    if u >= 1:
                        pe.wait_ge(sc_copied, u)
                    for h in range(GROUP):
                        head = GROUP * g + h
                        rows = slice(HD * (head % 2), HD * (head % 2) + HD)
                        last = nc.tensor.matmul(ps[:, h, 0:(k1 - k0) * P], QT[rows, head // 2, b * P:(b + 1) * P],
                                                KT[rows, g, k0 * P:k1 * P], start=True, stop=True)
                    last.then_inc(sc_out, 1)

                scores(0)
                kbs = 0
                for u, (b, g) in enumerate(units):
                    if u + 1 < len(units):
                        scores(u + 1)
                    if HY_ROPE + u < HY_A:
                        hyena_in(HY_ROPE + u)
                    k0, k1 = keys_of(b)
                    pe.wait_ge(probs_ready, u + 1)
                    for i in range(k1 - k0):
                        if kbs + i >= 2:
                            pe.wait_ge(pt_copied, kbs + i - 1)
                        for h in range(GROUP):
                            last = nc.tensor.transpose(ps[:, 4 + (kbs + i) % 2, h * P:(h + 1) * P],
                                                       SC[:, u % 2, h, i * P:(i + 1) * P], ident)
                        last.then_inc(probs_turned, 1)
                    kbs += k1 - k0
                    pe.wait_ge(pt_copied, kbs)
                    if u >= 1:
                        pe.wait_ge(o_copied, u)
                    for odd in range(2):
                        for i in range(k1 - k0):
                            pt = PT[:, u % 2, i, :].rearrange("p (a b q) -> p b a q", b=2, q=P)
                            last = nc.tensor.matmul(
                                ps[HD * odd:HD * odd + HD, 7, 0:2 * P].rearrange("p (a q) -> p a q", q=P),
                                QKV[:, k0 + i, AW + KVW + g * HD:AW + KVW + (g + 1) * HD],
                                pt[:, odd], start=(i == 0), stop=(i == k1 - k0 - 1))
                    last.then_inc(o_out, 1)
                arrive(pe)

                all_at(pe, 1)
                pe.wait_ge(params, P_B)
                pe.wait_ge(pads_zero, 3)
                nc.tensor.matmul(ps[0:HID, 4, :], W1[:], ZE[:], start=True, stop=True).then_inc(f_out, 1)

                for n in range(HY_A, HY_A + 2):
                    hyena_in(n)
                pe.wait_ge(f_sin, 1)
                nc.tensor.matmul(ps[0:HID, 5, :], W2[:], FR[0:HID, :], start=True, stop=True).then_inc(f_out, 1)
                for n in range(HY_A + 2, NHY):
                    hyena_in(n)
                pe.wait_ge(f_sin, 2)
                for s in range(NB):
                    if s >= 2:
                        pe.wait_ge(hs_ready, s - 1)
                    for i in range(2):
                        last = nc.tensor.matmul(ps[:, 4 + 2 * (s % 2) + i, :], FR[:, s * P:(s + 1) * P],
                                                W3[:, i * HW:(i + 1) * HW], start=True, stop=True)
                    last.then_inc(h3_out, 1)
                need_tile(pe, T_FWD)
                ft = WR[:, T_FWD % RING, :].rearrange("p (s r f) -> p s r f", s=NB, r=2)
                pe.wait_ge(hs_ready, NB)
                pe.wait_ge(hy_copied, NHY)
                for f in range(HC):
                    for r in range(2):
                        n = 2 * f + r
                        if n >= 4:
                            pe.wait_ge(kf_copied, n - 3)
                        for s in range(NB):
                            last = nc.tensor.matmul(ps[:, n % 4, :], ft[:, s, r, f * P:(f + 1) * P], HS[:, r, s, :],
                                                    start=(s == 0), stop=(s == NB - 1))
                        last.then_inc(kf_out, 1)
                pe.wait_ge(z_ready, HC)
                for s in range(NB):
                    for c in range(HC):
                        last = nc.tensor.transpose(ps[:, 4 + s, c * P:(c + 1) * P], ZT[:, c, s * P:(s + 1) * P], ident)
                    last.then_inc(z_turned, 1)
                pe.wait_ge(ztok_ready, NB)
                pe.wait_ge(kf_copied, 2 * HC)
                for f in range(HC):
                    if f >= 2:
                        pe.wait_ge(zf_used, f - 1)
                    for r in range(2):
                        for s in range(NB):
                            last = nc.tensor.matmul(ps[:, 2 * (f % 2) + r, :], ft[:, s, r, f * P:(f + 1) * P],
                                                    ZTOK[:, s, :], start=(s == 0), stop=(s == NB - 1))
                    last.then_inc(zf_out, 1)
                need_tile(pe, T_INV)
                vt = WR[:, T_INV % RING, :].rearrange("p (f r t) -> p f r t", f=HC, r=2)
                pe.wait_ge(yf_ready, HC)
                for c in range(HC):
                    for f in range(HC):
                        for r in range(2):
                            last = nc.tensor.matmul(ps[:, 4 + c, :], YF[:, r, f, c * P:(c + 1) * P], vt[:, f, r, :],
                                                    start=(f == 0 and r == 0), stop=(f == HC - 1 and r == 1))
                    last.then_inc(y_out, 1)
                arrive(pe)

                all_at(pe, 2)

                def three(bank, pairs):
                    for i, (a, c) in enumerate(((0, 0), (0, 1), (1, 0))):
                        for k, (lhs, rhs) in enumerate(pairs):
                            last = nc.tensor.matmul(ps[:, bank, :], lhs[a], rhs[c], start=(i == 0 and k == 0),
                                                    stop=(i == 2 and k == len(pairs) - 1))
                    return last

                for n in range(KC):
                    t = T_BR + n
                    if n >= 2:
                        pe.wait_ge(br_used, n - 1)
                    for bank, i, k0, nk, (xh, xl), ready in ((0, 0, 0, 4, (ATTH, ATTL), 1), (2, 0, 4, 4, (YHH, YHL), 2),
                                                             (1, 1, 0, 8, (XH, XL), 4), (3, 2, 0, 8, (XH, XL), 4)):
                        if n == 0:
                            pe.wait_ge(in_split, ready)
                        if k0 == 0:
                            pe.wait_ge(wb_split, 3 * n + i + 1)
                        _, hi, lo = branch_weights(n, i)
                        last = three(4 * (n % 2) + bank,
                                     [((hi[:, (k0 + k) * P:(k0 + k + 1) * P], lo[:, (k0 + k) * P:(k0 + k + 1) * P]),
                                       (xh[:, k, :], xl[:, k, :])) for k in range(nk)])
                    last.then_inc(br_out, 1)
                pe.wait_ge(mrg_split, KC)
                for half in range(2):
                    pe.wait_ge(wo_split, 4 * half + 4)
                    for b in range(NB):
                        n = half * NB + b
                        if n >= 4:
                            pe.wait_ge(wo_added, n - 3)
                        pairs = []
                        for k in range(KC):
                            _, hi, lo = out_weights(half, k // 2)
                            w = slice(k % 2 * 512, k % 2 * 512 + 512)
                            x = slice(b * P, (b + 1) * P)
                            pairs.append(((MRGH[:, k, x], MRGL[:, k, x]), (hi[:, w], lo[:, w])))
                        three(n % 4, pairs).then_inc(wo_out, 1)
                arrive(pe)

                all_at(pe, 3)
                turn_norm(NB, XS2)
                pe.wait_ge(xnt_ready, 4 * NB)
                pe.wait_ge(params, P_D)

                def queries(n):
                    i, m = divmod(n, QG)
                    if m == 0:
                        need_tile(pe, T_PQ + i)
                    w = WR[:, (T_PQ + i) % RING, :].rearrange("p (k n) -> p k n", n=512)
                    if n >= QG:
                        pe.wait_ge(pq_copied, n - (QG - 1))
                    for k in range(KC):
                        last = nc.tensor.matmul(ps[:, m, :], w[:, k, m * P:(m + 1) * P], XN2[:, k, :],
                                                start=(k == 0), stop=(k == KC - 1))
                    last.then_inc(pq_out, 1)

                def expert_scores(n):
                    i, m = divmod(n, QG)
                    pe.wait_ge(pq_copied, n + 1)
                    if n >= QG:
                        pe.wait_ge(ps_copied, n - (QG - 1))
                    for b in range(NB):
                        last = nc.tensor.matmul(ps[:, 4 + m, b * NK:(b + 1) * NK], PQT[:, i % 2, m, b * P:(b + 1) * P],
                                                KEY[:, m % 2, :], start=True, stop=True)
                    last.then_inc(ps_out, 1)

                queries(0)
                for n in range(HP):
                    if n + 1 < HP:
                        queries(n + 1)
                    expert_scores(n)
                pe.wait_ge(sel_ready, NGRP)
                for b in range(DB):
                    for i in range(3):
                        last = nc.tensor.transpose(ps[:, b, i * P:(i + 1) * P],
                                                   SEL[:, i, b].rearrange("p h m -> p (h m)"), ident)
                    last.then_inc(sel_turned, 1)
                arrive(pe)

                all_at(pe, 4)
                pe.nop().then_inc(g_out, OHR * (OH // 4))
                with pe.Fori(0, DT // TOK_IT) as it:
                    for q in range(TOK_IT // OH):
                        pe.wait_ge(oh_ready, it * OHN + q + 1)
                        for s in range(OH // 4):
                            n = q * (OH // 4) + s
                            pe.wait_ge(g_bank_free, it * 32 + n + 1)
                            for k in range(4):
                                last = nc.tensor.matmul(ps[:, n % 8, k * NK:(k + 1) * NK], OHS[:, q % OHR, 0, 4 * s + k, :],
                                                        OHS[:, q % OHR, 1, 4 * s + k, :], start=True, stop=True)
                            last.then_inc(g_out, 1)
                arrive(pe)

                all_at(pe, 5)

                pe.nop().then_inc(v_out, 1)

                def up(j, jj):
                    pe.wait_ge(u_split, j + 1)
                    if not isinstance(j, int) or j >= JG:
                        pe.wait_ge(act_ready, j - 3)
                    parts = [(UHI, XHI), (UHI, XLO), (ULO, XHI)]
                    for i, (a, c) in enumerate(parts):
                        for k in range(KC):
                            last = nc.tensor.matmul(ps[:, jj, 0:DT], a[:, jj, k, :], c[:, k, :],
                                                    start=(i == 0 and k == 0), stop=(i == 2 and k == KC - 1))
                    last.then_inc(u_done, 1)

                def down(g, par, o):
                    dh, b = divmod(o, DB)
                    if o == 0:
                        pe.wait_ge(w_ready, g * 4 + 4)
                    if b == 0:
                        pe.wait_ge(v_split, g * 8 + 4 * dh + 4)
                    pe.wait_ge(out_free, g * NOUT + o + 1)
                    n, g0 = 0, par * NOUT
                    for a, c in ((WHI, VHI), (WHI, VLO), (WLO, VHI)):
                        for jj in range(JG):
                            last = nc.tensor.matmul(ps[:, 4 + (g0 + o) % 4, :], a[:, par, jj, b * P:(b + 1) * P],
                                                    c[:, dh, jj, :], start=(n == 0), stop=(n == 3 * JG - 1))
                            n += 1
                    last.then_inc(v_out, 1)

                def step(g, par, more=True):
                    for jj in range(JG):
                        if more:
                            up(g * 4 + 4 + jj, jj)
                        for o in SLOTS[jj]:
                            down(g, par, o)

                for jj in range(JG):
                    up(jj, jj)
                with pe.Fori(0, (NG - 2) // 2) as it:
                    step(it * 2, 0)
                    step(it * 2 + 1, 1)
                step(NG - 2, 0)
                step(NG - 1, 1, more=False)
                end_layer(pe, l)

        @block.scalar
        def _(act):
            act.wait_ge(pre_steps, SINCOS_ARGS)
            nc.scalar.activation(SINCOS[:], SINCOS[:], ACT.Sin).then_inc(pre_sin, 1)
            act.wait_ge(x_loaded, 16)

            def squares(n, xs):
                for b in range(NB):
                    nc.scalar.activation(xs[:, 0, :], X[:, b, :], ACT.Square,
                                         accum_out=SS[:, b:b + 1]).then_inc(sumsq, 1)
                    act.wait_ge(sumsq, n + b + 1)
                act.wait_ge(var_ready, n // NB + 1)
                nc.scalar.activation(SR, SV, ACT.Sqrt).then_inc(root_ready, 1)

            with act.Fori(0, DEPTH) as l:
                squares(0, XS)
                for b in range(NB):
                    for o, n, c0 in ((0, AW, 0), (1, 2 * KVW, AW)):
                        act.wait_ge(qkv_out, 2 * b + o + 1)
                        nc.scalar.copy(QKV[:, b, c0:c0 + n], ps[:, 4 + 2 * (b % 2) + o, 0:n]).then_inc(qkv_copied, 1)
                def hyena_copy(n):
                    act.wait_ge(hy_out, n + 1)
                    nc.scalar.copy(HYT[:, n, 1:SEQ + 1], ps[:, hy_bank(n), :]).then_inc(hy_copied, 1)

                for n in range(HY_ROPE):
                    hyena_copy(n)
                for c in range(4 + KVH):
                    act.wait_ge(qk_turned, c + 1)
                    dst = QT[:, c, :] if c < 4 else KT[:, c - 4, :]
                    nc.scalar.copy(dst, ps[:, c, :]).then_inc(qk_copied, 1)
                units = [(b, g) for b in range(NB) for g in range(KVH)]
                kbs = [0]

                def probs(u):
                    b, g = units[u]
                    n = (min(NB, b + 2) - max(0, b - 1)) * P
                    act.wait_ge(mx_ready, u + 1)
                    for h in range(GROUP):
                        nc.scalar.activation(SC[:, u % 2, h, 0:n], SC[:, u % 2, h, 0:n], ACT.Exp,
                                             bias=MX[:, 4 * (u % 2) + h:4 * (u % 2) + h + 1],
                                             accum_out=DEN[:, 4 * (u % 2) + h:4 * (u % 2) + h + 1])
                    nc.scalar.activation(DSK[:, 4 * (u % 2):4 * (u % 2) + 4], DSK[:, 4 * (u % 2):4 * (u % 2) + 4],
                                         ACT.Exp).then_inc(exp_done, 1)

                def copies(u):
                    b, g = units[u]
                    for i in range(min(NB, b + 2) - max(0, b - 1)):
                        act.wait_ge(probs_turned, kbs[0] + 1)
                        nc.scalar.copy(PT[:, u % 2, i, :], ps[:, 4 + kbs[0] % 2, :]).then_inc(pt_copied, 1)
                        kbs[0] += 1
                    act.wait_ge(o_out, u + 1)
                    nc.scalar.copy(ATT[:, 2 * g:2 * g + 2, b * P:(b + 1) * P],
                                   ps[:, 7, 0:2 * P].rearrange("p (a q) -> p a q", q=P)).then_inc(o_copied, 1)

                probs(0)
                for u in range(len(units)):
                    if u + 1 < len(units):
                        probs(u + 1)
                    if HY_ROPE + u < HY_A:
                        hyena_copy(HY_ROPE + u)
                    copies(u)
                arrive(act)

                all_at(act, 1)
                act.wait_ge(pads_zero, 3)
                act.wait_ge(f_arg, 1)
                nc.scalar.activation(FR[0:HID, :], FA[:], ACT.Sin).then_inc(f_sin, 1)

                for n in range(HY_A, HY_A + 2):
                    hyena_copy(n)
                act.wait_ge(f_arg, 2)
                nc.scalar.activation(FR[0:HID, :], FA[:], ACT.Sin).then_inc(f_sin, 1)
                for n in range(HY_A + 2, NHY):
                    hyena_copy(n)
                for s in range(NB):
                    act.wait_ge(h3_out, s + 1)
                    if s >= 1:
                        act.wait_ge(hs_ready, s)
                    nc.scalar.copy(VT[:, 0, :], ps[:, 4 + 2 * (s % 2) + 1, :]).then_inc(h3_copied, 1)
                for n in range(2 * HC):
                    act.wait_ge(kf_out, n + 1)
                    nc.scalar.copy(KF[:, n % 2, n // 2, :], ps[:, n % 4, :]).then_inc(kf_copied, 1)
                for s in range(NB):
                    act.wait_ge(z_turned, s + 1)
                    nc.scalar.copy(ZTOK[:, s, :], ps[:, 4 + s, :]).then_inc(ztok_ready, 1)
                arrive(act)

                all_at(act, 2)

                def branch_high(n):
                    need_tile(act, T_BR + n)
                    if n >= 2:
                        act.wait_ge(br_out, n - 1)
                    for i in range(3):
                        high(*branch_weights(n, i)).then_inc(wb_hi, 1)

                def merged_high(n):
                    act.wait_ge(mrg_ready, n + 1)
                    high(MRG[:, n, :], MRGH[:, n, :], MRGL[:, n, :]).then_inc(mrg_hi, 1)

                def out_high(half):
                    need_tile(act, T_OUT + half)
                    act.wait_ge(br_out, KC - 1 + half)
                    for i in range(4):
                        high(*out_weights(half, i)).then_inc(wo_hi, 1)

                high(*C_IN[0]).then_inc(in_hi, 1)
                branch_high(0)
                for part in C_IN[1:]:
                    high(*part).then_inc(in_hi, 1)
                for n in range(KC):
                    if n + 1 < KC:
                        branch_high(n + 1)
                    else:
                        out_high(0)
                    act.wait_ge(br_out, n + 1)
                    if n >= 2:
                        act.wait_ge(br_used, n - 1)
                    for i in range(2):
                        last = nc.scalar.activation(SG[:, n % 2, i, :], ps[:, 4 * (n % 2) + 2 * i + 1, :], ACT.Sigmoid)
                    last.then_inc(sg_ready, 1)
                    if n >= 1:
                        merged_high(n - 1)
                merged_high(KC - 1)
                out_high(1)
                arrive(act)

                all_at(act, 3)
                squares(NB, XS2)
                for n in range(2 * DB):
                    act.wait_ge(xnt_ready, 2 * NB + n + 1)
                    b, half = divmod(n, 2)
                    part = (slice(None), slice(4 * half, 4 * half + 4), slice(b * P, (b + 1) * P))
                    nc.scalar.copy(XHI[part], XN2[part]).then_inc(xhi_ready, 1)

                def one_hot_rows(i, k):
                    act.wait_ge(rows_apart, 2 * i + 2 - k)
                    nc.scalar.activation(EQ[:, k], EQ[:, k], ACT.Abs).then_inc(rows_abs, 1)
                    act.wait_ge(rows_abs, 2 * i + 2 - k)
                    nc.scalar.activation(EQ[:, k], EQ[:, k], ACT.Relu, bias=1.0, scale=-1.0).then_inc(rows_ready, 1)

                for n in range(HP + 1):
                    if n < HP:
                        i, m = divmod(n, QG)
                        act.wait_ge(pq_out, n + 1)
                        if m == 0 and i >= 2:
                            act.wait_ge(ps_out, QG * (i - 1))
                        nc.scalar.copy(PQT[:, i % 2, m, :], ps[:, m, :]).then_inc(pq_copied, 1)
                    if n >= 1:
                        i, m = divmod(n - 1, QG)
                        if m == 0 and i >= 2:
                            act.wait_ge(ps_free, i - 1)
                        act.wait_ge(ps_out, n)
                        nc.scalar.copy(PS[:, i % 2, m].rearrange("p b k -> p (b k)"), ps[:, 4 + m, :]).then_inc(ps_copied, 1)
                        if m == QG - 1 and i >= 1:
                            act.wait_ge(bmax_ready, i)
                            nc.scalar.activation(BE[:, (i - 1) % 2], BE[:, (i - 1) % 2], ACT.Exp).then_inc(bexp_ready, 1)
                            one_hot_rows(i - 1, 1)
                        if m == 0 and i >= 2:
                            one_hot_rows(i - 2, 0)
                one_hot_rows(NGRP - 2, 0)
                act.wait_ge(bmax_ready, NGRP)
                nc.scalar.activation(BE[:, (NGRP - 1) % 2], BE[:, (NGRP - 1) % 2], ACT.Exp).then_inc(bexp_ready, 1)
                for b in range(DB):
                    act.wait_ge(sel_turned, b + 1)
                    nc.scalar.copy(IDXT[:, :, b * P:(b + 1) * P],
                                   ps[:, b, 0:3 * P].rearrange("p (a c) -> p a c", a=3)).then_inc(idx_copied, 1)
                arrive(act)

                all_at(act, 4)
                act.nop().then_inc(g_bank_free, 8)
                with act.Fori(0, DT // TOK_IT) as it:
                    for n in range(TOK_IT // 4):
                        s, c = divmod(4 * n, CB)
                        act.wait_ge(g_out, it * 32 + n + 1 + OHR * (OH // 4))
                        if c == 0:
                            act.wait_ge(gst_free, it * 2 + s + 1)
                        nc.scalar.copy(GST[:, s, :, c:c + 4].rearrange("p j c -> p c j"),
                                       ps[:, n % 8, :].rearrange("p (c j) -> p c j", c=4)).then_inc(g_bank_free, 1)
                arrive(act)

                all_at(act, 5)

                def split_u(g, jj):
                    j = g * 4 + jj
                    act.wait_ge(u_loaded[jj // 2], g * 16 + 16)
                    if not isinstance(j, int) or j >= JG:
                        act.wait_ge(u_done, j - 3)
                    nc.scalar.copy(UHI[:, jj].rearrange("p k i -> p (k i)"), URAW[:, jj // 2, jj % 2, :]).then_inc(u_hi, 1)

                def split_v(g, dh, pair):
                    if pair == 0:
                        act.wait_ge(v_loaded[dh], g * 16 + 16)
                        if dh == 1:
                            act.wait_ge(v_out, g * NOUT + 1)
                        elif not isinstance(g, int) or g >= 1:
                            act.wait_ge(v_out, g * NOUT - (NOUT // 2 - 1))
                    for jj in (2 * pair, 2 * pair + 1):
                        nc.scalar.copy(VHI[:, dh, jj, :], VRAW[:, dh, jj, :]).then_inc(v_hi, 1)

                def gelu(j, jj):
                    act.wait_ge(u_done, j + 1)
                    if not isinstance(j, int) or j >= 2:
                        act.wait_ge(w_ready, j - 1)
                    nc.scalar.activation(AC[:, jj % 2, :], ps[:, jj, 0:DT], ACT.Gelu).then_inc(act_ready, 1)

                def step(g, columns=True, first=False, ahead=JG):
                    for jj in range(JG):
                        if columns and jj < ahead:
                            split_u(g + 1 + (2 + jj) // 4, (2 + jj) % 4)
                        if first and jj == 0:
                            g_all_stored(act)
                        if jj < 2 and not first:
                            split_v(g, 1, jj)
                        if jj >= 2 and columns:
                            split_v(g + 1, 0, jj - 2)
                        if columns:
                            gelu(g * 4 + 4 + jj, jj)

                split_u(0, 0)
                split_u(0, 1)
                step(-1, first=True)
                with act.Fori(0, GSTEPS) as g:
                    step(g)
                act.wait_ge(dots_done, GSTEPS)
                nc.scalar.activation(DOT[:], DOT[:], ACT.Gelu).then_inc(gelu_done, 1)
                with act.Fori(GSTEPS, NG - 2) as g:
                    step(g)
                step(NG - 2, ahead=2)
                step(NG - 1, columns=False)
                end_layer(act, l)
            for b in range(NB):
                nc.scalar.activation(OUTB[:, 0, :], X[:, b, :], ACT.Square,
                                     accum_out=SS[:, b:b + 1]).then_inc(pre_sin, 1)
                act.wait_ge(pre_sin, 2 + b)
            act.wait_ge(pre_steps, FINAL_VAR)
            nc.scalar.activation(SR, SV, ACT.Sqrt).then_inc(pre_sin, 1)

        @block.vector
        def _(dve):
            pre = Steps(pre_steps)

            def reduce_angle(steps, r, a, k, quarter, shift):
                steps.did(nc.vector.tensor_scalar(k, a, 1.0 / (2 * math.pi), quarter, ALU.mult, ALU.add))
                steps.then(dve)
                steps.did(nc.vector.tensor_scalar(k, k, ROUND, ROUND, ALU.add, ALU.subtract))
                steps.then(dve)
                for i, c in enumerate((TWO_PI_HI, TWO_PI_MID, TWO_PI_LO)):
                    steps.did(nc.vector.scalar_tensor_tensor(r, k, -c, a if i == 0 else r, ALU.mult, ALU.add))
                    steps.then(dve)
                if shift:
                    steps.did(nc.vector.tensor_scalar(r, r, shift, None, ALU.add))
                    steps.then(dve)
                steps.did(nc.vector.tensor_scalar(r, r, PI_IN, -PI_IN, ALU.min, ALU.max))
                steps.then(dve)

            dve.wait_ge(x_loaded, 16)
            dve.wait_ge(pos_loaded, 16)
            dve.wait_ge(first_loads, 16)
            ang, kk = RT[:, 0, :, 0, :], RT[:, 1, :, 0, :]
            pre.did(nc.vector.tensor_copy(SV, POSF[:].bitcast(I32)))
            pre.then(dve)
            pre.did(nc.vector.tensor_tensor(ang, SV.unsqueeze(2).to_broadcast([P, NB, ROT]),
                                            CST[:, C_FREQ:C_FREQ + ROT].unsqueeze(1).to_broadcast([P, NB, ROT]), ALU.mult))
            pre.then(dve)
            reduce_angle(pre, SINCOS[:, 0], ang, kk, 0.0, 0.0)
            reduce_angle(pre, SINCOS[:, 1], ang, kk, 0.25, math.pi / 2)
            assert pre.n == SINCOS_ARGS
            dve.wait_ge(pre_sin, 1)

            def inverse_root(steps, n):
                steps.did(nc.vector.reciprocal(SR, SR))
                steps.then(dve)
                steps.did(nc.vector.tensor_tensor(ST, SR, SR, ALU.mult))
                steps.then(dve)
                steps.did(nc.vector.tensor_tensor(ST, ST, SV, ALU.mult))
                steps.then(dve)
                steps.did(nc.vector.tensor_scalar(ST, ST, -0.5, 1.5, ALU.mult, ALU.add))
                steps.then(dve)
                steps.did(nc.vector.tensor_tensor(SR, SR, ST, ALU.mult))
                steps.then(dve)

            def norm(steps, first, xs, xnt, gcol):
                dve.wait_ge(sumsq, first + NB)
                nc.vector.tensor_scalar(SV, SS, 1.0 / DM, EPS, ALU.mult, ALU.add).then_inc(var_ready, 1)
                dve.wait_ge(var_ready, first // NB + 1)
                dve.wait_ge(root_ready, first // NB + 1)
                inverse_root(steps, NB)
                scaled = lambda b: nc.vector.tensor_scalar(xs[:, b % 2, :], X[:, b, :], SR[:, b:b + 1], None,
                                                           ALU.mult).then_inc(xs_ready, 1)
                for b in range(NB + 1):
                    if b < NB:
                        if b >= 2:
                            dve.wait_ge(xs_turned, 2 * first + 2 * (b - 1))
                        scaled(b)
                    if b >= 1:
                        for half in range(2):
                            n = 2 * (b - 1) + half
                            dve.wait_ge(xs_turned, 2 * first + n + 1)
                            nc.vector.tensor_tensor(
                                xnt[:, 4 * half:4 * half + 4, (b - 1) * P:b * P],
                                ps[:, n % 4, :].rearrange("p (k c) -> p k c", k=4),
                                COL[:, gcol + 4 * half:gcol + 4 * half + 4].unsqueeze(2).to_broadcast([P, 4, P]),
                                ALU.mult).then_inc(xnt_ready, 1)

            with dve.Fori(0, DEPTH) as l:
                st = Steps(dve_steps)
                dve.wait_ge(params, P_A)
                norm(st, 0, XS, XNT, L_GMIX)
                dve.wait_ge(qkv_copied, 2 * NB)
                heads = QKV[:, :, 0:AW + KVW].rearrange("p b (h d) -> p b h d", d=HD)
                shape = [P, NB, QH + KVH, ROT]
                t1, t2 = heads[:, :, :, 0:ROT], heads[:, :, :, ROT:2 * ROT]
                sin, cos = (SINCOS[:, i].unsqueeze(2).to_broadcast(shape) for i in range(2))
                for i, (a, c) in enumerate(((t1, cos), (t2, sin), (t2, cos), (t1, sin))):
                    st.did(nc.vector.tensor_tensor(RT[:, i], a, c, ALU.mult))
                st.then(dve)
                nc.vector.tensor_tensor(t1, RT[:, 0], RT[:, 1], ALU.subtract)
                nc.vector.tensor_tensor(t2, RT[:, 2], RT[:, 3], ALU.add).then_inc(roped, 1)
                dve.wait_ge(roped, 1)
                for r in range(2):
                    nc.vector.tensor_copy(KREP[:, :, :, r, :], QKV[:, :, AW:AW + KVW].rearrange("p b (g d) -> p b g d", d=HD)
                                          ).then_inc(roped, 1)

                units = [(b, g) for b in range(NB) for g in range(KVH)]

                def take_scores(u):
                    b, g = units[u]
                    k0, k1 = max(0, b - 1), min(NB, b + 2)
                    n = (k1 - k0) * P
                    m0 = (k0 - (b - 1)) * P
                    m = MX[:, 4 * (u % 2):4 * (u % 2) + 4]
                    dve.wait_ge(sc_out, u + 1)
                    if u >= 2:
                        dve.wait_ge(probs_turned, kb_done[u - 2])
                    mask = CST[:, C_MASK + m0:C_MASK + m0 + n].unsqueeze(1).to_broadcast([P, GROUP, n])
                    nc.vector.scalar_tensor_tensor(SC[:, u % 2, :, 0:n], ps[:, 0:GROUP, 0:n], HD ** -0.5, mask,
                                                   ALU.mult, ALU.add).then_inc(sc_copied, 1)
                    dve.wait_ge(sc_copied, u + 1)
                    st.did(nc.vector.tensor_reduce(m, SC[:, u % 2, :, 0:n], axis=AX, op=ALU.max))
                    st.then(dve)
                    sink4 = SINK[:, GROUP * g:GROUP * g + 4]
                    st.did(nc.vector.tensor_tensor(m, m, sink4, ALU.max))
                    st.then(dve)
                    st.did(nc.vector.tensor_tensor(DSK[:, 4 * (u % 2):4 * (u % 2) + 4], sink4, m, ALU.subtract))
                    nc.vector.tensor_scalar(m, m, -1.0, None, ALU.mult).then_inc(mx_ready, 1)

                def normalise(u):
                    b, g = units[u]
                    n = (min(NB, b + 2) - max(0, b - 1)) * P
                    den = DEN[:, 4 * (u % 2):4 * (u % 2) + 4]
                    dve.wait_ge(exp_done, u + 1)
                    st.did(nc.vector.tensor_tensor(den, den, DSK[:, 4 * (u % 2):4 * (u % 2) + 4], ALU.add))
                    st.then(dve)
                    st.did(nc.vector.reciprocal(den, den))
                    st.then(dve)
                    for h in range(GROUP):
                        last = nc.vector.tensor_scalar(SC[:, u % 2, h, 0:n], SC[:, u % 2, h, 0:n], den[:, h:h + 1], None,
                                                       ALU.mult)
                    last.then_inc(probs_ready, 1)

                kb_done, total = [], 0
                for b, g in units:
                    total += min(NB, b + 2) - max(0, b - 1)
                    kb_done.append(total)
                take_scores(0)
                for u in range(len(units)):
                    if u + 1 < len(units):
                        take_scores(u + 1)
                    normalise(u)
                arrive(dve)

                all_at(dve, 1)
                dve.wait_ge(params, P_B)

                def short_conv(i, dst):
                    for c in range(HC):
                        n = HC * i + c
                        if c == 0:
                            dve.wait_ge(hy_copied, n + HC)
                        st.did(nc.vector.tensor_scalar(dst[:, c, :], HYT[:, n, 0:SEQ], COL[:, L_CONVW + 3 * n:L_CONVW + 3 * n + 1],
                                                       COL[:, L_CONVB + n:L_CONVB + n + 1], ALU.mult, ALU.add))
                    for tap in (1, 2):
                        st.then(dve)
                        for c in range(HC):
                            n = HC * i + c
                            w = COL[:, L_CONVW + 3 * n + tap:L_CONVW + 3 * n + tap + 1]
                            st.did(nc.vector.scalar_tensor_tensor(dst[:, c, :], HYT[:, n, tap:tap + SEQ], w, dst[:, c, :],
                                                                  ALU.mult, ALU.add))
                    st.then(dve)

                dve.wait_ge(pads_zero, 3)
                for i in range(2):
                    dve.wait_ge(f_out, i + 1)
                    if i == 1:
                        dve.wait_ge(f_sin, 1)
                    st.did(nc.vector.tensor_scalar(FA[:], ps[0:HID, 4 + i, :], FCOL[:, 2 * i:2 * i + 1],
                                                   FCOL[:, 2 * i + 1:2 * i + 2], ALU.add, ALU.mult))
                    st.then(dve)
                    reduce_angle(st, FA[:], FA[:], FK[:], 0.0, 0.0)
                    dve.nop().then_inc(f_arg, 1)
                    if i == 0:
                        short_conv(0, X0)
                dve.wait_ge(dec_loaded, 16)
                for s in range(NB):
                    f, b = ps[:, 4 + 2 * (s % 2), :], VT[:, 0, :]
                    dve.wait_ge(h3_copied, s + 1)
                    st.did(nc.vector.tensor_tensor(HS[:, 0, s, :], f, b, ALU.add))
                    st.did(nc.vector.tensor_tensor(HS[:, 1, s, :], f, b, ALU.subtract))
                    st.then(dve)
                    nc.vector.tensor_tensor(HS[:, 0, s, :], HS[:, 0, s, :], DEC[:, s, :], ALU.mult)
                    nc.vector.tensor_tensor(HS[:, 1, s, :], HS[:, 1, s, :], DEC[:, s, :], ALU.mult).then_inc(hs_ready, 1)
                short_conv(1, ZT)
                dve.wait_ge(hs_ready, NB)
                short_conv(2, VT)
                for c in range(HC):
                    nc.vector.tensor_tensor(ZT[:, c, :], ZT[:, c, :], VT[:, c, :], ALU.mult).then_inc(z_ready, 1)
                dve.wait_ge(kf_copied, 2 * HC)
                dve.wait_ge(z_ready, HC)
                for f in range(HC):
                    zr, zs = ps[:, 2 * (f % 2), :], ps[:, 2 * (f % 2) + 1, :]
                    kr, ks = KF[:, 0, f, :], KF[:, 1, f, :]
                    dve.wait_ge(zf_out, f + 1)
                    if f:
                        dve.wait_ge(yf_ready, f)
                    st.did(nc.vector.tensor_tensor(VT[:, 0, :], zr, kr, ALU.mult))
                    st.did(nc.vector.tensor_tensor(VT[:, 1, :], zs, ks, ALU.mult))
                    st.did(nc.vector.tensor_tensor(VT[:, 2, :], zr, ks, ALU.mult))
                    nc.vector.tensor_tensor(VT[:, 3, :], zs, kr, ALU.mult).then_inc(zf_used, 1)
                    dve.wait_ge(zf_used, f + 1)
                    nc.vector.tensor_tensor(YF[:, 0, f, :], VT[:, 0, :], VT[:, 1, :], ALU.subtract)
                    nc.vector.tensor_tensor(YF[:, 1, f, :], VT[:, 2, :], VT[:, 3, :], ALU.add).then_inc(yf_ready, 1)
                dve.wait_ge(yf_ready, HC)
                for c in range(HC):
                    dve.wait_ge(y_out, c + 1)
                    st.did(nc.vector.scalar_tensor_tensor(VT[:, c, :], ZT[:, c, :], COL[:, L_SKIP + c:L_SKIP + c + 1],
                                                          ps[:, 4 + c, :], ALU.mult, ALU.add))
                    st.then(dve)
                    nc.vector.tensor_tensor(YH[:, c, :], VT[:, c, :], X0[:, c, :], ALU.mult).then_inc(y_used, 1)
                arrive(dve)

                all_at(dve, 2)

                def branch_low(n):
                    for i in range(3):
                        dve.wait_ge(wb_hi, 3 * n + i + 1)
                        low(*branch_weights(n, i)).then_inc(wb_split, 1)

                def merged_low(n):
                    dve.wait_ge(mrg_hi, n + 1)
                    low(MRG[:, n, :], MRGH[:, n, :], MRGL[:, n, :]).then_inc(mrg_split, 1)

                def out_low(half):
                    for i in range(4):
                        dve.wait_ge(wo_hi, 4 * half + i + 1)
                        low(*out_weights(half, i)).then_inc(wo_split, 1)

                for i, part in enumerate(C_IN):
                    dve.wait_ge(in_hi, i + 1)
                    low(*part).then_inc(in_split, 1)
                    if i == 0:
                        branch_low(0)
                for n in range(KC):
                    if n + 1 < KC:
                        branch_low(n + 1)
                    else:
                        out_low(0)
                    dve.wait_ge(sg_ready, n + 1)
                    if n >= 2:
                        dve.wait_ge(mrg_ready, n - 1)
                    st.did(nc.vector.tensor_tensor(MP[:, n % 2, 0, :], ps[:, 4 * (n % 2), :], SG[:, n % 2, 0, :], ALU.mult))
                    nc.vector.tensor_tensor(MP[:, n % 2, 1, :], ps[:, 4 * (n % 2) + 2, :], SG[:, n % 2, 1, :],
                                            ALU.mult).then_inc(br_used, 1)
                    dve.wait_ge(br_used, n + 1)
                    nc.vector.tensor_tensor(MRG[:, n, :], MP[:, n % 2, 0, :], MP[:, n % 2, 1, :],
                                            ALU.add).then_inc(mrg_ready, 1)
                    if n >= 1:
                        merged_low(n - 1)
                merged_low(KC - 1)
                out_low(1)
                for n in range(2 * NB):
                    half, b = divmod(n, NB)
                    dve.wait_ge(wo_out, n + 1)
                    xb = X[:, b, 512 * half:512 * half + 512]
                    nc.vector.tensor_tensor(xb, ps[:, n % 4, :], xb, ALU.add).then_inc(wo_added, 1)
                arrive(dve)

                all_at(dve, 3)
                norm(st, NB, XS2, XN2, L_GFFN)
                dve.wait_ge(params, P_D)
                nc.vector.tensor_tensor(XG[:], XS2[:, (NB - 1) % 2, :], GF[:], ALU.mult)
                for n in range(2 * DB):
                    b, half = divmod(n, 2)
                    part = (slice(None), slice(4 * half, 4 * half + 4), slice(b * P, (b + 1) * P))
                    dve.wait_ge(xhi_ready, n + 1)
                    dve.wait_ge(xnt_ready, 2 * NB + n + 1)
                    nc.vector.tensor_tensor(XLO[part], XN2[part], XHI[part].bitcast(F32), ALU.subtract)
                NV, NS = NB * QG, NB * HG

                def finish_group(i):
                    place = [SEL[:, k, :, HG * i:HG * i + HG, :].rearrange("p b h m -> p b (h m)") for k in range(3)]
                    for k in (1, 0) if i < NGRP - 1 else (0, 1):
                        if k == 1 or i < NGRP - 1:
                            dve.wait_ge(keys_found, 2 * i + 2 - k)
                        if i < NGRP - 1:
                            st.did(nc.vector.tensor_copy(place[k], EQ[:, k, :, 0].rearrange("p (b m) -> p b m", b=NB)))
                        else:
                            st.did(nc.vector.tensor_reduce(place[k], EQ[:, k].rearrange("p (b m) a -> p b m a", b=NB),
                                                           axis=AX, op=ALU.add))
                    dve.wait_ge(bexp_ready, i + 1)
                    be = BE[:, i % 2]
                    st.did(nc.vector.tensor_reduce(GSUM, be, axis=AX, op=ALU.add))
                    st.then(dve)
                    st.did(nc.vector.reciprocal(GSUM, GSUM))
                    st.then(dve)
                    st.did(nc.vector.tensor_tensor(be, be, GSUM.unsqueeze(2).to_broadcast([P, NS, TOPK]), ALU.mult))
                    st.then(dve)
                    nc.vector.tensor_copy(place[2], be.rearrange("p (b h) m -> p b (h m)", b=NB)).then_inc(sel_ready, 1)

                for i in range(NGRP):
                    for m in range(QG):
                        rows = [(b * QG + m, PS[:, i % 2, m, b, :]) for b in range(NB)]
                        dve.wait_ge(ps_copied, QG * i + m + 1)
                        for n, row in rows:
                            st.did(nc.vector.max(TV[:, n, 0:8], row))
                        st.then(dve)
                        for n, row in rows:
                            st.did(nc.vector.max_index(TI[:, n, 0:8], TV[:, n, 0:8], row))
                        st.then(dve)
                        for n, row in rows:
                            st.did(nc.vector.match_replace(row, TV[:, n, 0:8], row, NEG))
                        st.then(dve)
                        for n, row in rows:
                            st.did(nc.vector.max(TV[:, n, 8:16], row))
                        st.then(dve)
                        for n, row in rows:
                            last = nc.vector.max_index(TI[:, n, 8:16], TV[:, n, 8:16], row)
                            if n < NV - 1:
                                st.did(last)
                    last.then_inc(ps_free, 1)
                    dve.wait_ge(ps_free, i + 1)
                    tv = TV[:].rearrange("p (h s) k -> p h s k", s=2)
                    for c0, a0, a1, nb in ((0, 0, FULL, TOPK), (CFULL, FULL, TOPK, NARROW)):
                        st.did(nc.vector.tensor_tensor(
                            CD[:, :, c0:c0 + (a1 - a0) * nb].rearrange("p h (a b) -> p h a b", b=nb),
                            tv[:, :, 0, a0:a1].unsqueeze(3).to_broadcast([P, NS, a1 - a0, nb]),
                            tv[:, :, 1, 0:nb].unsqueeze(2).to_broadcast([P, NS, a1 - a0, nb]), ALU.add))
                    st.did(nc.vector.tensor_copy(TIF[:, i % 2], TI[:]))
                    st.then(dve)
                    cd = [CD[:, h] for h in range(NS)]
                    for h in range(NS):
                        st.did(nc.vector.max(BV[:, h, 0:8], cd[h]))
                    st.then(dve)
                    for h in range(NS):
                        st.did(nc.vector.max_index(BP[:, h, 0:8], BV[:, h, 0:8], cd[h]))
                    st.then(dve)
                    for h in range(NS):
                        st.did(nc.vector.match_replace(cd[h], BV[:, h, 0:8], cd[h], NEG))
                    st.then(dve)
                    for h in range(NS):
                        st.did(nc.vector.max(BV[:, h, 8:16], cd[h]))
                    st.then(dve)
                    for h in range(NS):
                        st.did(nc.vector.max_index(BP[:, h, 8:16], BV[:, h, 8:16], cd[h]))
                    st.then(dve)
                    nc.vector.tensor_tensor(BE[:, i % 2], BV[:], BV[:, :, 0:1].to_broadcast([P, NS, TOPK]),
                                            ALU.subtract).then_inc(bmax_ready, 1)
                    if i >= 1:
                        finish_group(i - 1)
                    bp = BP[:].rearrange("p h m -> p (h m)")
                    for k, (op, n) in enumerate(((ALU.logical_shift_right, 4), (ALU.bitwise_and, TOPK - 1),
                                                 (ALU.logical_shift_right, 2), (ALU.bitwise_and, NARROW - 1))):
                        st.did(nc.vector.tensor_scalar(BA[:, k, :], bp, n, None, op))
                    st.then(dve)
                    st.did(nc.vector.tensor_copy(BAF[:], BA[:]))
                    st.then(dve)
                    st.did(nc.vector.tensor_scalar(NARW[:], BAF[:, 2, :], float(CFULL // NARROW), None, ALU.is_ge))
                    st.did(nc.vector.scalar_tensor_tensor(BAF[:, 2, :], BAF[:, 2, :], float(CFULL // NARROW - FULL),
                                                          BAF[:, 0, :], ALU.subtract, ALU.subtract))
                    st.did(nc.vector.tensor_tensor(BAF[:, 3, :], BAF[:, 3, :], BAF[:, 1, :], ALU.subtract))
                    st.then(dve)
                    st.did(nc.vector.tensor_tensor(BAF[:, 2:4, :], BAF[:, 2:4, :],
                                                   NARW[:].unsqueeze(1).to_broadcast([P, 2, NS * TOPK]), ALU.mult))
                    st.then(dve)
                    nc.vector.tensor_tensor(BAF[:, 0:2, :], BAF[:, 0:2, :], BAF[:, 2:4, :], ALU.add).then_inc(places_ready, 1)
                dve.wait_ge(places_ready, NGRP)
                for k in (1, 0):
                    nc.vector.tensor_tensor(EQ[:, k], *places_and_columns(k), ALU.is_equal).then_inc(rows_ready, 1)
                dve.wait_ge(rows_ready, 2 * NGRP)
                st.did(times_keys(nc.vector, NGRP - 1, 0))
                st.then(dve)
                finish_group(NGRP - 1)
                dve.wait_ge(sel_ready, NGRP)
                picks = [SEL[:, k, NB - 1].rearrange("p h m -> p (h m)") for k in range(3)]
                nc.vector.tensor_copy(GG[:], picks[2])
                st.did(nc.vector.scalar_tensor_tensor(GIF[:], picks[0], float(NK), picks[1], ALU.mult, ALU.add))
                st.then(dve)
                st.did(nc.vector.tensor_scalar(GIF[:], GIF[:], COL[:, L_BASE:L_BASE + 1], None, ALU.add))
                st.then(dve)
                nc.vector.tensor_copy(GI[:], GIF[:])
                arrive(dve)

                all_at(dve, 4)
                with dve.Fori(0, DT // TOK_IT) as it:
                    for q in range(TOK_IT // OH):
                        picks = IDXT[:, 0:2, bass.ds(it * TOK_IT + q * OH, OH)]
                        dve.wait_ge(g_out, it * 32 + OH // 4 * (q + 1))
                        nc.vector.tensor_tensor(OHS[:, q % OHR], picks.unsqueeze(3).to_broadcast([P, 2, OH, NK]),
                                                CST[:, C_IOTA:C_IOTA + NK].unsqueeze(1).unsqueeze(1).to_broadcast([P, 2, OH, NK]),
                                                ALU.is_equal).then_inc(oh_made, 1)
                arrive(dve)

                all_at(dve, 5)
                dve.nop().then_inc(out_free, 4)

                def split_u(j, jj):
                    dve.wait_ge(u_hi, j + 1)
                    nc.vector.tensor_tensor(ULO[:, jj].rearrange("p k i -> p (k i)"), URAW[:, jj // 2, jj % 2, :],
                                            UHI[:, jj].rearrange("p k i -> p (k i)").bitcast(F32),
                                            ALU.subtract).then_inc(u_split, 1)

                def split_v(g, dh, pair):
                    for jj in (2 * pair, 2 * pair + 1):
                        dve.wait_ge(v_hi, g * 8 + 4 * dh + jj + 1)
                        nc.vector.tensor_tensor(VLO[:, dh, jj, :], VRAW[:, dh, jj, :], VHI[:, dh, jj, :].bitcast(F32),
                                                ALU.subtract).then_inc(v_split, 1)

                def weigh(j, jj, par, use):
                    blocks = "p (b c) -> p b c"
                    dve.wait_ge(act_ready, j + 1)
                    dve.wait_ge(g_loaded[par], use)
                    nc.vector.tensor_tensor(WF[:, jj % 2, :].rearrange(blocks, c=CB),
                                            AC[:, jj % 2, :].rearrange(blocks, c=CB), GT[:, par, :, jj, :],
                                            ALU.mult).then_inc(wf_ready, 1)
                    dve.wait_ge(wf_ready, j + 1)
                    nc.vector.tensor_copy(WHI[:, par, jj, :], WF[:, jj % 2, :]).then_inc(whi_ready, 1)
                    dve.wait_ge(whi_ready, j + 1)
                    nc.vector.tensor_tensor(WLO[:, par, jj, :], WF[:, jj % 2, :], WHI[:, par, jj, :].bitcast(F32),
                                            ALU.subtract).then_inc(w_ready, 1)

                def dot(s, par, k):
                    dve.wait_ge(rows_loaded[k % GR], l * ROWS_LAYER + s * (16 * GS // GR) + 16 * (k // GR + 1))
                    nc.vector.tensor_tensor_reduce(ROWS[:, k % GR, :], ROWS[:, k % GR, :], XG[:], 1.0, 0.0, ALU.mult, ALU.add,
                                                   accum_out=STG[:, par, k:k + 1]).then_inc(rows_used, 1)

                def keep_dots(s, par):
                    dve.wait_ge(rows_used, s * GS + (GR + GS))
                    nc.vector.tensor_copy(DOT[:, bass.ds(s * GS, GS)], STG[:, par, :]).then_inc(dots_done, 1)

                def stage_weights(s, par):
                    nc.vector.tensor_copy(STG[:, par, :], GW[:, bass.ds((s - GSTEPS) * GS, GS)]).then_inc(stg_ready, 1)

                def add_row(s, par, k):
                    dve.wait_ge(rows_loaded[k % GR], l * ROWS_LAYER + s * (16 * GS // GR) + 16 * (k // GR + 1))
                    if k == 0:
                        dve.wait_ge(stg_ready, s - (GSTEPS - 1))
                    dve.wait_ge(rows_used, s * GS + (GR + k))
                    nc.vector.scalar_tensor_tensor(X[:, NB - 1, :], ROWS[:, k % GR, :], STG[:, par, k:k + 1],
                                                   X[:, NB - 1, :], ALU.mult, ALU.add).then_inc(rows_used, 1)

                def add_output(g, par, o):
                    dh, b = divmod(o, DB)
                    xb = X[:, b, 512 * dh:512 * dh + 512]
                    dve.wait_ge(v_out, g * NOUT + o + 2)
                    nc.vector.tensor_tensor(xb, ps[:, 4 + (par * NOUT + o) % 4, :], xb, ALU.add).then_inc(out_free, 1)

                def step(g, par, use, columns=True, first=False, ahead=JG, rows=None):
                    if rows is add_row:
                        stage_weights(g, 1 - par)
                    for jj in range(JG):
                        if columns and jj < ahead:
                            split_u(g * 4 + 6 + jj, (2 + jj) % 4)
                        if jj < 2 and not first:
                            split_v(g, 1, jj)
                        if jj >= 2 and columns:
                            split_v(g + 1, 0, jj - 2)
                        if columns:
                            weigh(g * 4 + 4 + jj, jj, par, use)
                        if rows:
                            rows(g, 1 - par, 2 * jj)
                        if not first:
                            for o in SLOTS[jj]:
                                add_output(g, 1 - par, o)
                        if rows:
                            rows(g, 1 - par, 2 * jj + 1)
                    if rows is dot:
                        keep_dots(g, 1 - par)

                split_u(0, 0)
                split_u(1, 1)
                step(-1, 0, 16, first=True)
                dve.nop().then_inc(rows_used, GR)
                with dve.Fori(0, GSTEPS // 2) as it:
                    step(it * 2, 1, it * 16 + 16, rows=dot)
                    step(it * 2 + 1, 0, it * 16 + 32, rows=dot)
                dve.wait_ge(gelu_done, 1)
                nc.vector.tensor_tensor(GW[:], DOT[:], GG[:], ALU.mult).then_inc(gw_ready, 1)
                dve.wait_ge(gw_ready, 1)
                with dve.Fori(GSTEPS // 2, (NG - 2) // 2) as it:
                    step(it * 2, 1, it * 16 + 16, rows=add_row)
                    step(it * 2 + 1, 0, it * 16 + 32, rows=add_row)
                step(NG - 2, 1, 8 * NG, ahead=2, rows=add_row)
                step(NG - 1, 0, 0, columns=False, rows=add_row)
                end_layer(dve, l)

            dve.wait_ge(pre_sin, 1 + NB)
            pre.did(nc.vector.tensor_scalar(SV, SS, 1.0 / DM, EPS, ALU.mult, ALU.add))
            assert pre.n == FINAL_VAR
            dve.wait_ge(pre_sin, 2 + NB)
            inverse_root(pre, NB)
            dve.wait_ge(first_loads, 32)
            for b in range(NB):
                pre.did(nc.vector.tensor_scalar(OUTB[:, b, :], X[:, b, :], SR[:, b:b + 1], None, ALU.mult))
            pre.then(dve)
            assert pre.n == FINAL0
            for b in range(NB):
                pre.did(nc.vector.tensor_tensor(OUTB[:, b, :], OUTB[:, b, :], GFIN[:], ALU.mult))


def shape_tables():
    f4 = np.float32
    const = np.zeros((P, NCONST), f4)
    const[:, C_ID:C_ID + P] = np.eye(P)
    const[:, C_IOTA:C_IOTA + NK] = np.arange(NK)
    q, k = np.arange(P)[:, None], np.arange(3 * P)[None, :] - P
    const[:, C_MASK:C_MASK + 3 * P] = np.where(np.abs(q - k) <= P, 0.0, -1e30)
    const[:, C_IOTA16:C_IOTA16 + TOPK] = np.arange(TOPK)
    const[:, C_FREQ:C_FREQ + ROT] = f4(500000.0) ** (-np.arange(0, 2 * ROT, 2, dtype=f4) / f4(2 * ROT))
    t = np.linspace(0.0, 1.0, SEQ, dtype=f4)[:, None]
    bands = (EMB - 1) // 2
    w = f4(2.0 * math.pi) * np.arange(SEQ, dtype=f4)[:, None] / f4(SEQ)
    f = np.linspace(1e-4, bands - 1, bands, dtype=f4)[None, :]
    fw = (f * w).astype(f4)
    zemb = np.concatenate([t, np.cos(fw), -np.sin(fw)], axis=1).astype(f4).T
    lo, hi = math.log(1e-2) / 1.5, math.log(1e-2) / 0.3
    deltas = np.abs(np.linspace(lo, hi, HW, dtype=f4))[None, :]
    decay = np.exp(-t * deltas).astype(f4).reshape(NB, P, HW).transpose(1, 0, 2)
    ang = (2 * math.pi / (2 * SEQ)) * np.outer(np.arange(SEQ), np.arange(SEQ) + 0.5)
    both = np.stack([np.cos(ang), np.sin(ang)], axis=1)
    fwd = both.reshape(NB, P, 2, SEQ).transpose(1, 0, 2, 3).reshape(P, -1)
    inv = (both / SEQ).transpose(2, 1, 0).reshape(NB, P, 2, SEQ).transpose(1, 0, 2, 3).reshape(P, -1)
    return [np.ascontiguousarray(a, dtype=f4) for a in (const, zemb, decay, fwd, inv)]


def kernel(x, positions, norm_mix, w_in, conv_w, conv_b, filt_w1, filt_b1, filt_freq1, filt_w2, filt_b2, filt_freq2,
           filt_w3, filt_b3, hyena_skip, attn_sink, w_attn_branch, w_hyena_branch, w_out, norm_ffn, w_query, sub_keys,
           expert_u, expert_v, norm_final):
    import concourse.bacc as bacc
    from concourse.bass_utils import run_bass_kernel_spmd

    def chunks(a, n):
        return np.asarray(a).reshape(DEPTH, n, P).transpose(0, 2, 1)

    const, zemb, decay, fwd, inv = shape_tables()
    conv = np.asarray(conv_w).reshape(DEPTH, 3, NHY, P).transpose(0, 3, 2, 1).reshape(DEPTH, P, 3 * NHY)
    cols = np.concatenate([chunks(norm_mix, KC), chunks(norm_ffn, KC), conv, chunks(conv_b, NHY), chunks(hyena_skip, HC),
                           np.broadcast_to((np.arange(DEPTH, dtype=np.float32) * NK * NK)[:, None, None], (DEPTH, P, 1))], axis=2)
    fcols = np.stack([np.asarray(a) for a in (filt_b1, filt_freq1, filt_b2, filt_freq2)], axis=2)
    w3 = np.concatenate([np.asarray(filt_w3), np.asarray(filt_b3)[:, None, :]], axis=1)
    ut = (np.asarray(expert_u).reshape(DEPTH, NK, NK // 2, 2, KC, P).transpose(0, 2, 5, 3, 4, 1)
          .reshape(DEPTH, NK // 2, P, 2, KC * P))
    v = np.asarray(expert_v).reshape(DEPTH, NK, NG, JG, 2, DM // 2).transpose(0, 2, 4, 1, 3, 5)
    given = {
        "x": np.asarray(x).reshape(SEQ, DM), "positions": np.asarray(positions).reshape(SEQ), "consts": const,
        "gfinal": np.asarray(norm_final), "gffn": np.asarray(norm_ffn), "cols": cols, "fcols": fcols, "sink": np.asarray(attn_sink),
        "w1": np.asarray(filt_w1), "w2": np.asarray(filt_w2), "w3": w3, "zemb": zemb, "decay": decay,
        "fwd": fwd, "inv": inv, "w_in": np.asarray(w_in), "w_ab": np.asarray(w_attn_branch),
        "w_hb": np.asarray(w_hyena_branch), "w_out": np.asarray(w_out), "w_q": np.asarray(w_query),
        "keys": np.asarray(sub_keys).transpose(0, 3, 1, 2), "ut": ut, "v": v,
        "u_rows": np.asarray(expert_u).reshape(DEPTH * NK * NK, DM),
        "v_rows": np.asarray(expert_v).reshape(DEPTH * NK * NK, DM),
    }
    nc = bacc.Bacc("TRN2", target_bir_lowering=False, num_devices=1)
    arrays, args = {}, []
    for name, a in given.items():
        a = np.ascontiguousarray(a)
        arrays[f"{name}_dram"] = a
        args.append(nc.dram_tensor(f"{name}_dram", a.shape, mybir.dt.from_np(a.dtype), kind="ExternalInput").ap())
    args.append(nc.dram_tensor("out_dram", (SEQ, DM), F32, kind="ExternalOutput").ap())
    encoder(nc, *args)
    got = run_bass_kernel_spmd(nc, [arrays], core_ids=[0]).results[0]["out_dram"]
    return got.reshape(1, SEQ, DM)
```
